# Optimizing a Trainium2 kernel written in Bass

```python
import math
import jax, jax.numpy as jnp
from jax import lax
import numpy as np

D_MODEL = 1024
BATCH = 1
SEQ = 512
DEPTH = 1

N_MIXERS = 4
N_HEADS_PER_MIXER = 4
N_HEADS_TOTAL = N_MIXERS * N_HEADS_PER_MIXER
HEAD_DIM = D_MODEL // N_HEADS_TOTAL
GROUP_W = N_HEADS_PER_MIXER * HEAD_DIM
MIX_WIDTH = N_MIXERS * GROUP_W
PROJ_W = 12 * GROUP_W + N_HEADS_PER_MIXER

DIL_PATTERNS = ((128, 1), (512, 4), (2048, 16))
DIFF_DIM = HEAD_DIM // 2
MOBA_BLOCK = 256
MOBA_TOPK = 3
Q_BLOCK = 128
N_BUCKETS = 32
MAX_DISTANCE = 2048
N_BIAS_HEADS = 3 * N_HEADS_PER_MIXER
N_GROUPS = 4
EXPERTS_PER_GROUP = 8
N_EXPERTS = N_GROUPS * EXPERTS_PER_GROUP
TOP_K_INNER = 2
D_EXPERT = D_MODEL // 4
RMS_EPS = 1e-6
NEG_INF = -1e30

kernel_name = "hybrid_dilated_diff_moba_fox_hmoe"

def rmsnorm(x, g):
    xf = x.astype(jnp.float32)
    y = xf * lax.rsqrt(jnp.mean(xf * xf, axis=-1, keepdims=True) + RMS_EPS)
    return (y * g.astype(jnp.float32)).astype(x.dtype)

def t5_bucket(dist):
    max_exact = N_BUCKETS // 2
    d = jnp.maximum(dist, 0)
    df = jnp.maximum(d, 1).astype(jnp.float32)
    large = max_exact + (jnp.log(df / max_exact) / math.log(MAX_DISTANCE / max_exact)
                         * (N_BUCKETS - max_exact)).astype(jnp.int32)
    large = jnp.minimum(large, N_BUCKETS - 1)
    return jnp.where(d < max_exact, d, large)

def _unblock(o):
    nb, B, H, Q, d = o.shape
    return o.transpose(1, 2, 0, 3, 4).reshape(B, H, nb * Q, d)

def dilated_attention(q, k, v, bias_h):
    B, H, S, hd = q.shape
    scale = hd ** -0.5

    def block(i):
        t0 = i * Q_BLOCK
        t = t0 + jnp.arange(Q_BLOCK)
        qb = lax.dynamic_slice_in_dim(q, t0, Q_BLOCK, axis=2)
        outs, lses = [], []
        for window, dil in DIL_PATTERNS:
            steps = jnp.arange(window // dil + 1)
            pos = t[:, None] - steps[None, :] * dil
            valid = pos >= 0
            idx = jnp.maximum(pos, 0)
            kg = k[:, :, idx]
            vg = v[:, :, idx]
            bias = bias_h[:, t5_bucket(steps * dil)]
            s = jnp.einsum('bhqd,bhqkd->bhqk', qb, kg).astype(jnp.float32) * scale + bias[None, :, None, :]
            s = jnp.where(valid, s, NEG_INF)
            m = jnp.max(s, axis=-1, keepdims=True)
            p = jnp.exp(s - m)
            l = jnp.sum(p, axis=-1, keepdims=True)
            outs.append(jnp.einsum('bhqk,bhqkd->bhqd', (p / l).astype(v.dtype), vg))
            lses.append(m + jnp.log(l))
        alpha = jax.nn.softmax(jnp.concatenate(lses, axis=-1), axis=-1)
        o = alpha[..., 0:1] * outs[0] + alpha[..., 1:2] * outs[1] + alpha[..., 2:3] * outs[2]
        return o.astype(v.dtype)

    return _unblock(lax.map(block, jnp.arange(S // Q_BLOCK)))

def diff_attention(q1, q2, k1, k2, v, lam, bias_h):
    B, H, S, dd = q1.shape
    scale = dd ** -0.5
    kpos = jnp.arange(S)

    def block(i):
        t0 = i * Q_BLOCK
        t = t0 + jnp.arange(Q_BLOCK)
        causal = kpos[None, :] <= t[:, None]
        bias = bias_h[:, t5_bucket(t[:, None] - kpos[None, :])]

        def probs(q, k):
            qb = lax.dynamic_slice_in_dim(q, t0, Q_BLOCK, axis=2)
            s = jnp.einsum('bhqd,bhkd->bhqk', qb, k).astype(jnp.float32) * scale + bias
            return jax.nn.softmax(jnp.where(causal, s, NEG_INF), axis=-1)

        w = probs(q1, k1) - lam * probs(q2, k2)
        return jnp.einsum('bhqk,bhkd->bhqd', w.astype(v.dtype), v)

    return _unblock(lax.map(block, jnp.arange(S // Q_BLOCK)))

def moba_attention(q, k, v, bias_h):
    B, H, S, hd = q.shape
    scale = hd ** -0.5
    n_blk = -(-S // MOBA_BLOCK)
    pad = n_blk * MOBA_BLOCK - S
    k_pad = jnp.pad(k, ((0, 0), (0, 0), (0, pad), (0, 0)))
    v_pad = jnp.pad(v, ((0, 0), (0, 0), (0, pad), (0, 0)))
    k_blocks = k_pad.reshape(B, H, n_blk, MOBA_BLOCK, hd)
    v_blocks = v_pad.reshape(B, H, n_blk, MOBA_BLOCK, hd)
    k_mean = jnp.mean(k_blocks.astype(jnp.float32), axis=3)
    n_sel = min(MOBA_TOPK, n_blk)
    n_past = n_sel * MOBA_BLOCK
    bi = jnp.arange(B)[:, None, None, None]
    hi = jnp.arange(H)[None, :, None, None]
    in_blk = jnp.arange(MOBA_BLOCK)
    blk_ids = jnp.arange(n_blk)

    def block(i):
        t0 = i * Q_BLOCK
        t = t0 + jnp.arange(Q_BLOCK)
        own = t0 // MOBA_BLOCK
        qb = lax.dynamic_slice_in_dim(q, t0, Q_BLOCK, axis=2)
        gate = jnp.einsum('bhqd,bhnd->bhqn', qb.astype(jnp.float32), k_mean)
        gate = jnp.where(blk_ids < own, gate, NEG_INF)
        _, sel = lax.top_k(gate, n_sel)
        ok = jnp.repeat(sel < own, MOBA_BLOCK, axis=-1)
        kg = k_blocks[bi, hi, sel].reshape(B, H, Q_BLOCK, n_past, hd)
        vg = v_blocks[bi, hi, sel].reshape(B, H, Q_BLOCK, n_past, hd)
        pos = (sel[..., None] * MOBA_BLOCK + in_blk).reshape(B, H, Q_BLOCK, n_past)
        s_sel = (jnp.einsum('bhqd,bhqnd->bhqn', qb, kg).astype(jnp.float32) * scale
                 + bias_h[hi, t5_bucket(t[:, None] - pos)])
        s_sel = jnp.where(ok, s_sel, NEG_INF)
        own_pos = own * MOBA_BLOCK + in_blk
        k_own = lax.dynamic_slice_in_dim(k_pad, own * MOBA_BLOCK, MOBA_BLOCK, axis=2)
        v_own = lax.dynamic_slice_in_dim(v_pad, own * MOBA_BLOCK, MOBA_BLOCK, axis=2)
        s_own = (jnp.einsum('bhqd,bhkd->bhqk', qb, k_own).astype(jnp.float32) * scale
                 + bias_h[:, t5_bucket(t[:, None] - own_pos[None, :])])
        s_own = jnp.where(own_pos[None, :] <= t[:, None], s_own, NEG_INF)
        p = jax.nn.softmax(jnp.concatenate([s_sel, s_own], axis=-1), axis=-1).astype(v.dtype)
        return (jnp.einsum('bhqn,bhqnd->bhqd', p[..., :n_past], vg)
                + jnp.einsum('bhqk,bhkd->bhqd', p[..., n_past:], v_own))

    return _unblock(lax.map(block, jnp.arange(S // Q_BLOCK)))

def forgetting_attention(q, k, v, log_f):
    B, H, S, hd = q.shape
    scale = hd ** -0.5
    c = jnp.cumsum(log_f, axis=-1)
    kpos = jnp.arange(S)

    def block(i):
        t0 = i * Q_BLOCK
        t = t0 + jnp.arange(Q_BLOCK)
        qb = lax.dynamic_slice_in_dim(q, t0, Q_BLOCK, axis=2)
        c_q = lax.dynamic_slice_in_dim(c, t0, Q_BLOCK, axis=2)
        s = (jnp.einsum('bhqd,bhkd->bhqk', qb, k).astype(jnp.float32) * scale
             + c_q[..., None] - c[:, :, None, :])
        s = jnp.where(kpos[None, :] <= t[:, None], s, NEG_INF)
        p = jax.nn.softmax(s, axis=-1).astype(v.dtype)
        return jnp.einsum('bhqk,bhkd->bhqd', p, v)

    return _unblock(lax.map(block, jnp.arange(S // Q_BLOCK)))

def hybrid_mixer(h, w_in, w_out, lam_q1, lam_k1, lam_q2, lam_k2, subln_g, b_forget, rel_bias, lambda_init):
    B, S, _ = h.shape
    H = N_HEADS_PER_MIXER
    proj = h @ w_in
    qa, ka, va, qb, kb, vb, qc, kc, vc, qd, kd, vd, zf = jnp.split(
        proj, [GROUP_W * i for i in range(1, 13)], axis=-1)

    def heads(t):
        return t.reshape(B, S, H, -1).transpose(0, 2, 1, 3)

    def diff_heads(t):
        t = t.reshape(B, S, H, 2, DIFF_DIM)
        return t[..., 0, :].transpose(0, 2, 1, 3), t[..., 1, :].transpose(0, 2, 1, 3)

    bias_h = rel_bias.T.astype(jnp.float32)

    o_a = dilated_attention(heads(qa), heads(ka), heads(va), bias_h[0:H])

    q1, q2 = diff_heads(qb)
    k1, k2 = diff_heads(kb)
    lam = (jnp.exp(jnp.sum(lam_q1.astype(jnp.float32) * lam_k1.astype(jnp.float32)))
           - jnp.exp(jnp.sum(lam_q2.astype(jnp.float32) * lam_k2.astype(jnp.float32))) + lambda_init)
    o_b = diff_attention(q1, q2, k1, k2, heads(vb), lam, bias_h[H:2 * H])
    o_b = rmsnorm(o_b, subln_g) * (1.0 - lambda_init)

    o_c = moba_attention(heads(qc), heads(kc), heads(vc), bias_h[2 * H:3 * H])

    log_f = jax.nn.log_sigmoid(zf.astype(jnp.float32) + b_forget.astype(jnp.float32)).transpose(0, 2, 1)
    o_d = forgetting_attention(heads(qd), heads(kd), heads(vd), log_f)

    o = jnp.concatenate([o_a.astype(h.dtype), o_b.astype(h.dtype),
                         o_c.astype(h.dtype), o_d.astype(h.dtype)], axis=1)
    o = o.transpose(0, 2, 1, 3).reshape(B, S, MIX_WIDTH)
    return o @ w_out

def hier_moe(h, w_group, b_group, w_expert, b_expert, w_gate, w_up, w_down):
    B, S, D = h.shape
    t = h.reshape(-1, D)
    n_tok = t.shape[0]
    g_logits = (t @ w_group).astype(jnp.float32) + b_group.astype(jnp.float32)
    g_prob = jax.nn.softmax(g_logits, axis=-1)
    g_idx = jnp.argmax(g_logits, axis=-1)
    g_w = jnp.take_along_axis(g_prob, g_idx[:, None], axis=-1)
    e_all = ((t @ w_expert).astype(jnp.float32).reshape(n_tok, N_GROUPS, EXPERTS_PER_GROUP)
             + b_expert.astype(jnp.float32))
    e_logits = jnp.take_along_axis(e_all, g_idx[:, None, None], axis=1)[:, 0]
    top_v, top_i = lax.top_k(e_logits, TOP_K_INNER)
    comb = g_w * jax.nn.softmax(top_v, axis=-1)
    expert_id = g_idx[:, None] * EXPERTS_PER_GROUP + top_i
    combine = jnp.sum(jax.nn.one_hot(expert_id, N_EXPERTS, dtype=jnp.float32) * comb[..., None], axis=1)
    combine = combine.astype(t.dtype)
    out = jnp.zeros_like(t)
    for e in range(N_EXPERTS):
        hid = jax.nn.silu(t @ w_gate[e]) * (t @ w_up[e])
        out = out + combine[:, e:e + 1] * (hid @ w_down[e])
    return out.reshape(B, S, D)

def setup_inputs(seed: int = 0) -> dict:
    key = jax.random.key(seed)
    ks = jax.random.split(key, 21)
    f32 = jnp.float32

    def nrm(k, shape, scale):
        return jax.random.normal(k, shape, f32) * scale

    return {
        "x": nrm(ks[0], (BATCH, SEQ, D_MODEL), 1.0),
        "rel_bias": nrm(ks[1], (N_BUCKETS, N_BIAS_HEADS), 0.5),
        "ln1": 1.0 + nrm(ks[2], (DEPTH, D_MODEL), 0.02),
        "w_in": nrm(ks[3], (DEPTH, D_MODEL, PROJ_W), D_MODEL ** -0.5),
        "w_out": nrm(ks[4], (DEPTH, MIX_WIDTH, D_MODEL), MIX_WIDTH ** -0.5),
        "lam_q1": nrm(ks[5], (DEPTH, DIFF_DIM), 0.1),
        "lam_k1": nrm(ks[6], (DEPTH, DIFF_DIM), 0.1),
        "lam_q2": nrm(ks[7], (DEPTH, DIFF_DIM), 0.1),
        "lam_k2": nrm(ks[8], (DEPTH, DIFF_DIM), 0.1),
        "subln_g": 1.0 + nrm(ks[9], (DEPTH, HEAD_DIM), 0.02),
        "b_forget": 2.0 + nrm(ks[10], (DEPTH, N_HEADS_PER_MIXER), 0.1),
        "ln2": 1.0 + nrm(ks[11], (DEPTH, D_MODEL), 0.02),
        "w_group": nrm(ks[12], (DEPTH, D_MODEL, N_GROUPS), D_MODEL ** -0.5),
        "b_group": nrm(ks[13], (DEPTH, N_GROUPS), 0.01),
        "w_expert": nrm(ks[14], (DEPTH, D_MODEL, N_EXPERTS), D_MODEL ** -0.5),
        "b_expert": nrm(ks[15], (DEPTH, N_GROUPS, EXPERTS_PER_GROUP), 0.01),
        "w_gate": nrm(ks[16], (DEPTH, N_EXPERTS, D_MODEL, D_EXPERT), D_MODEL ** -0.5),
        "w_up": nrm(ks[17], (DEPTH, N_EXPERTS, D_MODEL, D_EXPERT), D_MODEL ** -0.5),
        "w_down": nrm(ks[18], (DEPTH, N_EXPERTS, D_EXPERT, D_MODEL), D_EXPERT ** -0.5),
        "ln_f": 1.0 + nrm(ks[19], (D_MODEL,), 0.02),
    }

def reference(x, rel_bias, ln1, w_in, w_out, lam_q1, lam_k1, lam_q2, lam_k2, subln_g, b_forget,
              ln2, w_group, b_group, w_expert, b_expert, w_gate, w_up, w_down, ln_f):
    for l in range(DEPTH):
        lambda_init = 0.8 - 0.6 * math.exp(-0.3 * l)
        h = rmsnorm(x, ln1[l])
        x = x + hybrid_mixer(h, w_in[l], w_out[l], lam_q1[l], lam_k1[l], lam_q2[l], lam_k2[l],
                             subln_g[l], b_forget[l], rel_bias, lambda_init)
        h2 = rmsnorm(x, ln2[l])
        x = x + hier_moe(h2, w_group[l], b_group[l], w_expert[l], b_expert[l],
                         w_gate[l], w_up[l], w_down[l])
    return rmsnorm(x, ln_f)


_drawn_inputs = setup_inputs


def setup_inputs(seed=0):
    import zlib

    import numpy as np

    out = dict(_drawn_inputs(seed))
    spreads = {}
    factors = {'lam_q2': 4.813,
     'lam_k2': 5.969,
     'subln_g': 3.496,
     'b_forget': 25.424,
     'b_group': 27.539,
     'b_expert': 7.411,
     'ln_f': 8.024,
     'ln2': 2.823}
    for name, (base, spread) in spreads.items():
        noise = np.random.default_rng([zlib.crc32(name.encode()), seed]).standard_normal(out[name].shape)
        drawn = base * np.exp(spread * noise) if base else spread * noise
        out[name] = __import__('jax').numpy.asarray(drawn.astype(out[name].dtype))
    for name, factor in factors.items():
        out[name] = (out[name] * factor).astype(out[name].dtype)
    return out
```

```python
import math
from contextlib import ExitStack

import concourse.bass as bass
from concourse import mybir

ALU = mybir.AluOpType
ACT = mybir.ActivationFunctionType
AX = mybir.AxisListType
F32 = mybir.dt.float32
BF16 = mybir.dt.bfloat16
U32 = mybir.dt.uint32
I32 = mybir.dt.int32

P = 128
S = 512
D = 1024
NT = S // P
KC = D // P
HD = 64
H = 4
GW = H * HD
A, B, C, F = range(4)
BUCKETS = 32
SPAN = S + P - 1
NEG = -1e30
EPS = 1e-6
LAMBDA_INIT = 0.8 - 0.6 * math.exp(-0.3 * 0)

NG, EPG = 4, 8
E = NG * EPG
FE = D // 4
FT = FE // P
CAP = 64
PAIRS = E // 2
SLOT = KC * GW
NSLOT = 12


def plan_front():
    plan = [("table",)]
    for i in range(NT):
        plan += [("ln1", i), ("hT", i)]
    plan += [("proj", A, g) for g in range(4)]
    plan += [("rev", A, h) for h in range(H)]
    plan += [("proj", A, g) for g in range(4, 6)]
    plan += [("rev", B, h) for h in range(H)]
    fill = {}
    for m in (B, C, F):
        for g, at in enumerate((0, 2, 5, 8, 10, 13)):
            fill[16 * (m - 1) + at] = [("proj", m, g)]
    fill[16 * B + 1] = [("z",)]
    last = [fill.pop(16 * C + 10)[0], fill.pop(16 * C + 13)[0]]
    fill[16 * F] = [last[0]]
    fill[16 * F + 1] = [last[1]]
    n_units = 4 * 4 * NT
    for n in range(n_units + 6):
        if n < n_units:
            m = n // 16
            if n == 16 * C:
                plan += [("rev", C, h) for h in range(H)]
            if n == 16 * F:
                plan += [("cb", h) for h in range(H)]
            plan.append(("score", n))
            plan += fill.get(n, [])
        if 0 <= n - 1 < n_units and (n - 1) // 16 == B:
            plan.append(("mix", n - 1))
        if 0 <= n - 2 < n_units:
            plan.append(("turn", n - 2))
        if 0 <= n - 3 < n_units:
            plan.append(("pv", n - 3))
        if 0 <= n - 4 < n_units and n % 4 == 3:
            plan.append(("onorm", n // 4 - 1))
        i, r = divmod(n - 16 * F - 8, 4)
        if 0 <= i < NT and r == 0:
            plan += [("oT", i), ("out", i), ("ln2", i)]
            if i >= 1:
                plan += after_out(i - 1)
    plan += after_out(NT - 1) + [("slots",)]
    plan += [("count",)] + [("weights", i) for i in range(NT)]
    return plan


def after_out(i):
    return [("h2T", i), ("route", i), ("pick", i), ("rank", i), ("slot", i)]


def uses(plan, kinds):
    at, first = 0, {}
    for item in plan:
        if item[0] in kinds:
            first[item] = at
            at += kinds[item[0]]
    return first, at


def hybrid_layer(nc, x, rel_bias, ln1, w_in, w_out, lam_q1, lam_k1, lam_q2, lam_k2, subln_g, b_forget,
                 ln2, w_group, b_group, w_expert, b_expert, w_gate, w_up, w_down, ln_f,
                 bucket_rows, bias_cols, out):
    plan = plan_front()
    P_AT, P_N = uses(plan, {"table": 2, "rev": 1, "proj": 1, "z": 1, "cb": 1, "out": 2, "route": 1,
                            "rank": 1, "slot": 1, "count": 1})
    T_AT, T_N = uses(plan, {"hT": 2, "turn": 1, "oT": 2, "h2T": 2})
    units = [(n // 16, (n // 4) % 4, n % 4) for n in range(16 * 4)]
    t_of, parts = {}, []
    for n, (m, i, h) in enumerate(units):
        for s in range(2 if m == B else 1):
            t_of[(n, s)] = len(parts)
            parts.append((n, s))

    with ExitStack() as ctx:
        def sb(name, shape, dt=F32):
            return ctx.enter_context(nc.sbuf_tensor(name, shape, dt))

        def sem(name):
            return ctx.enter_context(nc.semaphore(name))

        bank = {b: ctx.enter_context(nc.psum_tensor(f"bank_{b}", [P, 512], F32))
                for b in ("P0", "P1", "S0", "S1", "T0", "T1", "O0", "O1")}
        pbank = [bank["P0"], bank["P1"]]
        sbank = [bank["S0"], bank["S1"]]
        tbank = [bank["T0"], bank["T1"]]
        obank = [bank["O0"], bank["O1"]]

        ring = sb("ring", [P, NSLOT, SLOT])
        hT = sb("hT", [P, KC, S])
        xo = sb("xo", [P, NT, D])
        qk = sb("qk", [P, 2, 4, S])
        vv = sb("vv", [P, 2, NT, GW])
        gb = sb("gb", [P, 2, H, S])
        sc = sb("sc", [P, 4, S])
        pt = sb("pt", [P, 2, S])
        hrow = sb("hrow", [P, 2, D])
        junk = sb("junk", [P, D], BF16)
        sqh = sb("sqh", [P, GW])
        lnb = sb("lnb", [P, D])
        ident = sb("ident", [P, P])
        anti = sb("anti", [P, P])
        upto = sb("upto", [P, S])
        before = sb("before", [P, P])
        future = sb("future", [P, P])
        iota_e = sb("iota_e", [P, E])
        iota_s = sb("iota_s", [P, CAP])
        tokid = sb("tokid", [P, NT])
        relb = sb("relb", [BUCKETS + 2, 12])
        lamv = sb("lamv", [P, 4, HD // 2])
        lams = sb("lams", [P, 8])
        subg = sb("subg", [P, HD])
        bf = sb("bf", [P, H])
        wz = sb("wz", [P, KC, H])
        wr = sb("wr", [P, KC, NG + E])
        rb = sb("rb", [P, NG + E])
        ms = sb("ms", [P, 4, NT])
        rs = sb("rs", [P, 3, NT])
        negmax = sb("negmax", [P, len(parts)])
        lsum = sb("lsum", [P, len(parts)])
        linv = sb("linv", [P, len(parts)])
        mixc = sb("mixc", [P, 16])
        power = sb("power", [P, H])
        rtmp = sb("rtmp", [P, H])
        onrm = sb("onrm", [P, 2, H])
        zt = sb("zt", [P, 4, NT * H])
        logit = sb("logit", [P, NT, NG + E])
        pick = sb("pick", [P, 4, E])
        picks = sb("picks", [P, NT, 4])
        oh = sb("oh", [P, NT, 2, E])
        mem = sb("mem", [P, NT, E])
        rank = sb("rank", [P, NT, E])
        rankm = sb("rankm", [P, E])
        slotf = sb("slotf", [P, NT, PAIRS])
        slott = sb("slott", [P, PAIRS])
        idx = sb("idx", [P, PAIRS], U32)
        gexp = sb("gexp", [P, NT, NG])
        gsc = sb("gsc", [P, NT, 4])
        tw = sb("tw", [P, NT, 12])
        comb = sb("comb", [P, NT, 2])
        posf = sb("posf", [P, NT, 2])
        pos = sb("pos", [P, NT * 2], U32)
        late = sb("late", [P, NT, E])
        lcur = sb("lcur", [P, NT])
        busiest = sb("busiest", [P, 1])
        crowd = sb("crowd", [P, 1], I32)

        onehot_rows = sc[0:BUCKETS + 2, 0:2, :].rearrange("p a b -> p (a b)")[:, 0:SPAN]
        table_rows = sc[0:12, 2:4, :].rearrange("p a b -> p (a b)")[:, 0:SPAN]
        oT = vv[:, 0, :, :].rearrange("p i n -> p (i n)").rearrange("p (c t) -> p c t", c=KC)
        xres = qk[:, 0, :, :].rearrange("p (a b) s -> p a (b s)", a=2)
        spread = gb[:, 0, :, :].rearrange("p a b -> p (a b)")
        wout = ring[:, 0:4, :].rearrange("p a b -> p (a b)").rearrange("p (c n) -> p c n", c=KC)
        xg = qk[:, 1, :, :].rearrange("p (a b) s -> p a (b s)", a=2)
        xgT = gb[:, 1, :, :].rearrange("p a b -> p (a b)").rearrange("p (c s) -> p c s", c=2 * KC)
        lnfb = gb[:, 0, 0:2, :].rearrange("p a b -> p (a b)")
        yrow = hrow
        gate_act = sc[:, 0:2, 0:FT * CAP]
        hid = sc[:, 2:4, 0:FT * CAP]
        ybuf = ring[:, 0:4, :].rearrange("p a b -> p (a b)").rearrange("p (i k n) -> p i k n", i=NT, k=2)
        orow = ring[:, 4:6, :].rearrange("p a b -> p (a b)").rearrange("p (i n) -> p i n", i=NT)
        dense_act = qk[:, 0, 0:2, :]
        dense_hid = qk[:, 0, 2:4, :]

        table_d = nc.dram_tensor("table_scratch", (12, SPAN), F32, kind="Internal").ap()
        h2_d = nc.dram_tensor("h2_scratch", (S, D), F32, kind="Internal").ap()
        y_d = nc.dram_tensor("y_scratch", (E * CAP, D), F32, kind="Internal").ap()

        s_xin = [sem(f"s_xin{i}") for i in range(NT)]
        s_tabin, s_ln1b, s_small, s_ln2b, s_lnfb = map(sem, ("s_tabin", "s_ln1b", "s_small", "s_ln2b", "s_lnfb"))
        s_win = [sem(f"s_win{i}") for i in range(12)]
        s_wout = [sem(f"s_wout{i}") for i in range(4)]
        s_strip = [sem(f"s_strip{m}") for m in range(3)]
        s_xres = [sem(f"s_xres{i}") for i in range(2)]
        s_tabout = sem("s_tabout")
        s_h2out = [sem(f"s_h2out{i}") for i in range(NT)]
        s_const, s_pool = sem("s_const"), sem("s_pool")
        s_lfused = sem("s_lfused")
        s_sq, s_hrow = sem("s_sq"), sem("s_hrow")
        s_pfull, s_pempty = sem("s_pfull"), sem("s_pempty")
        s_tfull, s_tempty = sem("s_tfull"), sem("s_tempty")
        s_score, s_biased, s_exp, s_mix = map(sem, ("s_score", "s_biased", "s_exp", "s_mix"))
        s_pv, s_onorm = sem("s_pv"), sem("s_onorm")
        s_lam, s_lamexp = sem("s_lam"), sem("s_lamexp")
        s_zabs, s_zexp, s_zln, s_lf = map(sem, ("s_zabs", "s_zexp", "s_zln", "s_lf"))
        s_x2, s_sq2, s_h2 = map(sem, ("s_x2", "s_sq2", "s_h2"))
        s_pick, s_gexp, s_spread, s_idx, s_pos, s_crowd = map(
            sem, ("s_pick", "s_gexp", "s_spread", "s_idx", "s_pos", "s_crowd"))
        s_dve = sem("s_dve")
        s_rs1, s_rs2, s_rs3, s_osq, s_ors, s_root = map(sem, ("s_rs1", "s_rs2", "s_rs3", "s_osq", "s_ors", "s_root"))
        s_wgt = [sem(f"s_wgt{b}") for b in range(4)]
        s_xg = [sem(f"s_xg{b}") for b in range(2)]
        s_yst = [sem(f"s_yst{b}") for b in range(2)]
        s_mt, s_mx, s_gu, s_silu, s_hid, s_down, s_yd, s_ya = map(
            sem, ("s_mt", "s_mx", "s_gu", "s_silu", "s_hid", "s_down", "s_yd", "s_ya"))
        s_dw, s_dgu, s_dsilu, s_dhid, s_dy, s_dacc, s_dcur = map(
            sem, ("s_dw", "s_dgu", "s_dsilu", "s_dhid", "s_dy", "s_dacc", "s_dcur"))
        s_yg = [sem(f"s_yg{i}") for i in range(NT)]
        s_sum, s_sq3, s_orow, s_out = map(sem, ("s_sum", "s_sq3", "s_orow", "s_out"))

        def landed(eng, item, n=1):
            eng.wait_ge(s_pempty, P_AT[item] + n)

        def turned(eng, item, n=1):
            eng.wait_ge(s_tempty, T_AT[item] + n)

        win_d = w_in[0].rearrange("(p c) n -> p c n", c=KC)
        wout_d = w_out[0].rearrange("(c p) n -> p c n", p=P)

        def expert_chunks(e, b):
            s = 3 * b
            wide = lambda t: ring[:, t, :].rearrange("p (c f) -> p c f", c=KC)
            return ((wide(s), w_gate[0, bass.ds(e, 1)].rearrange("e (p c) f -> p (e c) f", c=KC)),
                    (wide(s + 1), w_up[0, bass.ds(e, 1)].rearrange("e (p c) f -> p (e c) f", c=KC)),
                    (ring[:, s + 2, :].rearrange("p (a n) -> p a n", a=FT),
                     w_down[0, bass.ds(e, 1)].rearrange("e (a p) n -> p (e a) n", p=P)))

        def gate_up(b):
            return [ring[:, 3 * b + z, :].rearrange("p (c f) -> p c f", c=KC) for z in range(2)]

        def down(b):
            return ring[:, 3 * b + 2, :].rearrange("p (a n) -> p a n", a=FT)

        def strip(m):
            return bass.AP(table_d.tensor, m * H * SPAN, [[1, P], [SPAN, H], [1, S]])

        def lfb_view(i):
            return hrow[:, 0, (i % 2) * P:(i % 2 + 1) * P]

        block = ctx.enter_context(nc.Block())

        @block.sync
        def _(sp):
            for i in range(NT):
                sp.dma_start(xo[:, i, :], x[0, i * P:(i + 1) * P, :]).then_inc(s_xin[i], 16)
                if i == 0:
                    sp.dma_start(lnb[:], ln1.to_broadcast([P, D])).then_inc(s_ln1b, 16)
            for g in range(12):
                sp.dma_start(ring[:, g, :].rearrange("p (c n) -> p c n", c=KC),
                             win_d[:, :, g * GW:(g + 1) * GW]).then_inc(s_win[g], 16)
                if g == 1:
                    sp.wait_ge(s_tabout, 16)
                    for m in (A, B):
                        sp.dma_start(gb[:, m % 2], strip(m)).then_inc(s_strip[m], 16)
            sp.wait_ge(s_hrow, NT)
            sp.dma_start(lnb[:], ln2.to_broadcast([P, D])).then_inc(s_ln2b, 16)
            for j in range(4):
                sp.wait_ge(s_pfull, P_AT[("proj", j // 3, 2 * (j % 3) + 1)] + 1)
                sp.dma_start(ring[:, j, :].rearrange("p (c n) -> p c n", c=2),
                             wout_d[:, 2 * j:2 * j + 2, :]).then_inc(s_wout[j], 16)
            sp.wait_ge(s_biased, t_of[(16 * B - 1, 0)] + 1)
            sp.dma_start(gb[:, 0], strip(C)).then_inc(s_strip[C], 16)
            for z, m in enumerate((C, F)):
                sp.wait_ge(s_pfull, P_AT[("proj", m, 5)] + 1)
                for dst, src in expert_chunks(z, z + 2):
                    sp.dma_start(dst, src).then_inc(s_wgt[z + 2], 16)
            sp.wait_ge(s_score, t_of[(16 * F - 1, 0)] + 1)
            for i in range(2):
                sp.dma_start(xres[:, i], x[0, i * P:(i + 1) * P, :]).then_inc(s_xres[i], 16)
            for i in range(NT):
                if i + 2 < NT:
                    landed(sp, ("out", i), 2)
                    sp.dma_start(xres[:, i], x[0, (i + 2) * P:(i + 3) * P, :]).then_inc(s_xres[i], 16)
                if i == NT - 1:
                    sp.wait_ge(s_pfull, P_AT[("out", i)] + 2)
                    for z in range(2):
                        for dst, src in expert_chunks(2 + z, z):
                            sp.dma_start(dst, src).then_inc(s_wgt[z], 16)
                sp.wait_ge(s_h2, i + 1)
                sp.dma_start(h2_d[i * P:(i + 1) * P, :], hrow[:, i % 2, :]).then_inc(s_h2out[i], 16)
            sp.wait_ge(s_pfull, P_AT[("slot", NT - 1)] + 1)
            sp.dma_start(lnfb, ln_f.rearrange("(a n) -> a n", a=1).to_broadcast([P, D])).then_inc(s_lnfb, 16)
            with sp.Fori(1, E // 4, 1) as it:
                for j in range(4):
                    b = (j + 2) % 4
                    sp.wait_ge(s_down, 4 * it + (j - 3))
                    for dst, src in expert_chunks(4 * it + j, b):
                        sp.dma_start(dst, src).then_inc(s_wgt[b], 16)
            sp.wait_ge(s_crowd, 1)
            with sp.register("sp_crowd") as r:
                sp.reg_load(r, crowd[0:1, 0:1])
                with sp.If(sp.snap(r) > CAP):
                    sp.wait_ge(s_down, E)
                    with sp.Fori(0, E, 1) as e:
                        sp.wait_ge(s_dcur, e + 1)
                        for dst, src in expert_chunks(e, 0):
                            sp.dma_start(dst, src).then_inc(s_dw, 16)
            for i in range(NT):
                sp.wait_ge(s_orow, i + 1)
                sp.dma_start(out[0, i * P:(i + 1) * P, :], orow[:, i, :]).then_inc(s_out, 16)
            sp.wait_ge(s_out, 16 * NT)

        @block.gpsimd
        def _(pool):
            made = 0
            for tile, value in ((ident, 0.0), (anti, 0.0), (upto, 1.0), (before, 1.0), (future, 0.0),
                                (power, -0.5)):
                pool.memset(tile[:], value).then_inc(s_pool, 1)
                made += 1
            pool.iota(iota_e[:], [[1, E]], base=0, channel_multiplier=0,
                      allow_small_or_imprecise_dtypes=True).then_inc(s_const, 1)
            pool.iota(iota_s[:], [[1, CAP]], base=1, channel_multiplier=0,
                      allow_small_or_imprecise_dtypes=True).then_inc(s_const, 1)
            pool.iota(tokid[:], [[P, NT]], base=0, channel_multiplier=1,
                      allow_small_or_imprecise_dtypes=True).then_inc(s_const, 1)
            pool.wait_ge(s_pool, made)
            for tile, op, fill, base, step, cm in (
                    (ident, ALU.not_equal, 1.0, 0, -1, 1), (anti, ALU.not_equal, 1.0, 1 - P, 1, 1),
                    (upto, ALU.is_ge, 0.0, 0, 1, -1), (before, ALU.is_gt, 0.0, 0, 1, -1),
                    (future, ALU.is_ge, NEG, 0, -1, 1)):
                pool.affine_select(out=tile[:], in_=tile[:], compare_op=op, fill=fill, base=base,
                                   pattern=[[step, tile.shape[1]]], channel_multiplier=cm).then_inc(s_const, 1)
            roots = [0]

            def inverse_root(dst, src, scale):
                n = src.shape[1]
                roots[0] += 1
                pool.tensor_scalar(rtmp[:, 0:n], src, scale, EPS, ALU.mult, ALU.add).then_inc(s_root, 1)
                pool.wait_ge(s_root, roots[0])
                return pool.tensor_tensor(dst, rtmp[:, 0:n], power[:, 0:n], ALU.pow)

            for item in plan:
                kind = item[0]
                if kind == "ln1":
                    i = item[1]
                    pool.wait_ge(s_sq, i + 1)
                    inverse_root(rs[:, 0, i:i + 1], ms[:, 0, i:i + 1], 1.0).then_inc(s_rs1, 1)
                elif kind == "ln2":
                    i = item[1]
                    pool.wait_ge(s_sq2, i + 1)
                    inverse_root(rs[:, 1, i:i + 1], ms[:, 1, i:i + 1], 1.0).then_inc(s_rs2, 1)
                elif kind == "onorm" and item[1] // 4 == B:
                    pool.wait_ge(s_osq, item[1] - 4 * B + 1)
                    inverse_root(onrm[:, 1, :], onrm[:, 0, :], 1.0 / HD).then_inc(s_ors, 1)

            def gather(pair):
                pool.indirect_dma_start(out=xg[:, pair % 2], out_offset=None, in_=h2_d[:, :],
                                        in_offset=bass.IndirectOffsetOnAxis(ap=idx[:, pair:pair + 1], axis=0)
                                        ).then_inc(s_xg[pair % 2], 16)

            pool.wait_ge(s_idx, 1)
            for i in range(NT):
                pool.wait_ge(s_h2out[i], 16)
            gather(0)
            gather(1)
            for pair in range(PAIRS):
                pool.wait_ge(s_yd, pair + 1)
                pool.wait_ge(s_ya, pair + 1)
                pool.dma_start(y_d[pair * P:(pair + 1) * P, :], yrow[:, pair % 2, :]).then_inc(s_yst[pair % 2], 16)
                if pair + 2 < PAIRS:
                    gather(pair + 2)
            for j in range(2):
                pool.wait_ge(s_yst[j], 16 * (PAIRS // 2))
            pool.wait_ge(s_pos, 1)
            pool.wait_ge(s_crowd, 1)
            pool.wait_ge(s_down, E)
            with pool.register("pool_crowd") as r:
                pool.reg_load(r, crowd[0:1, 0:1])
                with pool.If(pool.snap(r) > CAP):
                    pool.wait_ge(s_dacc, 2 * NT * E)
            for i in range(NT):
                for k in range(2):
                    n = 2 * i + k
                    pool.indirect_dma_start(out=ybuf[:, i, k], out_offset=None, in_=y_d[:, :],
                                            in_offset=bass.IndirectOffsetOnAxis(ap=pos[:, n:n + 1], axis=0)
                                            ).then_inc(s_yg[i], 16)
            for i in range(NT):
                pool.wait_ge(s_sq3, i + 1)
                inverse_root(rs[:, 2, i:i + 1], ms[:, 2, i:i + 1], 1.0).then_inc(s_rs3, 1)

        @block.scalar
        def _(act):
            act.dma_start(onehot_rows, bucket_rows).then_inc(s_tabin, 16)
            act.dma_start(relb[0:BUCKETS, :], rel_bias).then_inc(s_tabin, 16)
            act.dma_start(relb[BUCKETS:BUCKETS + 2, :], bias_cols).then_inc(s_tabin, 16)
            for z, v in enumerate((lam_q1, lam_k1, lam_q2, lam_k2)):
                act.dma_start(lamv[:, z, :], v.to_broadcast([P, HD // 2])).then_inc(s_small, 16)
            act.dma_start(subg[:], subln_g.to_broadcast([P, HD])).then_inc(s_small, 16)
            act.dma_start(bf[:], b_forget.to_broadcast([P, H])).then_inc(s_small, 16)
            act.dma_start(wz[:], win_d[:, :, 12 * GW:12 * GW + H]).then_inc(s_small, 16)
            act.dma_start(wr[:, :, 0:NG], w_group[0].rearrange("(p c) n -> p c n", c=KC)).then_inc(s_small, 16)
            act.dma_start(wr[:, :, NG:], w_expert[0].rearrange("(p c) n -> p c n", c=KC)).then_inc(s_small, 16)
            act.dma_start(rb[:, 0:NG], b_group.to_broadcast([P, NG])).then_inc(s_small, 16)
            act.dma_start(rb[:, NG:], b_expert[0:1].rearrange("a g e -> a (g e)").to_broadcast([P, E])).then_inc(s_small, 16)

            def copy_out(k, dst, src):
                act.wait_ge(s_tfull, k + 1)
                act.activation(dst, src, ACT.Copy).then_inc(s_tempty, 1)

            for item in plan:
                kind = item[0]
                if kind == "table":
                    landed(act, item, 2)
                    act.dma_start(table_d, table_rows).then_inc(s_tabout, 16)
                elif kind == "ln1":
                    i = item[1]
                    act.wait_ge(s_xin[i], 16)
                    act.activation(junk[:], xo[:, i, :], ACT.Square, scale=1.0 / 32,
                                   accum_out=ms[:, 0, i:i + 1]).then_inc(s_sq, 1)
                elif kind in ("hT", "h2T"):
                    i = item[1]
                    for z in range(2):
                        k = T_AT[item] + z
                        copy_out(k, hT[:, 4 * z:4 * z + 4, i * P:(i + 1) * P],
                                 tbank[k % 2][:].rearrange("p (c t) -> p c t", c=4))
                elif kind == "score":
                    n = item[1]
                    if n == 16 * A:
                        act.wait_ge(s_lam, 2)
                        act.activation(lams[:, 2:4], lams[:, 0:2], ACT.Exp).then_inc(s_lamexp, 1)
                    m, i, h = units[n]
                    for s in range(2 if m == B else 1):
                        t = t_of[(n, s)]
                        e = sc[:, t % 4, 0:(i + 1) * P]
                        act.wait_ge(s_biased, t + 1)
                        act.activation(e, e, ACT.Exp, bias=negmax[:, t:t + 1], scale=-1.0,
                                       accum_out=lsum[:, t:t + 1]).then_inc(s_exp, 1)
                elif kind == "turn":
                    n = item[1]
                    k = T_AT[item]
                    nk = (units[n][1] + 1) * P
                    if n >= 2:
                        act.wait_ge(s_pv, n - 1)
                    copy_out(k, pt[:, n % 2, 0:nk], tbank[k % 2][:, 0:nk])
                elif kind == "z":
                    landed(act, item)
                    act.activation(zt[:, 1, :], zt[:, 0, :], ACT.Abs).then_inc(s_zabs, 1)
                    act.wait_ge(s_zabs, 1)
                    act.activation(zt[:, 2, :], zt[:, 1, :], ACT.Exp, scale=-1.0).then_inc(s_zexp, 1)
                    act.wait_ge(s_zexp, 1)
                    act.activation(zt[:, 3, :], zt[:, 2, :], ACT.Ln, bias=1.0).then_inc(s_zln, 1)
                elif kind == "oT":
                    i = item[1]
                    for z in range(2):
                        k = T_AT[item] + z
                        if i and not z:
                            act.wait_ge(s_pfull, P_AT[("out", i - 1)] + 2)
                        copy_out(k, oT[:, 4 * z:4 * z + 4, :], tbank[k % 2][:].rearrange("p (c t) -> p c t", c=4))
                elif kind == "ln2":
                    i = item[1]
                    act.wait_ge(s_pempty, P_AT[("out", i)] + 2)
                    act.activation(junk[:], xo[:, i, :], ACT.Square, scale=1.0 / 32,
                                   accum_out=ms[:, 1, i:i + 1]).then_inc(s_sq2, 1)
                elif kind == "weights":
                    i = item[1]
                    act.wait_ge(s_pick, i + 1)
                    act.activation(gexp[:, i, :], logit[:, i, 0:NG], ACT.Exp, bias=picks[:, i, 3:4],
                                   accum_out=gsc[:, i, 0:1]).then_inc(s_gexp, 1)
                    act.activation(gsc[:, i, 1:2], picks[:, i, 1:2], ACT.Exp, scale=-1.0,
                                   bias=picks[:, i, 2:3]).then_inc(s_gexp, 1)

            def rows_to_chunks(q, first, j):
                for z in range(2):
                    act.wait_ge(s_mt, 2 * q + (z + 1))
                    act.activation(xgT[:, 8 * j + 4 * z:8 * j + 4 * z + 4, :],
                                   tbank[z][:].rearrange("p (c t) -> p c t", c=4), ACT.Copy).then_inc(s_mx, 1)

            def pair_steps(it, j, first, last):
                q = 2 * it + j
                for z in range(2):
                    e = 4 * it + (2 * j + z)
                    act.wait_ge(s_gu, e + 1)
                    act.activation(gate_act[:, z, :], sbank[z][:, 0:FT * CAP], ACT.Silu).then_inc(s_silu, 1)
                if not (last and j == 1):
                    if not (first and j == 0):
                        act.wait_ge(s_gu, 2 * q)
                    rows_to_chunks(q + 1, first, (j + 1) % 2)
                act.wait_ge(s_down, 2 * q + 2)
                if not first:
                    act.wait_ge(s_yst[j], 16 * it)
                act.activation(yrow[:, j, 512:1024], (pbank, obank)[j][1][:], ACT.Copy).then_inc(s_ya, 1)

            rows_to_chunks(0, True, 0)
            for j in range(2):
                pair_steps(0, j, True, False)
            with act.Fori(1, E // 4 - 1, 1) as it:
                for j in range(2):
                    pair_steps(it, j, False, False)
            for j in range(2):
                pair_steps(E // 4 - 1, j, False, True)

            act.wait_ge(s_crowd, 1)
            with act.register("act_crowd") as r:
                act.reg_load(r, crowd[0:1, 0:1])
                with act.If(act.snap(r) > CAP):
                    with act.Fori(0, E, 1) as e:
                        for a in range(FT):
                            act.wait_ge(s_dgu, FT * e + (a + 1))
                            act.activation(dense_act[:, a, :], pbank[0][:], ACT.Silu).then_inc(s_dsilu, 1)
            for i in range(NT):
                act.wait_ge(s_sum, 2 * i + 2)
                act.activation(junk[:], xo[:, i, :], ACT.Square, scale=1.0 / 32,
                               accum_out=ms[:, 2, i:i + 1]).then_inc(s_sq3, 1)

        @block.tensor
        def _(pe):
            def open_p(k):
                if k >= 2:
                    pe.wait_ge(s_pempty, k - 1)
                return pbank[k % 2]

            def open_t(k):
                if k >= 2:
                    pe.wait_ge(s_tempty, k - 1)
                return tbank[k % 2]

            def turn8(item, src):
                for z in range(2):
                    k = T_AT[item] + z
                    t = open_t(k)
                    for c in range(4):
                        last = pe.transpose(t[:, c * P:(c + 1) * P], src[:, (4 * z + c) * P:(4 * z + c + 1) * P], ident[:])
                    last.then_inc(s_tfull, 1)

            for item in plan:
                kind = item[0]
                if kind == "table":
                    pe.wait_ge(s_const, 8)
                    pe.wait_ge(s_tabin, 48)
                    k = P_AT[item]
                    for z, (a, b) in enumerate(((0, 512), (512, SPAN))):
                        pe.matmul(open_p(k + z)[0:12, 0:b - a], relb[:], onehot_rows[:, a:b],
                                  start=True, stop=True).then_inc(s_pfull, 1)
                elif kind == "hT":
                    i = item[1]
                    pe.wait_ge(s_hrow, i + 1)
                    turn8(item, hrow[:, i % 2, :])
                elif kind == "rev":
                    m, h = item[1:]
                    k = P_AT[item]
                    pe.wait_ge(s_strip[m], 16)
                    pe.matmul(open_p(k)[:], anti[:], gb[:, m % 2, h, :], start=True, stop=True).then_inc(s_pfull, 1)
                elif kind == "proj":
                    m, g = item[1:]
                    k = P_AT[item]
                    if (m, g) == (A, 0):
                        turned(pe, ("hT", NT - 1), 2)
                    w = ring[:, 3 * m + g // 2, :].rearrange("p (c n) -> p c n", c=KC)
                    if g % 2 == 0:
                        pe.wait_ge(s_win[3 * m + g // 2], 16)
                    o = open_p(k)
                    if g < 4:
                        for c in range(KC):
                            last = pe.matmul(o[:], w[:, c, (g % 2) * P:(g % 2 + 1) * P], hT[:, c, :],
                                             start=(c == 0), stop=(c == KC - 1))
                    else:
                        for i in range(2):
                            t0 = (2 * (g - 4) + i) * P
                            for c in range(KC):
                                last = pe.matmul(o[:, i * GW:(i + 1) * GW], hT[:, c, t0:t0 + P], w[:, c, :],
                                                 start=(c == 0), stop=(c == KC - 1))
                    last.then_inc(s_pfull, 1)
                elif kind == "z":
                    o = open_p(P_AT[item])
                    pe.wait_ge(s_small, 16 * 11)
                    for i in range(NT):
                        for c in range(KC):
                            last = pe.matmul(o[:, i * H:(i + 1) * H], hT[:, c, i * P:(i + 1) * P], wz[:, c, :],
                                             start=(c == 0), stop=(c == KC - 1))
                    last.then_inc(s_pfull, 1)
                elif kind == "cb":
                    h = item[1]
                    o = open_p(P_AT[item])
                    for i in range(NT):
                        pe.wait_ge(s_lf, NT * h + i + 1)
                        last = pe.matmul(o[:, i * P:S], lfb_view(i), upto[:, 0:S - i * P],
                                         start=(i == 0), stop=(i == NT - 1))
                        if i < NT - 1:
                            last.then_inc(s_lfused, 1)
                    last.then_inc(s_pfull, 1)
                elif kind == "score":
                    n = item[1]
                    m, i, h = units[n]
                    nk = (i + 1) * P
                    if i == 0 and h % 2 == 0:
                        landed(pe, ("proj", m, h // 2))
                        landed(pe, ("proj", m, 2 + h // 2))
                    for s in range(2 if m == B else 1):
                        t = t_of[(n, s)]
                        if t >= 2:
                            pe.wait_ge(s_biased, t - 1)
                        kd = HD // 2 if m == B else HD
                        r0 = (h % 2) * HD + s * kd
                        q = qk[r0:r0 + kd, m % 2, h // 2, i * P:(i + 1) * P]
                        k = qk[r0:r0 + kd, m % 2, 2 + h // 2, 0:nk]
                        last = pe.matmul(sbank[t % 2][:, 0:nk], q, k, start=True, stop=(m != F))
                        if m == F:
                            last = pe.matmul(sbank[t % 2][:, i * P:nk], ident[:], future[:], start=False, stop=True)
                        last.then_inc(s_score, 1)
                elif kind == "turn":
                    n = item[1]
                    m, i, h = units[n]
                    k = T_AT[item]
                    t = t_of[(n, 0)]
                    if m == B:
                        pe.wait_ge(s_mix, n - 16 * B + 1)
                    else:
                        pe.wait_ge(s_exp, t + 1)
                    o = open_t(k)
                    for b in range(i + 1):
                        last = pe.transpose(o[:, b * P:(b + 1) * P], sc[:, t % 4, b * P:(b + 1) * P], ident[:])
                    last.then_inc(s_tfull, 1)
                elif kind == "pv":
                    n = item[1]
                    m, i, h = units[n]
                    turned(pe, ("turn", n))
                    if h == 0:
                        if n // 4 >= 2:
                            pe.wait_ge(s_onorm, n // 4 - 1)
                        landed(pe, ("proj", m, 4 + i // 2))
                    o = obank[(n // 4) % 2]
                    for b in range(i + 1):
                        last = pe.matmul(o[:, h * HD:(h + 1) * HD], pt[:, n % 2, b * P:(b + 1) * P],
                                         vv[:, m % 2, b, h * HD:(h + 1) * HD], start=(b == 0), stop=(b == i))
                    last.then_inc(s_pv, 1)
                elif kind == "oT":
                    i = item[1]
                    pe.wait_ge(s_onorm, 4 * F + i + 1)
                    turn8(item, xo[:, i, :])
                elif kind == "out":
                    i = item[1]
                    turned(pe, ("oT", i), 2)
                    if i == 0:
                        for j in range(4):
                            pe.wait_ge(s_wout[j], 16)
                    for z in range(2):
                        k = P_AT[item] + z
                        o = open_p(k)
                        for c in range(KC):
                            last = pe.matmul(o[:], oT[:, c, :], wout[:, c, z * 512:(z + 1) * 512],
                                             start=(c == 0), stop=(c == KC - 1))
                        last.then_inc(s_pfull, 1)
                elif kind == "h2T":
                    i = item[1]
                    pe.wait_ge(s_h2, i + 1)
                    turn8(item, hrow[:, i % 2, :])
                elif kind == "route":
                    i = item[1]
                    turned(pe, ("h2T", i), 2)
                    o = open_p(P_AT[item])
                    for c in range(KC):
                        last = pe.matmul(o[:, 0:NG + E], hT[:, c, i * P:(i + 1) * P], wr[:, c, :],
                                         start=(c == 0), stop=(c == KC - 1))
                    last.then_inc(s_pfull, 1)
                elif kind in ("rank", "count"):
                    i = item[1] if kind == "rank" else NT
                    o = open_p(P_AT[item])
                    pe.wait_ge(s_pick, min(i, NT - 1) + 1)
                    for z in range(min(i, NT - 1) + 1):
                        own = kind == "rank" and z == i
                        last = pe.matmul(o[:, 0:E], before[:] if own else upto[:, P:2 * P], mem[:, z, :],
                                         start=(z == 0), stop=(z == min(i, NT - 1)))
                    last.then_inc(s_pfull, 1)
                elif kind == "slot":
                    i = item[1]
                    o = open_p(P_AT[item])
                    pe.wait_ge(s_spread, i + 1)
                    for q in range(PAIRS):
                        last = pe.matmul(o[:, q:q + 1], spread[:, q * P:(q + 1) * P], tokid[:, i:i + 1],
                                         start=True, stop=True)
                    last.then_inc(s_pfull, 1)

            def turn_rows(q, j, first):
                for z in range(2):
                    if not first:
                        pe.wait_ge(s_mx, 2 * q + (z - 1))
                    for c in range(4):
                        last = pe.transpose(tbank[z][:, c * P:(c + 1) * P],
                                            xg[:, j, (4 * z + c) * P:(4 * z + c + 1) * P], ident[:])
                    last.then_inc(s_mt, 1)

            def pair_steps(it, j, first, last_it):
                q = 2 * it + j
                pe.wait_ge(s_mx, 2 * q + 2)
                for z in range(2):
                    e = 4 * it + (2 * j + z)
                    b = (2 * j + z + 2) % 4
                    pe.wait_ge(s_wgt[b], 48 * it + 48)
                    if not (first and j == 0):
                        pe.wait_ge(s_hid, 4 * it + (2 * j + z - 1))
                    for u, w in enumerate(gate_up(b)):
                        for a in range(FT):
                            col = (u * FT + a) * CAP
                            for c in range(KC):
                                last = pe.matmul(sbank[z][:, col:col + CAP], w[:, c, a * P:(a + 1) * P],
                                                 xgT[:, 8 * j + c, z * CAP:(z + 1) * CAP],
                                                 start=(c == 0), stop=(c == KC - 1))
                    last.then_inc(s_gu, 1)
                if not (last_it and j == 1):
                    pe.wait_ge(s_xg[(j + 1) % 2], 16 * (it + j) + 16)
                    turn_rows(q + 1, (j + 1) % 2, False)
                y = (pbank, obank)[j]
                for z in range(2):
                    b = (2 * j + z + 2) % 4
                    pe.wait_ge(s_hid, 4 * it + (2 * j + z + 1))
                    if not first and z == 0:
                        pe.wait_ge(s_yd, 2 * it + (j - 1))
                        pe.wait_ge(s_ya, 2 * it + (j - 1))
                    for half in range(2):
                        for a in range(FT):
                            last = pe.matmul(y[half][z * CAP:(z + 1) * CAP, :], hid[:, z, a * CAP:(a + 1) * CAP],
                                             down(b)[:, a, half * 512:(half + 1) * 512],
                                             start=(a == 0), stop=(a == FT - 1))
                    last.then_inc(s_down, 1)

            pe.wait_ge(s_tempty, T_N)
            pe.wait_ge(s_pempty, P_N)
            pe.wait_ge(s_xg[0], 16)
            turn_rows(0, 0, True)
            for j in range(2):
                pair_steps(0, j, True, False)
            with pe.Fori(1, E // 4 - 1, 1) as it:
                for j in range(2):
                    pair_steps(it, j, False, False)
            for j in range(2):
                pair_steps(E // 4 - 1, j, False, True)

            pe.wait_ge(s_crowd, 1)
            with pe.register("pe_crowd") as r:
                pe.reg_load(r, crowd[0:1, 0:1])
                with pe.If(pe.snap(r) > CAP):
                    pe.wait_ge(s_yd, PAIRS)
                    pe.wait_ge(s_ya, PAIRS)
                    with pe.Fori(0, E, 1) as e:
                        pe.wait_ge(s_dw, 48 * e + 48)
                        pe.wait_ge(s_dcur, e + 1)
                        for a in range(FT):
                            if a:
                                pe.wait_ge(s_dhid, FT * e + a)
                            for u, w in enumerate(gate_up(0)):
                                for c in range(KC):
                                    last = pe.matmul(pbank[u][:], w[:, c, a * P:(a + 1) * P], hT[:, c, :],
                                                     start=(c == 0), stop=(c == KC - 1))
                            last.then_inc(s_dgu, 1)
                        pe.wait_ge(s_dhid, FT * e + FT)
                        for i in range(NT):
                            for half in range(2):
                                n = 2 * i + half
                                if n >= 2:
                                    pe.wait_ge(s_dacc, 2 * NT * e + (n - 1))
                                for a in range(FT):
                                    last = pe.matmul(obank[half][:], dense_hid[:, a, i * P:(i + 1) * P],
                                                     down(0)[:, a, half * 512:(half + 1) * 512],
                                                     start=(a == 0), stop=(a == FT - 1))
                                last.then_inc(s_dy, 1)

        @block.vector
        def _(dve):
            steps = [0]

            def link(ins):
                steps[0] += 1
                ins.then_inc(s_dve, 1)
                dve.wait_ge(s_dve, steps[0])

            def permuted(row):
                return row.rearrange("p (c j) -> p j c", c=KC)

            def normalise(dst, src, r):
                return dve.scalar_tensor_tensor(out=permuted(dst), in0=src.rearrange("p (j c) -> p j c", c=KC),
                                                scalar=r, in1=lnb[:].rearrange("p (j c) -> p j c", c=KC),
                                                op0=ALU.mult, op1=ALU.mult)

            def take(k):
                dve.wait_ge(s_pfull, k + 1)
                return pbank[k % 2]

            def first_max(v, n, top, onehot, i):
                link(dve.tensor_reduce(top, v, AX.X, ALU.max))
                link(dve.tensor_scalar(pick[:, 1, 0:n], v, top, None, ALU.is_equal))
                link(dve.scalar_tensor_tensor(out=pick[:, 2, 0:n], in0=pick[:, 1, 0:n], scalar=-1000.0,
                                              in1=iota_e[:, 0:n], op0=ALU.mult, op1=ALU.add))
                link(dve.tensor_reduce(picks[:, i, 0:1], pick[:, 2, 0:n], AX.X, ALU.min))
                link(dve.tensor_scalar(onehot, pick[:, 2, 0:n], picks[:, i, 0:1], None, ALU.is_equal))

            for item in plan:
                kind = item[0]
                if kind == "table":
                    for z, (a, b) in enumerate(((0, 512), (512, SPAN))):
                        o = take(P_AT[item] + z)
                        dve.tensor_copy(table_rows[:, a:b], o[0:12, 0:b - a]).then_inc(s_pempty, 1)
                elif kind == "ln1":
                    i = item[1]
                    if i == 0:
                        dve.wait_ge(s_ln1b, 16)
                    if i >= 2:
                        dve.wait_ge(s_tfull, T_AT[("hT", i - 2)] + 2)
                    dve.wait_ge(s_rs1, i + 1)
                    dve.wait_ge(s_xin[i], 16)
                    normalise(hrow[:, i % 2, :], xo[:, i, :], rs[:, 0, i:i + 1]).then_inc(s_hrow, 1)
                elif kind == "rev":
                    m, h = item[1:]
                    o = take(P_AT[item])
                    dve.tensor_copy(gb[:, m % 2, h, :], o[:]).then_inc(s_pempty, 1)
                    if (m, h) == (A, 0):
                        dve.wait_ge(s_small, 16 * 11)
                        for z in range(2):
                            dve.tensor_tensor_reduce(lamv[:, 2 * z, :], lamv[:, 2 * z, :], lamv[:, 2 * z + 1, :], 1.0, 0.0,
                                                     ALU.mult, ALU.add, lams[:, z:z + 1]).then_inc(s_lam, 1)
                elif kind == "proj":
                    m, g = item[1:]
                    o = take(P_AT[item])
                    if g < 2:
                        scale = (HD // 2 if m == B else HD) ** -0.5
                        dve.tensor_scalar(qk[:, m % 2, g, :], o[:], scale, None, ALU.mult).then_inc(s_pempty, 1)
                    elif g < 4:
                        dve.tensor_copy(qk[:, m % 2, g, :], o[:]).then_inc(s_pempty, 1)
                    else:
                        dve.tensor_copy(vv[:, m % 2, 2 * (g - 4):2 * (g - 4) + 2, :],
                                        o[:].rearrange("p (i n) -> p i n", i=2)).then_inc(s_pempty, 1)
                elif kind == "z":
                    o = take(P_AT[item])
                    dve.tensor_tensor(zt[:, 0, :].rearrange("p (i h) -> p i h", h=H),
                                      o[:, 0:NT * H].rearrange("p (i h) -> p i h", h=H),
                                      bf[:].unsqueeze(1).to_broadcast([P, NT, H]), ALU.add).then_inc(s_pempty, 1)
                    landed(dve, item)
                    dve.wait_ge(s_zabs, 1)
                    link(dve.tensor_scalar(zt[:, 0, :], zt[:, 0, :], 0.0, None, ALU.min))
                elif kind == "cb":
                    h = item[1]
                    if h == 0:
                        dve.wait_ge(s_zln, 1)
                        link(dve.tensor_tensor(zt[:, 0, :], zt[:, 0, :], zt[:, 3, :], ALU.subtract))
                    for i in range(NT):
                        n = NT * h + i
                        if i == 1 and h:
                            dve.wait_ge(s_pfull, P_AT[("cb", h - 1)] + 1)
                        elif i >= 2 or h:
                            dve.wait_ge(s_lfused, (NT - 1) * h + max(i - 1, 0))
                        dve.tensor_copy(lfb_view(i), zt[:, 0, i * H + h:i * H + h + 1].to_broadcast([P, P])).then_inc(s_lf, 1)
                    if h == 0:
                        dve.wait_ge(s_biased, t_of[(16 * C - 1, 1)] + 1)
                    dve.tensor_scalar(gb[:, 1, h, :], take(P_AT[item])[:], -1.0, None, ALU.mult).then_inc(s_pempty, 1)
                elif kind == "score":
                    n = item[1]
                    m, i, h = units[n]
                    nk = (i + 1) * P
                    if n == 16 * A + 1:
                        dve.wait_ge(s_lamexp, 1)
                        link(dve.tensor_tensor(lams[:, 4:5], lams[:, 2:3], lams[:, 3:4], ALU.subtract))
                        link(dve.tensor_scalar(lams[:, 5:6], lams[:, 4:5], LAMBDA_INIT, -1.0, ALU.add, ALU.mult))
                        link(dve.tensor_scalar(subg[:], subg[:], 1.0 - LAMBDA_INIT, None, ALU.mult))
                    if i == 0:
                        landed(dve, ("cb", h) if m == F else ("rev", m, h))
                    for s in range(2 if m == B else 1):
                        t = t_of[(n, s)]
                        bias = gb[:, m % 2, h, (0 if m == F else S - nk):(nk if m == F else S)]
                        if t >= 4:
                            dve.wait_ge(s_tfull, T_AT[("turn", parts[t - 4][0])] + 1)
                        dve.wait_ge(s_score, t + 1)
                        dve.tensor_tensor_reduce(sc[:, t % 4, 0:nk], sbank[t % 2][:, 0:nk], bias, -1.0, 3e38,
                                                 ALU.add, ALU.min, negmax[:, t:t + 1]).then_inc(s_biased, 1)
                elif kind == "mix":
                    n = item[1]
                    m, i, h = units[n]
                    nk = (i + 1) * P
                    t = t_of[(n, 0)]
                    dve.wait_ge(s_exp, t + 2)
                    link(dve.reciprocal(linv[:, t:t + 2], lsum[:, t:t + 2]))
                    c = mixc[:, n % 16:n % 16 + 1]
                    link(dve.scalar_tensor_tensor(out=c, in0=lsum[:, t:t + 1], scalar=lams[:, 5:6],
                                                  in1=linv[:, t + 1:t + 2], op0=ALU.mult, op1=ALU.mult))
                    dve.scalar_tensor_tensor(out=sc[:, t % 4, 0:nk], in0=sc[:, (t + 1) % 4, 0:nk], scalar=c,
                                             in1=sc[:, t % 4, 0:nk], op0=ALU.mult, op1=ALU.add).then_inc(s_mix, 1)
                elif kind == "onorm":
                    g4 = item[1]
                    m, i, _ = units[4 * g4]
                    dve.wait_ge(s_pv, 4 * g4 + 4)
                    t = t_of[(4 * g4, 0)]
                    o = obank[g4 % 2][:, 0:GW].rearrange("p (h n) -> p h n", h=H)
                    dst = xo[:, i, m * GW:(m + 1) * GW].rearrange("p (h n) -> p h n", h=H)
                    wide = lambda v: v.unsqueeze(2).to_broadcast([P, H, HD])
                    if m != B:
                        link(dve.reciprocal(linv[:, t:t + H], lsum[:, t:t + H]))
                        dve.tensor_tensor(dst, o, wide(linv[:, t:t + H]), ALU.mult).then_inc(s_onorm, 1)
                    else:
                        l1 = linv[:, t:t + 2 * H].rearrange("p (h s) -> p h s", s=2)[:, :, 0]
                        dve.tensor_tensor(dst, o, wide(l1), ALU.mult).then_inc(s_onorm, 1)
                        dve.wait_ge(s_onorm, g4 + 1)
                        sq = sqh[:]
                        link(dve.tensor_tensor(sq.rearrange("p (h n) -> p h n", h=H), dst, dst, ALU.mult))
                        dve.tensor_reduce(onrm[:, 0, :], sq.rearrange("p (h n) -> p h n", h=H), AX.X,
                                          ALU.add).then_inc(s_osq, 1)
                        dve.wait_ge(s_ors, g4 - 4 * B + 1)
                        link(dve.tensor_tensor(dst, dst, wide(onrm[:, 1, :]), ALU.mult))
                        link(dve.tensor_tensor(dst, dst, subg[:].unsqueeze(1).to_broadcast([P, H, HD]), ALU.mult))
                elif kind == "out":
                    i = item[1]
                    dve.wait_ge(s_xres[i % 2], 16 * (i // 2 + 1))
                    for z in range(2):
                        o = take(P_AT[item] + z)
                        dve.tensor_tensor(xo[:, i, z * 512:(z + 1) * 512], o[:], xres[:, i % 2, z * 512:(z + 1) * 512],
                                          ALU.add).then_inc(s_pempty, 1)
                elif kind == "ln2":
                    i = item[1]
                    if i == 0:
                        dve.wait_ge(s_ln2b, 16)
                    if i >= 2:
                        dve.wait_ge(s_tfull, T_AT[("h2T", i - 2)] + 2)
                        dve.wait_ge(s_h2out[i - 2], 16)
                    dve.wait_ge(s_rs2, i + 1)
                    normalise(hrow[:, i % 2, :], xo[:, i, :], rs[:, 1, i:i + 1]).then_inc(s_h2, 1)
                elif kind == "route":
                    i = item[1]
                    o = take(P_AT[item])
                    dve.tensor_tensor(logit[:, i, :], o[:, 0:NG + E], rb[:], ALU.add).then_inc(s_pempty, 1)
                    landed(dve, item)
                elif kind == "pick":
                    i = item[1]
                    g, e = logit[:, i, 0:NG], logit[:, i, NG:]
                    top, v1, v2 = pick[:, 3, 8:9], picks[:, i, 1:2], picks[:, i, 2:3]
                    first_max(g, NG, top, pick[:, 3, 0:NG], i)
                    link(dve.tensor_scalar(picks[:, i, 3:4], top, -1.0, None, ALU.mult))
                    link(dve.tensor_scalar(pick[:, 3, 0:NG], pick[:, 3, 0:NG], -NEG, NEG, ALU.mult, ALU.add))
                    link(dve.tensor_tensor(pick[:, 0, :].rearrange("p (g e) -> p g e", g=NG),
                                           e.rearrange("p (g e) -> p g e", g=NG),
                                           pick[:, 3, 0:NG].unsqueeze(2).to_broadcast([P, NG, EPG]), ALU.add))
                    first_max(pick[:, 0, :], E, v1, oh[:, i, 0, :], i)
                    link(dve.scalar_tensor_tensor(out=pick[:, 0, :], in0=oh[:, i, 0, :], scalar=2 * NEG,
                                                  in1=pick[:, 0, :], op0=ALU.mult, op1=ALU.add))
                    first_max(pick[:, 0, :], E, v2, oh[:, i, 1, :], i)
                    dve.tensor_tensor(mem[:, i, :], oh[:, i, 0, :], oh[:, i, 1, :], ALU.add).then_inc(s_pick, 1)
                elif kind == "rank":
                    i = item[1]
                    o = take(P_AT[item])
                    dve.tensor_copy(rank[:, i, :], o[:, 0:E]).then_inc(s_pempty, 1)
                    dve.wait_ge(s_pempty, P_AT[item] + 1)
                    link(dve.scalar_tensor_tensor(out=rankm[:], in0=rank[:, i, :], scalar=1.0, in1=mem[:, i, :],
                                                  op0=ALU.add, op1=ALU.mult))
                    if i:
                        dve.wait_ge(s_pfull, P_AT[("slot", i - 1)] + 1)
                    dve.tensor_tensor(spread.rearrange("p (e s) -> p e s", e=E),
                                      rankm[:].unsqueeze(2).to_broadcast([P, E, CAP]),
                                      iota_s[:].unsqueeze(1).to_broadcast([P, E, CAP]), ALU.is_equal).then_inc(s_spread, 1)
                elif kind == "slot":
                    i = item[1]
                    o = take(P_AT[item])
                    dve.tensor_copy(slotf[:, i, :], o[:, 0:PAIRS]).then_inc(s_pempty, 1)
                elif kind == "slots":
                    dve.wait_ge(s_pempty, P_AT[("slot", NT - 1)] + 1)
                    link(dve.tensor_reduce(slott[:], slotf[:].rearrange("p i q -> p q i"), AX.X, ALU.add))
                    dve.tensor_copy(idx[:], slott[:]).then_inc(s_idx, 1)
                elif kind == "count":
                    o = take(P_AT[item])
                    dve.tensor_reduce(busiest[:], o[:, 0:E], AX.X, ALU.max).then_inc(s_pempty, 1)
                    landed(dve, item)
                    dve.tensor_copy(crowd[:], busiest[:]).then_inc(s_crowd, 1)
                elif kind == "weights":
                    i = item[1]
                    w = lambda c: tw[:, i, c:c + 1]
                    dve.wait_ge(s_gexp, 2 * i + 2)
                    link(dve.reciprocal(w(0), gsc[:, i, 0:1]))
                    link(dve.tensor_scalar(w(1), gsc[:, i, 1:2], 1.0, None, ALU.add))
                    link(dve.reciprocal(w(2), w(1)))
                    link(dve.tensor_tensor(w(3), w(0), w(2), ALU.mult))
                    link(dve.tensor_tensor(w(4), w(3), gsc[:, i, 1:2], ALU.mult))
                    for k in range(2):
                        link(dve.tensor_tensor_reduce(pick[:, 1, :], oh[:, i, k, :], rank[:, i, :], 1.0, 0.0,
                                                      ALU.mult, ALU.add, w(5 + k)))
                        link(dve.tensor_tensor_reduce(pick[:, 2, :], oh[:, i, k, :], iota_e[:], 1.0, 0.0,
                                                      ALU.mult, ALU.add, w(7 + k)))
                    link(dve.tensor_scalar(tw[:, i, 9:11], tw[:, i, 5:7], float(CAP), None, ALU.is_lt))
                    link(dve.tensor_tensor(comb[:, i, :], tw[:, i, 3:5], tw[:, i, 9:11], ALU.mult))
                    link(dve.tensor_scalar(tw[:, i, 5:7], tw[:, i, 5:7], CAP - 1.0, None, ALU.min))
                    link(dve.scalar_tensor_tensor(out=posf[:, i, :], in0=tw[:, i, 7:9], scalar=float(CAP),
                                                  in1=tw[:, i, 5:7], op0=ALU.mult, op1=ALU.add))
                    link(dve.tensor_scalar(pick[:, 0, :], oh[:, i, 0, :], w(3), None, ALU.mult))
                    link(dve.scalar_tensor_tensor(out=pick[:, 1, :], in0=oh[:, i, 1, :], scalar=w(4),
                                                  in1=pick[:, 0, :], op0=ALU.mult, op1=ALU.add))
                    link(dve.scalar_tensor_tensor(out=late[:, i, :], in0=rank[:, i, :], scalar=float(CAP),
                                                  in1=pick[:, 1, :], op0=ALU.is_ge, op1=ALU.mult))
                    if i == NT - 1:
                        dve.tensor_copy(pos[:], posf[:].rearrange("p i k -> p (i k)")).then_inc(s_pos, 1)

            def pair_steps(it, j, first):
                q = 2 * it + j
                for z in range(2):
                    e = 4 * it + (2 * j + z)
                    dve.wait_ge(s_silu, e + 1)
                    if not (first and j == 0):
                        dve.wait_ge(s_down, 4 * it + (2 * j + z - 1))
                    dve.tensor_tensor(hid[:, z, :], gate_act[:, z, :], sbank[z][:, FT * CAP:2 * FT * CAP],
                                      ALU.mult).then_inc(s_hid, 1)
                dve.wait_ge(s_down, 2 * q + 2)
                if first and j == 0:
                    for i in range(NT):
                        dve.wait_ge(s_h2out[i], 16)
                if not first:
                    dve.wait_ge(s_yst[j], 16 * it)
                dve.tensor_copy(yrow[:, j, 0:512], (pbank, obank)[j][0][:]).then_inc(s_yd, 1)

            for j in range(2):
                pair_steps(0, j, True)
            with dve.Fori(1, E // 4, 1) as it:
                for j in range(2):
                    pair_steps(it, j, False)

            dve.wait_ge(s_crowd, 1)
            with dve.register("dve_crowd") as r:
                dve.reg_load(r, crowd[0:1, 0:1])
                with dve.If(dve.snap(r) > CAP):
                    with dve.Fori(0, E, 1) as e:
                        dve.tensor_copy(lcur[:], late[:, :, bass.ds(e, 1)].rearrange("p i e -> p (i e)")).then_inc(s_dcur, 1)
                        dve.wait_ge(s_dcur, e + 1)
                        for a in range(FT):
                            dve.wait_ge(s_dsilu, FT * e + (a + 1))
                            dve.tensor_tensor(dense_hid[:, a, :], dense_act[:, a, :], pbank[1][:], ALU.mult).then_inc(s_dhid, 1)
                        for i in range(NT):
                            for half in range(2):
                                dve.wait_ge(s_dy, 2 * NT * e + (2 * i + half + 1))
                                x2 = xo[:, i, half * 512:(half + 1) * 512]
                                dve.scalar_tensor_tensor(out=x2, in0=obank[half][:], scalar=lcur[:, i:i + 1], in1=x2,
                                                         op0=ALU.mult, op1=ALU.add).then_inc(s_dacc, 1)
                        dve.wait_ge(s_dacc, 2 * NT * e + 2 * NT)

            dve.wait_ge(s_lnfb, 16)
            for i in range(NT):
                dve.wait_ge(s_yg[i], 32)
                for k in range(2):
                    dve.scalar_tensor_tensor(out=xo[:, i, :], in0=ybuf[:, i, k, :], scalar=comb[:, i, k:k + 1],
                                             in1=xo[:, i, :], op0=ALU.mult, op1=ALU.add).then_inc(s_sum, 1)
                    dve.wait_ge(s_sum, 2 * i + k + 1)
                dve.wait_ge(s_rs3, i + 1)
                dve.scalar_tensor_tensor(out=orow[:, i, :], in0=xo[:, i, :], scalar=rs[:, 2, i:i + 1], in1=lnfb,
                                         op0=ALU.mult, op1=ALU.mult).then_inc(s_orow, 1)


def bucket_tables():
    import numpy as np
    dist = S - 1 - np.arange(SPAN)
    d = np.maximum(dist, 0)
    exact = BUCKETS // 2
    large = exact + (np.log(np.maximum(d, 1) / exact) / math.log(2048 / exact) * (BUCKETS - exact)).astype(np.int32)
    bucket = np.where(d < exact, d, np.minimum(large, BUCKETS - 1))
    rows = np.zeros((BUCKETS + 2, SPAN), np.float32)
    past = dist >= 0
    rows[bucket[past], np.nonzero(past)[0]] = 1.0
    held = sum(((d % dil == 0) & (d <= window)).astype(int) for window, dil in ((128, 1), (512, 4), (2048, 16)))
    rows[BUCKETS, past] = np.where(held > 0, np.log(np.maximum(held, 1)), NEG)[past]
    rows[BUCKETS + 1, ~past] = NEG
    cols = np.zeros((2, 12), np.float32)
    cols[0, 0:H] = 1.0
    cols[1, :] = 1.0
    return rows, cols


_INS = ["x", "rel_bias", "ln1", "w_in", "w_out", "lam_q1", "lam_k1", "lam_q2", "lam_k2", "subln_g", "b_forget",
        "ln2", "w_group", "b_group", "w_expert", "b_expert", "w_gate", "w_up", "w_down", "ln_f"]


def kernel(**inputs):
    import numpy as _np
    import concourse.bacc as _bacc
    from concourse import mybir as _mybir
    from concourse.bass_utils import run_bass_kernel_spmd as _run

    nc = _bacc.Bacc("TRN2", target_bir_lowering=False, num_devices=1)
    arrays, args = {}, []
    host = {name: _np.ascontiguousarray(inputs[name]) for name in _INS}
    host["bucket_rows"], host["bias_cols"] = bucket_tables()
    for name, a in host.items():
        arrays[f"in_{name}_dram"] = a
        args.append(nc.dram_tensor(f"in_{name}_dram", a.shape, _mybir.dt.from_np(a.dtype), kind="ExternalInput").ap())
    args.append(nc.dram_tensor("out_0_dram", (1, S, D), F32, kind="ExternalOutput").ap())
    hybrid_layer(nc, *args)
    r = _run(nc, [arrays], core_ids=[0])
    return r.results[0]["out_0_dram"]
```

```python
import math
from contextlib import ExitStack

import concourse.bass as bass
from concourse import mybir

ALU = mybir.AluOpType
ACT = mybir.ActivationFunctionType
AX = mybir.AxisListType
F32 = mybir.dt.float32
BF16 = mybir.dt.bfloat16
U32 = mybir.dt.uint32
I32 = mybir.dt.int32

P = 128
S = 512
D = 1024
NT = S // P
KC = D // P
HD = 64
H = 4
GW = H * HD
A, B, C, F = range(4)
BUCKETS = 32
SPAN = S + P - 1
NEG = -1e30
EPS = 1e-6
LAMBDA_INIT = 0.8 - 0.6 * math.exp(-0.3 * 0)

NG, EPG = 4, 8
E = NG * EPG
FE = D // 4
FT = FE // P
CAP = 64
PAIRS = E // 2
SLOT = KC * GW
NSLOT = 12


def plan_front():
    def project(m, groups):
        return [("proj", m, g, s) for g in groups for s in range(KC)]

    plan = [("table",)]
    for i in range(NT + 1):
        plan += [("ln1", i)] if i < NT else []
        plan += [("hT", i - 1)] if i else []
    plan += project(A, range(6))
    fill = {A: project(B, range(6)), B: project(C, range(6)), C: project(F, range(8))}
    n_units = 4 * 4 * NT
    per_mixer = 4 * NT
    for n in range(n_units + 8):
        m, at = divmod(n, per_mixer)
        between = []
        if m < F:
            count = len(fill[m])
            between = fill[m][at * count // per_mixer:(at + 1) * count // per_mixer]
        if n == per_mixer * F:
            plan.append(("z",))
        if 0 <= n - per_mixer * F < H:
            plan.append(("cb", n - per_mixer * F))
        if n < n_units:
            plan.append(("score", n))
        i, r = divmod(n - per_mixer * F - 8, 4)
        if 0 <= i < NT:
            half = lambda z: [("out", i, z, s) for s in range(KC)]
            if r == 0:
                plan.append(("oT", i))
                if i:
                    plan += [("h2T", i - 1), ("route", i - 1), ("pick", i - 1)]
                between = half(0)[0:2]
            elif r == 1:
                between = half(0)[2:]
            elif r == 2:
                if i:
                    plan.append(("rank", i - 1))
                between = half(1)[0:6]
            else:
                between = half(1)[6:]
        third = -(-len(between) // 3)
        plan += between[0:third]
        if 0 <= n - 1 < n_units and (n - 1) // per_mixer == B:
            plan.append(("mix", n - 1))
        if 0 <= n - 2 < n_units:
            plan.append(("turn", n - 2))
        plan += between[third:2 * third]
        if 0 <= n - 3 < n_units:
            plan.append(("pv", n - 3))
        plan += between[2 * third:]
        if 0 <= n - 4 < n_units and n % 4 == 3:
            plan.append(("onorm", n // 4 - 1))
        if 0 <= i < NT and r == 3:
            if i:
                plan += [("slot", i - 1), ("weights", i - 1)]
            plan.append(("ln2", i))
    last = NT - 1
    plan += [("h2T", last), ("route", last), ("pick", last), ("rank", last), ("slot", last), ("slots",), ("count",)]
    plan.append(("weights", last))
    return plan


def uses(plan, kinds):
    at, first = 0, {}
    for item in plan:
        if item[0] in kinds:
            key = item[:3] if item[0] in ("proj", "out") else item
            if key not in first:
                first[key] = at
                at += kinds[item[0]]
    return first, at


def hybrid_layer(nc, x, rel_bias, ln1, w_in, w_out, lam_q1, lam_k1, lam_q2, lam_k2, subln_g, b_forget,
                 ln2, w_group, b_group, w_expert, b_expert, w_gate, w_up, w_down, ln_f,
                 bucket_rows, bias_cols, out):
    plan = plan_front()
    P_AT, P_N = uses(plan, {"table": 2, "proj": 1, "cb": 1, "out": 1, "route": 1,
                            "rank": 1, "slot": 1, "count": 1})
    T_AT, T_N = uses(plan, {"hT": 2, "turn": 1, "oT": 2, "h2T": 2})
    units = [(n // 16, (n // 4) % 4, n % 4) for n in range(16 * 4)]
    t_of, parts = {}, []
    for n, (m, i, h) in enumerate(units):
        for s in range(2 if m == B else 1):
            t_of[(n, s)] = len(parts)
            parts.append((n, s))

    with ExitStack() as ctx:
        def sb(name, shape, dt=F32):
            return ctx.enter_context(nc.sbuf_tensor(name, shape, dt))

        def sem(name):
            return ctx.enter_context(nc.semaphore(name))

        bank = {b: ctx.enter_context(nc.psum_tensor(f"bank_{b}", [P, 512], F32))
                for b in ("P0", "P1", "S0", "S1", "T0", "T1", "O0", "O1")}
        pbank = [bank["P0"], bank["P1"]]
        sbank = [bank["S0"], bank["S1"]]
        tbank = [bank["T0"], bank["T1"]]
        obank = [bank["O0"], bank["O1"]]

        zcols = H * KC
        ring_flat = sb("ring", [P, NSLOT * SLOT + zcols])
        ring = ring_flat[:, 0:NSLOT * SLOT].rearrange("p (a b) -> p a b", a=NSLOT)
        fv = ring_flat[:, (NSLOT - 1) * SLOT:].rearrange("p (c n) -> p c n", c=KC)
        hT = sb("hT", [P, KC, S])
        xo = sb("xo", [P, NT, D])
        qk = sb("qk", [P, 2, 4, S])
        vv = sb("vv", [P, 2, NT, GW])
        gb = sb("gb", [P, 2, H, S])
        sc = sb("sc", [P, 4, S])
        pt = sb("pt", [P, 2, S])
        hrow = sb("hrow", [P, 2, D])
        junk = sb("junk", [P, D], BF16)
        sqh = sb("sqh", [P, GW])
        lnb = sb("lnb", [P, D])
        ident = sb("ident", [P, P])
        upto = sb("upto", [P, S])
        before = sb("before", [P, P])
        future = sb("future", [P, P])
        iota_e = sb("iota_e", [P, E])
        iota_s = sb("iota_s", [P, CAP])
        token = sb("token", [P, 2], BF16)
        relb = sb("relb", [BUCKETS + 2, 12])
        lamv = sb("lamv", [P, 4, HD // 2])
        lams = sb("lams", [P, 8])
        subg = sb("subg", [P, HD])
        bf = sb("bf", [P, H])
        wr = sb("wr", [P, KC, NG + E])
        rb = sb("rb", [P, NG + E])
        ms = sb("ms", [P, 4, NT])
        rs = sb("rs", [P, 3, NT])
        negmax = sb("negmax", [P, len(parts)])
        lsum = sb("lsum", [P, len(parts)])
        linv = sb("linv", [P, len(parts)])
        mixc = sb("mixc", [P, 16])
        power = sb("power", [P, H])
        rtmp = sb("rtmp", [P, 4 * NT, H])
        onrm = sb("onrm", [P, 2, H])
        zraw = sb("zraw", [P, NT, H])
        zt = sb("zt", [P, 4, NT * H])
        logit = sb("logit", [P, NT, NG + E])
        pick = sb("pick", [P, 4, E])
        picks = sb("picks", [P, NT, 4])
        oh = sb("oh", [P, NT, 2, E])
        mem = sb("mem", [P, NT, E])
        rank = sb("rank", [P, NT, E])
        rankm = sb("rankm", [P, E])
        slotf = sb("slotf", [P, NT, 2 * PAIRS])
        slott = sb("slott", [P, PAIRS])
        idx = sb("idx", [P, PAIRS], U32)
        gexp = sb("gexp", [P, NT, NG])
        gsc = sb("gsc", [P, NT, 4])
        tw = sb("tw", [P, NT, 12])
        comb = sb("comb", [P, NT, 2])
        posf = sb("posf", [P, NT, 2])
        pos = sb("pos", [P, NT * 2], U32)
        late = sb("late", [P, NT, E])
        lcur = sb("lcur", [P, NT])
        busiest = sb("busiest", [P, 1])
        crowd = sb("crowd", [P, 1], I32)

        onehot_rows = sc[0:BUCKETS + 2, 0:2, :].rearrange("p a b -> p (a b)")[:, 0:SPAN]
        table_rows = sc[0:12, 2:4, :].rearrange("p a b -> p (a b)")[:, 0:SPAN]
        oT = vv[:, 0, :, :].rearrange("p i n -> p (i n)").rearrange("p (c t) -> p c t", c=KC)
        xres = qk[:, 0, :, :].rearrange("p (a b) s -> p a (b s)", a=2)
        spread = gb[:, 0, 0:2, :].rearrange("p a b -> p (a b)").bitcast(BF16)
        wout = ring[:, 0:4, :].rearrange("p a b -> p (a b)").rearrange("p (c n) -> p c n", c=KC)
        xg = qk[:, 1, :, :].rearrange("p (a b) s -> p a (b s)", a=2)
        xgT = gb[:, 1, :, :].rearrange("p a b -> p (a b)").rearrange("p (c s) -> p c s", c=2 * KC)
        lnfb = gb[:, 0, 2:4, :].rearrange("p a b -> p (a b)")
        yrow = hrow
        gate_act = sc[:, 0:2, 0:FT * CAP]
        hid = sc[:, 2:4, 0:FT * CAP]
        ybuf = ring[:, 0:4, :].rearrange("p a b -> p (a b)").rearrange("p (i k n) -> p i k n", i=NT, k=2)
        orow = ring[:, 4:6, :].rearrange("p a b -> p (a b)").rearrange("p (i n) -> p i n", i=NT)
        dense_act = qk[:, 0, 0:2, :]
        dense_hid = qk[:, 0, 2:4, :]

        table_d = nc.dram_tensor("table_scratch", (12, SPAN), F32, kind="Internal").ap()
        h2_d = nc.dram_tensor("h2_scratch", (S, D), F32, kind="Internal").ap()
        y_d = nc.dram_tensor("y_scratch", (E * CAP, D), F32, kind="Internal").ap()

        s_xin = [sem(f"s_xin{i}") for i in range(NT)]
        s_tabin, s_ln1b, s_small, s_ln2b, s_lnfb = map(sem, ("s_tabin", "s_ln1b", "s_small", "s_ln2b", "s_lnfb"))
        s_win = [sem(f"s_win{i}") for i in range(12)]
        s_wout = [sem(f"s_wout{i}") for i in range(4)]
        s_strip = [sem(f"s_strip{m}") for m in range(3)]
        s_xres = [sem(f"s_xres{i}") for i in range(2)]
        s_tabout = sem("s_tabout")
        s_h2out = [sem(f"s_h2out{i}") for i in range(NT)]
        s_const, s_pool = sem("s_const"), sem("s_pool")
        s_lfused, s_zraw = sem("s_lfused"), sem("s_zraw")
        N_SMALL = 10
        s_sq, s_hrow = sem("s_sq"), sem("s_hrow")
        s_pfull, s_pempty = sem("s_pfull"), sem("s_pempty")
        s_tfull, s_tempty = sem("s_tfull"), sem("s_tempty")
        s_score, s_biased, s_exp, s_mix = map(sem, ("s_score", "s_biased", "s_exp", "s_mix"))
        s_pv, s_onorm = sem("s_pv"), sem("s_onorm")
        s_lam, s_lamexp = sem("s_lam"), sem("s_lamexp")
        s_zin, s_zabs, s_zexp, s_zln, s_lf = map(sem, ("s_zin", "s_zabs", "s_zexp", "s_zln", "s_lf"))
        s_x2, s_sq2, s_h2 = map(sem, ("s_x2", "s_sq2", "s_h2"))
        s_pick, s_gexp, s_spread, s_idx, s_pos, s_crowd = map(
            sem, ("s_pick", "s_gexp", "s_spread", "s_idx", "s_pos", "s_crowd"))
        s_dve = sem("s_dve")
        s_rs1, s_rs2, s_rs3, s_osq, s_ors, s_root = map(sem, ("s_rs1", "s_rs2", "s_rs3", "s_osq", "s_ors", "s_root"))
        s_wgu = [sem(f"s_wgu{b}") for b in range(4)]
        s_wdn = [sem(f"s_wdn{b}") for b in range(4)]
        s_xg = [sem(f"s_xg{b}") for b in range(2)]
        s_yst = [sem(f"s_yst{b}") for b in range(2)]
        s_mt, s_mx, s_gu, s_silu, s_hid, s_down, s_yd, s_ya = map(
            sem, ("s_mt", "s_mx", "s_gu", "s_silu", "s_hid", "s_down", "s_yd", "s_ya"))
        s_dw, s_dgu, s_dsilu, s_dhid, s_dy, s_dacc, s_dcur = map(
            sem, ("s_dw", "s_dgu", "s_dsilu", "s_dhid", "s_dy", "s_dacc", "s_dcur"))
        s_yg = [sem(f"s_yg{i}") for i in range(NT)]
        s_sum, s_sq3, s_orow, s_out = map(sem, ("s_sum", "s_sq3", "s_orow", "s_out"))

        def landed(eng, item, n=1):
            eng.wait_ge(s_pempty, P_AT[item] + n)

        def turned(eng, item, n=1):
            eng.wait_ge(s_tempty, T_AT[item] + n)

        win_d = w_in[0].rearrange("(p c) n -> p c n", c=KC)
        wout_d = w_out[0].rearrange("(c p) n -> p c n", p=P)

        def expert_chunks(e, b):
            s = 3 * b
            wide = lambda t: ring[:, t, :].rearrange("p (c f) -> p c f", c=KC)
            return ((wide(s), w_gate[0, bass.ds(e, 1)].rearrange("e (p c) f -> p (e c) f", c=KC)),
                    (wide(s + 1), w_up[0, bass.ds(e, 1)].rearrange("e (p c) f -> p (e c) f", c=KC)),
                    (ring[:, s + 2, :].rearrange("p (a n) -> p a n", a=FT),
                     w_down[0, bass.ds(e, 1)].rearrange("e (a p) n -> p (e a) n", p=P)))

        def load_gate_up(eng, e, b):
            for dst, src in expert_chunks(e, b)[0:2]:
                eng.dma_start(dst, src).then_inc(s_wgu[b], 16)

        def load_down(eng, e, b):
            dst, src = expert_chunks(e, b)[2]
            eng.dma_start(dst, src).then_inc(s_wdn[b], 16)

        def gate_up(b):
            return [ring[:, 3 * b + z, :].rearrange("p (c f) -> p c f", c=KC) for z in range(2)]

        def down(b):
            return ring[:, 3 * b + 2, :].rearrange("p (a n) -> p a n", a=FT)

        def strip(m):
            return bass.AP(table_d.tensor, m * H * SPAN, [[1, P], [SPAN, H], [1, S]])

        def falling(v):
            return v[:, :, ::-1]

        def lfb_view(i):
            return hrow[:, 0, (i % 2) * P:(i % 2 + 1) * P]

        block = ctx.enter_context(nc.Block())

        @block.sync
        def _(sp):
            for i in range(NT):
                sp.dma_start(xo[:, i, :], x[0, i * P:(i + 1) * P, :]).then_inc(s_xin[i], 16)
                if i == 0:
                    sp.dma_start(lnb[:], ln1.to_broadcast([P, D])).then_inc(s_ln1b, 16)
            for g in range(12):
                wide = g == 11
                sp.dma_start(fv if wide else ring[:, g, :].rearrange("p (c n) -> p c n", c=KC),
                             win_d[:, :, g * GW:(g + 1) * GW + H * wide]).then_inc(s_win[g], 16)
                if g == 1:
                    sp.wait_ge(s_tabout, 16)
                    for m in (A, B):
                        sp.dma_start(gb[:, m % 2], strip(m)).then_inc(s_strip[m], 16)
            sp.wait_ge(s_hrow, NT)
            sp.dma_start(lnb[:], ln2.to_broadcast([P, D])).then_inc(s_ln2b, 16)
            for j in range(4):
                sp.wait_ge(s_pfull, P_AT[("proj", j // 3, 2 * (j % 3) + 1)] + 1)
                sp.dma_start(ring[:, j, :].rearrange("p (c n) -> p c n", c=2),
                             wout_d[:, 2 * j:2 * j + 2, :]).then_inc(s_wout[j], 16)
            sp.wait_ge(s_biased, t_of[(16 * B - 1, 0)] + 1)
            sp.dma_start(gb[:, 0], strip(C)).then_inc(s_strip[C], 16)
            for z, (m, g) in enumerate(((C, 5), (F, 7))):
                sp.wait_ge(s_pfull, P_AT[("proj", m, g)] + 1)
                load_gate_up(sp, z, z + 2)
                load_down(sp, z, z + 2)
            sp.wait_ge(s_score, t_of[(16 * F - 1, 0)] + 1)
            for i in range(2):
                sp.dma_start(xres[:, i], x[0, i * P:(i + 1) * P, :]).then_inc(s_xres[i], 16)
            for i in range(NT):
                if i + 2 < NT:
                    landed(sp, ("out", i, 1))
                    sp.dma_start(xres[:, i], x[0, (i + 2) * P:(i + 3) * P, :]).then_inc(s_xres[i], 16)
                if i == NT - 1:
                    sp.wait_ge(s_pfull, P_AT[("out", i, 1)] + 1)
                    for z in range(2):
                        load_gate_up(sp, 2 + z, z)
                        load_down(sp, 2 + z, z)
                sp.wait_ge(s_h2, i + 1)
                sp.dma_start(h2_d[i * P:(i + 1) * P, :], hrow[:, i % 2, :]).then_inc(s_h2out[i], 16)
            sp.wait_ge(s_pfull, P_AT[("slot", NT - 1)] + 1)
            sp.dma_start(lnfb, ln_f.rearrange("(a n) -> a n", a=1).to_broadcast([P, D])).then_inc(s_lnfb, 16)
            with sp.Fori(1, E // 4, 1) as it:
                for pair in range(2):
                    for j in (2 * pair, 2 * pair + 1):
                        sp.wait_ge(s_gu, 4 * it + (j - 3))
                        load_gate_up(sp, 4 * it + j, (j + 2) % 4)
                    for j in (2 * pair, 2 * pair + 1):
                        sp.wait_ge(s_down, 4 * it + (j - 3))
                        load_down(sp, 4 * it + j, (j + 2) % 4)
            sp.wait_ge(s_crowd, 1)
            with sp.register("sp_crowd") as r:
                sp.reg_load(r, crowd[0:1, 0:1])
                with sp.If(sp.snap(r) > CAP):
                    sp.wait_ge(s_down, E)
                    with sp.Fori(0, E, 1) as e:
                        sp.wait_ge(s_dcur, e + 1)
                        for dst, src in expert_chunks(e, 0):
                            sp.dma_start(dst, src).then_inc(s_dw, 16)
            for i in range(NT):
                sp.wait_ge(s_orow, i + 1)
                sp.dma_start(out[0, i * P:(i + 1) * P, :], orow[:, i, :]).then_inc(s_out, 16)
            sp.wait_ge(s_out, 16 * NT)

        @block.gpsimd
        def _(pool):
            made = 0
            for tile, value in ((ident, 0.0), (upto, 1.0), (before, 1.0), (future, 0.0),
                                (power, -0.5)):
                pool.memset(tile[:], value).then_inc(s_pool, 1)
                made += 1
            pool.iota(iota_e[:], [[1, E]], base=0, channel_multiplier=0,
                      allow_small_or_imprecise_dtypes=True).then_inc(s_const, 1)
            pool.iota(iota_s[:], [[1, CAP]], base=1, channel_multiplier=0,
                      allow_small_or_imprecise_dtypes=True).then_inc(s_const, 1)
            pool.iota(token[:, 0:1], [[0, 1]], base=0, channel_multiplier=1,
                      allow_small_or_imprecise_dtypes=True).then_inc(s_const, 1)
            pool.memset(token[:, 1:2], 1.0).then_inc(s_const, 1)
            pool.wait_ge(s_pool, made)
            for tile, op, fill, base, step, cm in (
                    (ident, ALU.not_equal, 1.0, 0, -1, 1), 
                    (upto, ALU.is_ge, 0.0, 0, 1, -1), (before, ALU.is_gt, 0.0, 0, 1, -1),
                    (future, ALU.is_ge, NEG, P - 1, -1, -1)):
                pool.affine_select(out=tile[:], in_=tile[:], compare_op=op, fill=fill, base=base,
                                   pattern=[[step, tile.shape[1]]], channel_multiplier=cm).then_inc(s_const, 1)
            roots = [0]

            def inverse_root(dst, src, scale):
                n = src.shape[1]
                tmp = rtmp[:, roots[0], 0:n]
                roots[0] += 1
                pool.tensor_scalar(tmp, src, scale, EPS, ALU.mult, ALU.add).then_inc(s_root, 1)
                pool.wait_ge(s_root, roots[0])
                return pool.tensor_tensor(dst, tmp, power[:, 0:n], ALU.pow)

            for item in plan:
                kind = item[0]
                if kind == "ln1":
                    i = item[1]
                    pool.wait_ge(s_sq, i + 1)
                    inverse_root(rs[:, 0, i:i + 1], ms[:, 0, i:i + 1], 1.0).then_inc(s_rs1, 1)
                elif kind == "ln2":
                    i = item[1]
                    pool.wait_ge(s_sq2, i + 1)
                    inverse_root(rs[:, 1, i:i + 1], ms[:, 1, i:i + 1], 1.0).then_inc(s_rs2, 1)
                elif kind == "onorm" and item[1] // 4 == B:
                    pool.wait_ge(s_osq, item[1] - 4 * B + 1)
                    inverse_root(onrm[:, 1, :], onrm[:, 0, :], 1.0 / HD).then_inc(s_ors, 1)

            def gather(pair):
                pool.indirect_dma_start(out=xg[:, pair % 2], out_offset=None, in_=h2_d[:, :],
                                        in_offset=bass.IndirectOffsetOnAxis(ap=idx[:, pair:pair + 1], axis=0)
                                        ).then_inc(s_xg[pair % 2], 16)

            pool.wait_ge(s_idx, 1)
            for i in range(NT):
                pool.wait_ge(s_h2out[i], 16)
            gather(0)
            gather(1)
            for pair in range(PAIRS):
                if pair + 2 < PAIRS:
                    pool.wait_ge(s_mt, 2 * pair + 2)
                    gather(pair + 2)
                pool.wait_ge(s_yd, pair + 1)
                pool.wait_ge(s_ya, pair + 1)
                pool.dma_start(y_d[pair * P:(pair + 1) * P, :], yrow[:, pair % 2, :]).then_inc(s_yst[pair % 2], 16)
            for j in range(2):
                pool.wait_ge(s_yst[j], 16 * (PAIRS // 2))
            pool.wait_ge(s_pos, 1)
            pool.wait_ge(s_crowd, 1)
            pool.wait_ge(s_down, E)
            with pool.register("pool_crowd") as r:
                pool.reg_load(r, crowd[0:1, 0:1])
                with pool.If(pool.snap(r) > CAP):
                    pool.wait_ge(s_dacc, 2 * NT * E)
            for i in range(NT):
                for k in range(2):
                    n = 2 * i + k
                    pool.indirect_dma_start(out=ybuf[:, i, k], out_offset=None, in_=y_d[:, :],
                                            in_offset=bass.IndirectOffsetOnAxis(ap=pos[:, n:n + 1], axis=0)
                                            ).then_inc(s_yg[i], 16)
            for i in range(NT):
                pool.wait_ge(s_sq3, i + 1)
                inverse_root(rs[:, 2, i:i + 1], ms[:, 2, i:i + 1], 1.0).then_inc(s_rs3, 1)

        @block.scalar
        def _(act):
            act.dma_start(onehot_rows, bucket_rows).then_inc(s_tabin, 16)
            act.dma_start(relb[0:BUCKETS, :], rel_bias).then_inc(s_tabin, 16)
            act.dma_start(relb[BUCKETS:BUCKETS + 2, :], bias_cols).then_inc(s_tabin, 16)

            def copy_out(k, dst, src):
                act.wait_ge(s_tfull, k + 1)
                act.activation(dst, src, ACT.Copy).then_inc(s_tempty, 1)

            for item in plan:
                kind = item[0]
                if kind == "hT" and item[1] == NT - 1:
                    for z, v in enumerate((lam_q1, lam_k1, lam_q2, lam_k2)):
                        act.dma_start(lamv[:, z, :], v.to_broadcast([P, HD // 2])).then_inc(s_small, 16)
                    act.dma_start(subg[:], subln_g.to_broadcast([P, HD])).then_inc(s_small, 16)
                    act.dma_start(bf[:], b_forget.to_broadcast([P, H])).then_inc(s_small, 16)
                    act.dma_start(wr[:, :, 0:NG], w_group[0].rearrange("(p c) n -> p c n", c=KC)).then_inc(s_small, 16)
                    act.dma_start(wr[:, :, NG:], w_expert[0].rearrange("(p c) n -> p c n", c=KC)).then_inc(s_small, 16)
                    act.dma_start(rb[:, 0:NG], b_group.to_broadcast([P, NG])).then_inc(s_small, 16)
                    act.dma_start(rb[:, NG:], b_expert[0:1].rearrange("a g e -> a (g e)").to_broadcast([P, E])).then_inc(s_small, 16)
                if kind == "table":
                    landed(act, item, 2)
                    act.dma_start(table_d, table_rows).then_inc(s_tabout, 16)
                elif kind == "ln1":
                    i = item[1]
                    act.wait_ge(s_xin[i], 16)
                    if i:
                        act.wait_ge(s_sq, i)
                    act.activation(junk[:], xo[:, i, :], ACT.Square, scale=1.0 / 32,
                                   accum_out=ms[:, 0, i:i + 1]).then_inc(s_sq, 1)
                elif kind in ("hT", "h2T"):
                    i = item[1]
                    for z in range(2):
                        k = T_AT[item] + z
                        copy_out(k, hT[:, 4 * z:4 * z + 4, i * P:(i + 1) * P],
                                 tbank[k % 2][:].rearrange("p (c t) -> p c t", c=4))
                elif kind == "score":
                    n = item[1]
                    if n == 16 * A:
                        act.wait_ge(s_lam, 2)
                        act.activation(lams[:, 2:4], lams[:, 0:2], ACT.Exp).then_inc(s_lamexp, 1)
                    m, i, h = units[n]
                    for s in range(2 if m == B else 1):
                        t = t_of[(n, s)]
                        e = sc[:, t % 4, 0:(i + 1) * P]
                        act.wait_ge(s_biased, t + 1)
                        act.activation(e, e, ACT.Exp, bias=negmax[:, t:t + 1], scale=-1.0,
                                       accum_out=lsum[:, t:t + 1]).then_inc(s_exp, 1)
                elif kind == "turn":
                    n = item[1]
                    k = T_AT[item]
                    nk = (units[n][1] + 1) * P
                    if n >= 2:
                        act.wait_ge(s_pv, n - 1)
                    copy_out(k, pt[:, n % 2, 0:nk], tbank[k % 2][:, 0:nk])
                elif kind == "z":
                    act.wait_ge(s_zin, 1)
                    act.activation(zt[:, 1, :], zt[:, 0, :], ACT.Abs).then_inc(s_zabs, 1)
                    act.wait_ge(s_zabs, 1)
                    act.activation(zt[:, 2, :], zt[:, 1, :], ACT.Exp, scale=-1.0).then_inc(s_zexp, 1)
                    act.wait_ge(s_zexp, 1)
                    act.activation(zt[:, 3, :], zt[:, 2, :], ACT.Ln, bias=1.0).then_inc(s_zln, 1)
                elif kind == "oT":
                    i = item[1]
                    for z in range(2):
                        k = T_AT[item] + z
                        if i and not z:
                            act.wait_ge(s_pfull, P_AT[("out", i - 1, 1)] + 1)
                        copy_out(k, falling(oT[:, 4 * z:4 * z + 4, :]), tbank[k % 2][:].rearrange("p (c t) -> p c t", c=4))
                elif kind == "ln2":
                    i = item[1]
                    landed(act, ("out", i, 1))
                    if i:
                        act.wait_ge(s_sq2, i)
                    act.activation(junk[:], xo[:, i, :], ACT.Square, scale=1.0 / 32,
                                   accum_out=ms[:, 1, i:i + 1]).then_inc(s_sq2, 1)
                elif kind == "weights":
                    i = item[1]
                    act.wait_ge(s_pick, i + 1)
                    act.activation(gexp[:, i, :], logit[:, i, 0:NG], ACT.Exp, bias=picks[:, i, 3:4],
                                   accum_out=gsc[:, i, 0:1]).then_inc(s_gexp, 1)
                    act.activation(gsc[:, i, 1:2], picks[:, i, 1:2], ACT.Exp, scale=-1.0,
                                   bias=picks[:, i, 2:3]).then_inc(s_gexp, 1)

            def rows_to_chunks(q, first, j):
                for z in range(2):
                    act.wait_ge(s_mt, 2 * q + (z + 1))
                    act.activation(xgT[:, 8 * j + 4 * z:8 * j + 4 * z + 4, :],
                                   tbank[z][:].rearrange("p (c t) -> p c t", c=4), ACT.Copy).then_inc(s_mx, 1)

            def pair_steps(it, j, first, last):
                q = 2 * it + j
                for z in range(2):
                    e = 4 * it + (2 * j + z)
                    act.wait_ge(s_gu, e + 1)
                    act.activation(gate_act[:, z, :], sbank[z][:, 0:FT * CAP], ACT.Silu).then_inc(s_silu, 1)
                if not (last and j == 1):
                    if not (first and j == 0):
                        act.wait_ge(s_gu, 2 * q)
                    rows_to_chunks(q + 1, first, (j + 1) % 2)
                act.wait_ge(s_down, 2 * q + 2)
                if not first:
                    act.wait_ge(s_yst[j], 16 * it)
                act.activation(yrow[:, j, 512:1024], (pbank, obank)[j][1][:], ACT.Copy).then_inc(s_ya, 1)

            rows_to_chunks(0, True, 0)
            for j in range(2):
                pair_steps(0, j, True, False)
            with act.Fori(1, E // 4 - 1, 1) as it:
                for j in range(2):
                    pair_steps(it, j, False, False)
            for j in range(2):
                pair_steps(E // 4 - 1, j, False, True)

            act.wait_ge(s_crowd, 1)
            with act.register("act_crowd") as r:
                act.reg_load(r, crowd[0:1, 0:1])
                with act.If(act.snap(r) > CAP):
                    with act.Fori(0, E, 1) as e:
                        for a in range(FT):
                            act.wait_ge(s_dgu, FT * e + (a + 1))
                            act.activation(dense_act[:, a, :], pbank[0][:], ACT.Silu).then_inc(s_dsilu, 1)
            for i in range(NT):
                act.wait_ge(s_sum, 2 * i + 2)
                if i:
                    act.wait_ge(s_sq3, i)
                act.activation(junk[:], xo[:, i, :], ACT.Square, scale=1.0 / 32,
                               accum_out=ms[:, 2, i:i + 1]).then_inc(s_sq3, 1)

        @block.tensor
        def _(pe):
            def open_p(k):
                if k >= 2:
                    pe.wait_ge(s_pempty, k - 1)
                return pbank[k % 2]

            def open_t(k):
                if k >= 2:
                    pe.wait_ge(s_tempty, k - 1)
                return tbank[k % 2]

            def turn8(item, src):
                for z in range(2):
                    k = T_AT[item] + z
                    t = open_t(k)
                    for c in range(4):
                        last = pe.transpose(t[:, c * P:(c + 1) * P], src[:, (4 * z + c) * P:(4 * z + c + 1) * P], ident[:])
                    last.then_inc(s_tfull, 1)

            for item in plan:
                kind = item[0]
                if kind == "table":
                    pe.wait_ge(s_const, 8)
                    pe.wait_ge(s_tabin, 48)
                    k = P_AT[item]
                    for z, (a, b) in enumerate(((0, 512), (512, SPAN))):
                        pe.matmul(open_p(k + z)[0:12, 0:b - a], relb[:], onehot_rows[:, a:b],
                                  start=True, stop=True).then_inc(s_pfull, 1)
                elif kind == "hT":
                    i = item[1]
                    pe.wait_ge(s_hrow, i + 1)
                    turn8(item, hrow[:, i % 2, :])
                elif kind == "proj":
                    m, g, step = item[1:]
                    k = P_AT[item[:3]]
                    if (m, g, step) == (A, 0, 0):
                        turned(pe, ("hT", NT - 1), 2)
                    chunk = 3 * m + min(g // 2, 2)
                    if g % 2 == 0 and step == 0:
                        pe.wait_ge(s_win[chunk], 16)
                    w = ring[:, chunk, :].rearrange("p (c n) -> p c n", c=KC)
                    o = pbank[k % 2] if step else open_p(k)
                    if g < 4:
                        last = pe.matmul(o[:], w[:, step, (g % 2) * P:(g % 2 + 1) * P], hT[:, step, :],
                                         start=(step == 0), stop=(step == KC - 1))
                    elif m == F:
                        last = pe.matmul(o[:, 0:GW + H], hT[:, step, (g - 4) * P:(g - 3) * P], fv[:, step, :],
                                         start=(step == 0), stop=(step == KC - 1))
                    else:
                        i, c0 = divmod(2 * step, KC)
                        t0 = (2 * (g - 4) + i) * P
                        for c in (c0, c0 + 1):
                            last = pe.matmul(o[:, i * GW:(i + 1) * GW], hT[:, c, t0:t0 + P], w[:, c, :],
                                             start=(c == 0), stop=(c == KC - 1))
                    if step == KC - 1:
                        last.then_inc(s_pfull, 1)
                elif kind == "cb":
                    h = item[1]
                    o = open_p(P_AT[item])
                    for i in range(NT):
                        pe.wait_ge(s_lf, NT * h + i + 1)
                        last = pe.matmul(o[:, i * P:S], lfb_view(i), upto[:, 0:S - i * P],
                                         start=(i == 0), stop=(i == NT - 1))
                        if i < NT - 1:
                            last.then_inc(s_lfused, 1)
                    last.then_inc(s_pfull, 1)
                elif kind == "score":
                    n = item[1]
                    m, i, h = units[n]
                    nk = (i + 1) * P
                    if i == 0 and h % 2 == 0:
                        landed(pe, ("proj", m, h // 2))
                        landed(pe, ("proj", m, 2 + h // 2))
                    for s in range(2 if m == B else 1):
                        t = t_of[(n, s)]
                        if t >= 2:
                            pe.wait_ge(s_biased, t - 1)
                        kd = HD // 2 if m == B else HD
                        r0 = (h % 2) * HD + s * kd
                        q = qk[r0:r0 + kd, m % 2, h // 2, i * P:(i + 1) * P]
                        k = qk[r0:r0 + kd, m % 2, 2 + h // 2, 0:nk]
                        last = pe.matmul(sbank[t % 2][:, 0:nk], q, k, start=True, stop=(m != F))
                        if m == F:
                            last = pe.matmul(sbank[t % 2][:, i * P:nk], ident[:], future[:], start=False, stop=True)
                        last.then_inc(s_score, 1)
                elif kind == "turn":
                    n = item[1]
                    m, i, h = units[n]
                    k = T_AT[item]
                    t = t_of[(n, 0)]
                    if m == B:
                        pe.wait_ge(s_mix, n - 16 * B + 1)
                    else:
                        pe.wait_ge(s_exp, t + 1)
                    o = open_t(k)
                    for b in range(i + 1):
                        last = pe.transpose(o[:, b * P:(b + 1) * P], sc[:, t % 4, b * P:(b + 1) * P], ident[:])
                    last.then_inc(s_tfull, 1)
                elif kind == "pv":
                    n = item[1]
                    m, i, h = units[n]
                    turned(pe, ("turn", n))
                    if h == 0:
                        if n // 4 >= 2:
                            pe.wait_ge(s_onorm, n // 4 - 1)
                        landed(pe, ("proj", m, 4 + (i if m == F else i // 2)))
                    o = obank[(n // 4) % 2]
                    for b in range(i + 1):
                        last = pe.matmul(o[:, h * HD:(h + 1) * HD], pt[:, n % 2, b * P:(b + 1) * P],
                                         vv[:, m % 2, b, h * HD:(h + 1) * HD], start=(b == 0), stop=(b == i))
                    last.then_inc(s_pv, 1)
                elif kind == "oT":
                    i = item[1]
                    pe.wait_ge(s_onorm, 4 * F + i + 1)
                    turn8(item, xo[:, i, :])
                elif kind == "out":
                    i, z, c = item[1:]
                    k = P_AT[item[:3]]
                    if z == 0 and c == 0:
                        turned(pe, ("oT", i), 2)
                        if i == 0:
                            for j in range(4):
                                pe.wait_ge(s_wout[j], 16)
                    o = pbank[k % 2] if c else open_p(k)
                    last = pe.matmul(o[:], oT[:, c, :], wout[:, c, z * 512:(z + 1) * 512],
                                     start=(c == 0), stop=(c == KC - 1))
                    if c == KC - 1:
                        last.then_inc(s_pfull, 1)
                elif kind == "h2T":
                    i = item[1]
                    pe.wait_ge(s_h2, i + 1)
                    turn8(item, hrow[:, i % 2, :])
                elif kind == "route":
                    i = item[1]
                    turned(pe, ("h2T", i), 2)
                    o = open_p(P_AT[item])
                    for c in range(KC):
                        last = pe.matmul(o[:, 0:NG + E], hT[:, c, i * P:(i + 1) * P], wr[:, c, :],
                                         start=(c == 0), stop=(c == KC - 1))
                    last.then_inc(s_pfull, 1)
                elif kind in ("rank", "count"):
                    i = item[1] if kind == "rank" else NT
                    o = open_p(P_AT[item])
                    pe.wait_ge(s_pick, min(i, NT - 1) + 1)
                    for z in range(min(i, NT - 1) + 1):
                        own = kind == "rank" and z == i
                        last = pe.matmul(o[:, 0:E], before[:] if own else upto[:, P:2 * P], mem[:, z, :],
                                         start=(z == 0), stop=(z == min(i, NT - 1)))
                    last.then_inc(s_pfull, 1)
                elif kind == "slot":
                    i = item[1]
                    o = open_p(P_AT[item])
                    pe.wait_ge(s_spread, i + 1)
                    for q in range(PAIRS):
                        last = pe.matmul(o[:, 2 * q:2 * q + 2], spread[:, q * P:(q + 1) * P], token[:],
                                         start=True, stop=True)
                    last.then_inc(s_pfull, 1)

            def turn_rows(q, j, first):
                for z in range(2):
                    if not first:
                        pe.wait_ge(s_mx, 2 * q + (z - 1))
                    for c in range(4):
                        last = pe.transpose(tbank[z][:, c * P:(c + 1) * P],
                                            xg[:, j, (4 * z + c) * P:(4 * z + c + 1) * P], ident[:])
                    last.then_inc(s_mt, 1)

            def pair_steps(it, j, first, last_it):
                q = 2 * it + j
                pe.wait_ge(s_mx, 2 * q + 2)
                for z in range(2):
                    e = 4 * it + (2 * j + z)
                    b = (2 * j + z + 2) % 4
                    pe.wait_ge(s_wgu[b], 32 * it + 32)
                    if not (first and j == 0):
                        pe.wait_ge(s_hid, 4 * it + (2 * j + z - 1))
                    for u, w in enumerate(gate_up(b)):
                        for a in range(FT):
                            col = (u * FT + a) * CAP
                            for c in range(KC):
                                last = pe.matmul(sbank[z][:, col:col + CAP], w[:, c, a * P:(a + 1) * P],
                                                 xgT[:, 8 * j + c, z * CAP:(z + 1) * CAP],
                                                 start=(c == 0), stop=(c == KC - 1))
                    last.then_inc(s_gu, 1)
                if not (last_it and j == 1):
                    pe.wait_ge(s_xg[(j + 1) % 2], 16 * (it + j) + 16)
                    turn_rows(q + 1, (j + 1) % 2, False)
                y = (pbank, obank)[j]
                for z in range(2):
                    b = (2 * j + z + 2) % 4
                    pe.wait_ge(s_hid, 4 * it + (2 * j + z + 1))
                    pe.wait_ge(s_wdn[b], 16 * it + 16)
                    if not first and z == 0:
                        pe.wait_ge(s_yd, 2 * it + (j - 1))
                        pe.wait_ge(s_ya, 2 * it + (j - 1))
                    for half in range(2):
                        for a in range(FT):
                            last = pe.matmul(y[half][z * CAP:(z + 1) * CAP, :], hid[:, z, a * CAP:(a + 1) * CAP],
                                             down(b)[:, a, half * 512:(half + 1) * 512],
                                             start=(a == 0), stop=(a == FT - 1))
                    last.then_inc(s_down, 1)

            pe.wait_ge(s_tempty, T_N)
            pe.wait_ge(s_pempty, P_N)
            pe.wait_ge(s_xg[0], 16)
            turn_rows(0, 0, True)
            for j in range(2):
                pair_steps(0, j, True, False)
            with pe.Fori(1, E // 4 - 1, 1) as it:
                for j in range(2):
                    pair_steps(it, j, False, False)
            for j in range(2):
                pair_steps(E // 4 - 1, j, False, True)

            pe.wait_ge(s_crowd, 1)
            with pe.register("pe_crowd") as r:
                pe.reg_load(r, crowd[0:1, 0:1])
                with pe.If(pe.snap(r) > CAP):
                    pe.wait_ge(s_yd, PAIRS)
                    pe.wait_ge(s_ya, PAIRS)
                    with pe.Fori(0, E, 1) as e:
                        pe.wait_ge(s_dw, 48 * e + 48)
                        pe.wait_ge(s_dcur, e + 1)
                        for a in range(FT):
                            if a:
                                pe.wait_ge(s_dhid, FT * e + a)
                            for u, w in enumerate(gate_up(0)):
                                for c in range(KC):
                                    last = pe.matmul(pbank[u][:], w[:, c, a * P:(a + 1) * P], hT[:, c, :],
                                                     start=(c == 0), stop=(c == KC - 1))
                            last.then_inc(s_dgu, 1)
                        pe.wait_ge(s_dhid, FT * e + FT)
                        for i in range(NT):
                            for half in range(2):
                                n = 2 * i + half
                                if n >= 2:
                                    pe.wait_ge(s_dacc, 2 * NT * e + (n - 1))
                                for a in range(FT):
                                    last = pe.matmul(obank[half][:], dense_hid[:, a, i * P:(i + 1) * P],
                                                     down(0)[:, a, half * 512:(half + 1) * 512],
                                                     start=(a == 0), stop=(a == FT - 1))
                                last.then_inc(s_dy, 1)

        @block.vector
        def _(dve):
            steps = [0]

            def link(ins):
                steps[0] += 1
                ins.then_inc(s_dve, 1)
                dve.wait_ge(s_dve, steps[0])

            def permuted(row):
                return row.rearrange("p (c j) -> p j c", c=KC)

            def normalise(dst, src, r):
                return dve.scalar_tensor_tensor(out=permuted(dst), in0=src.rearrange("p (j c) -> p j c", c=KC),
                                                scalar=r, in1=lnb[:].rearrange("p (j c) -> p j c", c=KC),
                                                op0=ALU.mult, op1=ALU.mult)

            def take(k):
                dve.wait_ge(s_pfull, k + 1)
                return pbank[k % 2]

            def first_max(v, n, top, onehot, i):
                link(dve.tensor_reduce(top, v, AX.X, ALU.max))
                link(dve.tensor_scalar(pick[:, 1, 0:n], v, top, None, ALU.is_equal))
                link(dve.scalar_tensor_tensor(out=pick[:, 2, 0:n], in0=pick[:, 1, 0:n], scalar=-1000.0,
                                              in1=iota_e[:, 0:n], op0=ALU.mult, op1=ALU.add))
                link(dve.tensor_reduce(picks[:, i, 0:1], pick[:, 2, 0:n], AX.X, ALU.min))
                link(dve.tensor_scalar(onehot, pick[:, 2, 0:n], picks[:, i, 0:1], None, ALU.is_equal))

            def combine_weights(i):
                w = lambda c: tw[:, i, c:c + 1]
                dve.wait_ge(s_gexp, 2 * i + 2)
                link(dve.reciprocal(w(0), gsc[:, i, 0:1]))
                link(dve.tensor_scalar(w(1), gsc[:, i, 1:2], 1.0, None, ALU.add))
                link(dve.reciprocal(w(2), w(1)))
                link(dve.tensor_tensor(w(3), w(0), w(2), ALU.mult))
                link(dve.tensor_tensor(w(4), w(3), gsc[:, i, 1:2], ALU.mult))
                for k in range(2):
                    link(dve.tensor_tensor_reduce(pick[:, 1, :], oh[:, i, k, :], rank[:, i, :], 1.0, 0.0,
                                                  ALU.mult, ALU.add, w(5 + k)))
                    link(dve.tensor_tensor_reduce(pick[:, 2, :], oh[:, i, k, :], iota_e[:], 1.0, 0.0,
                                                  ALU.mult, ALU.add, w(7 + k)))
                link(dve.tensor_scalar(tw[:, i, 9:11], tw[:, i, 5:7], float(CAP), None, ALU.is_lt))
                link(dve.tensor_tensor(comb[:, i, :], tw[:, i, 3:5], tw[:, i, 9:11], ALU.mult))
                link(dve.tensor_scalar(tw[:, i, 5:7], tw[:, i, 5:7], CAP - 1.0, None, ALU.min))
                link(dve.scalar_tensor_tensor(out=posf[:, i, :], in0=tw[:, i, 7:9], scalar=float(CAP),
                                              in1=tw[:, i, 5:7], op0=ALU.mult, op1=ALU.add))
                link(dve.tensor_scalar(pick[:, 0, :], oh[:, i, 0, :], w(3), None, ALU.mult))
                link(dve.scalar_tensor_tensor(out=pick[:, 1, :], in0=oh[:, i, 1, :], scalar=w(4),
                                              in1=pick[:, 0, :], op0=ALU.mult, op1=ALU.add))
                link(dve.scalar_tensor_tensor(out=late[:, i, :], in0=rank[:, i, :], scalar=float(CAP),
                                              in1=pick[:, 1, :], op0=ALU.is_ge, op1=ALU.mult))
                if i == NT - 1:
                    dve.tensor_copy(pos[:], posf[:].rearrange("p i k -> p (i k)")).then_inc(s_pos, 1)

            for item in plan:
                kind = item[0]
                if kind == "table":
                    for z, (a, b) in enumerate(((0, 512), (512, SPAN))):
                        o = take(P_AT[item] + z)
                        dve.tensor_copy(table_rows[:, a:b], o[0:12, 0:b - a]).then_inc(s_pempty, 1)
                elif kind == "ln1":
                    i = item[1]
                    if i == 0:
                        dve.wait_ge(s_ln1b, 16)
                    if i >= 2:
                        dve.wait_ge(s_tfull, T_AT[("hT", i - 2)] + 2)
                    dve.wait_ge(s_rs1, i + 1)
                    dve.wait_ge(s_xin[i], 16)
                    normalise(hrow[:, i % 2, :], xo[:, i, :], rs[:, 0, i:i + 1]).then_inc(s_hrow, 1)
                elif kind == "proj" and item[3] == KC - 1:
                    m, g = item[1:3]
                    o = take(P_AT[item[:3]])
                    if g < 2:
                        scale = (HD // 2 if m == B else HD) ** -0.5
                        dve.tensor_scalar(falling(qk[:, m % 2, g, :].rearrange("p (i t) -> p i t", i=NT)),
                                          o[:].rearrange("p (i t) -> p i t", i=NT), scale, None,
                                          ALU.mult).then_inc(s_pempty, 1)
                    elif g < 4:
                        dve.tensor_copy(qk[:, m % 2, g, :], o[:]).then_inc(s_pempty, 1)
                    elif m == F:
                        dve.tensor_copy(vv[:, 1, g - 4, :], o[:, 0:GW]).then_inc(s_zraw, 1)
                        dve.tensor_copy(zraw[:, g - 4, :], o[:, GW:GW + H]).then_inc(s_pempty, 1)
                    else:
                        dve.tensor_copy(vv[:, m % 2, 2 * (g - 4):2 * (g - 4) + 2, :],
                                        o[:].rearrange("p (i n) -> p i n", i=2)).then_inc(s_pempty, 1)
                elif kind == "z":
                    landed(dve, ("proj", F, 7))
                    dve.tensor_tensor(zt[:, 0, :].rearrange("p (i h) -> p i h", h=H), zraw[:],
                                      bf[:].unsqueeze(1).to_broadcast([P, NT, H]), ALU.add).then_inc(s_zin, 1)
                    dve.wait_ge(s_zin, 1)
                    dve.wait_ge(s_zabs, 1)
                    link(dve.tensor_scalar(zt[:, 0, :], zt[:, 0, :], 0.0, None, ALU.min))
                elif kind == "cb":
                    h = item[1]
                    if h == 0:
                        dve.wait_ge(s_zln, 1)
                        link(dve.tensor_tensor(zt[:, 0, :], zt[:, 0, :], zt[:, 3, :], ALU.subtract))
                    for i in range(NT):
                        n = NT * h + i
                        if i == 1 and h:
                            dve.wait_ge(s_pfull, P_AT[("cb", h - 1)] + 1)
                        elif i >= 2 or h:
                            dve.wait_ge(s_lfused, (NT - 1) * h + max(i - 1, 0))
                        dve.tensor_copy(lfb_view(i), zt[:, 0, i * H + h:i * H + h + 1].to_broadcast([P, P])).then_inc(s_lf, 1)
                    if h == 0:
                        dve.wait_ge(s_biased, t_of[(16 * C - 1, 1)] + 1)
                    dve.tensor_scalar(gb[:, 1, h, :], take(P_AT[item])[:], -1.0, None, ALU.mult).then_inc(s_pempty, 1)
                elif kind == "score":
                    n = item[1]
                    m, i, h = units[n]
                    nk = (i + 1) * P
                    if n == 16 * A:
                        dve.wait_ge(s_small, 16 * N_SMALL)
                        for z in range(2):
                            dve.tensor_tensor_reduce(lamv[:, 2 * z, :], lamv[:, 2 * z, :], lamv[:, 2 * z + 1, :], 1.0, 0.0,
                                                     ALU.mult, ALU.add, lams[:, z:z + 1]).then_inc(s_lam, 1)
                    if n == 16 * A + 1:
                        dve.wait_ge(s_lamexp, 1)
                        link(dve.tensor_tensor(lams[:, 4:5], lams[:, 2:3], lams[:, 3:4], ALU.subtract))
                        link(dve.tensor_scalar(lams[:, 5:6], lams[:, 4:5], LAMBDA_INIT, -1.0, ALU.add, ALU.mult))
                        link(dve.tensor_scalar(subg[:], subg[:], 1.0 - LAMBDA_INIT, None, ALU.mult))
                    if n % 16 == 0 and m != F:
                        dve.wait_ge(s_strip[m], 16)
                    if i == 0 and m == F:
                        landed(dve, ("cb", h))
                    for s in range(2 if m == B else 1):
                        t = t_of[(n, s)]
                        bias = gb[:, m % 2, h, (0 if m == F else S - nk):(nk if m == F else S)]
                        if t >= 4:
                            dve.wait_ge(s_tfull, T_AT[("turn", parts[t - 4][0])] + 1)
                        dve.wait_ge(s_score, t + 1)
                        dve.tensor_tensor_reduce(sc[:, t % 4, 0:nk], sbank[t % 2][:, 0:nk], bias, -1.0, 3e38,
                                                 ALU.add, ALU.min, negmax[:, t:t + 1]).then_inc(s_biased, 1)
                elif kind == "mix":
                    n = item[1]
                    m, i, h = units[n]
                    nk = (i + 1) * P
                    t = t_of[(n, 0)]
                    dve.wait_ge(s_exp, t + 2)
                    link(dve.reciprocal(linv[:, t:t + 2], lsum[:, t:t + 2]))
                    c = mixc[:, n % 16:n % 16 + 1]
                    link(dve.scalar_tensor_tensor(out=c, in0=lsum[:, t:t + 1], scalar=lams[:, 5:6],
                                                  in1=linv[:, t + 1:t + 2], op0=ALU.mult, op1=ALU.mult))
                    dve.scalar_tensor_tensor(out=sc[:, t % 4, 0:nk], in0=sc[:, (t + 1) % 4, 0:nk], scalar=c,
                                             in1=sc[:, t % 4, 0:nk], op0=ALU.mult, op1=ALU.add).then_inc(s_mix, 1)
                elif kind == "onorm":
                    g4 = item[1]
                    m, i, _ = units[4 * g4]
                    dve.wait_ge(s_pv, 4 * g4 + 4)
                    t = t_of[(4 * g4, 0)]
                    o = obank[g4 % 2][:, 0:GW].rearrange("p (h n) -> p h n", h=H)
                    dst = xo[:, i, m * GW:(m + 1) * GW].rearrange("p (h n) -> p h n", h=H)
                    wide = lambda v: v.unsqueeze(2).to_broadcast([P, H, HD])
                    if m != B:
                        link(dve.reciprocal(linv[:, t:t + H], lsum[:, t:t + H]))
                        dve.tensor_tensor(dst, o, wide(linv[:, t:t + H]), ALU.mult).then_inc(s_onorm, 1)
                    else:
                        l1 = linv[:, t:t + 2 * H].rearrange("p (h s) -> p h s", s=2)[:, :, 0]
                        dve.tensor_tensor(dst, o, wide(l1), ALU.mult).then_inc(s_onorm, 1)
                        dve.wait_ge(s_onorm, g4 + 1)
                        sq = sqh[:]
                        link(dve.tensor_tensor(sq.rearrange("p (h n) -> p h n", h=H), dst, dst, ALU.mult))
                        dve.tensor_reduce(onrm[:, 0, :], sq.rearrange("p (h n) -> p h n", h=H), AX.X,
                                          ALU.add).then_inc(s_osq, 1)
                        dve.wait_ge(s_ors, g4 - 4 * B + 1)
                        link(dve.tensor_tensor(dst, dst, wide(onrm[:, 1, :]), ALU.mult))
                        link(dve.tensor_tensor(dst, dst, subg[:].unsqueeze(1).to_broadcast([P, H, HD]), ALU.mult))
                elif kind == "out" and item[3] == KC - 1:
                    i, z = item[1:3]
                    dve.wait_ge(s_xres[i % 2], 16 * (i // 2 + 1))
                    o = take(P_AT[item[:3]])
                    dve.tensor_tensor(xo[:, i, z * 512:(z + 1) * 512], o[:], xres[:, i % 2, z * 512:(z + 1) * 512],
                                      ALU.add).then_inc(s_pempty, 1)
                elif kind == "ln2":
                    i = item[1]
                    if i == 0:
                        dve.wait_ge(s_ln2b, 16)
                    if i >= 2:
                        dve.wait_ge(s_tfull, T_AT[("h2T", i - 2)] + 2)
                        dve.wait_ge(s_h2out[i - 2], 16)
                    dve.wait_ge(s_rs2, i + 1)
                    normalise(hrow[:, i % 2, :], xo[:, i, :], rs[:, 1, i:i + 1]).then_inc(s_h2, 1)
                elif kind == "route":
                    i = item[1]
                    o = take(P_AT[item])
                    dve.tensor_tensor(logit[:, i, :], o[:, 0:NG + E], rb[:], ALU.add).then_inc(s_pempty, 1)
                    landed(dve, item)
                elif kind == "pick":
                    i = item[1]
                    g, e = logit[:, i, 0:NG], logit[:, i, NG:]
                    top, v1, v2 = pick[:, 3, 8:9], picks[:, i, 1:2], picks[:, i, 2:3]
                    first_max(g, NG, top, pick[:, 3, 0:NG], i)
                    link(dve.tensor_scalar(picks[:, i, 3:4], top, -1.0, None, ALU.mult))
                    link(dve.tensor_scalar(pick[:, 3, 0:NG], pick[:, 3, 0:NG], -NEG, NEG, ALU.mult, ALU.add))
                    link(dve.tensor_tensor(pick[:, 0, :].rearrange("p (g e) -> p g e", g=NG),
                                           e.rearrange("p (g e) -> p g e", g=NG),
                                           pick[:, 3, 0:NG].unsqueeze(2).to_broadcast([P, NG, EPG]), ALU.add))
                    first_max(pick[:, 0, :], E, v1, oh[:, i, 0, :], i)
                    link(dve.scalar_tensor_tensor(out=pick[:, 0, :], in0=oh[:, i, 0, :], scalar=2 * NEG,
                                                  in1=pick[:, 0, :], op0=ALU.mult, op1=ALU.add))
                    first_max(pick[:, 0, :], E, v2, oh[:, i, 1, :], i)
                    dve.tensor_tensor(mem[:, i, :], oh[:, i, 0, :], oh[:, i, 1, :], ALU.add).then_inc(s_pick, 1)
                elif kind == "rank":
                    i = item[1]
                    o = take(P_AT[item])
                    dve.tensor_copy(rank[:, i, :], o[:, 0:E]).then_inc(s_pempty, 1)
                    dve.wait_ge(s_pempty, P_AT[item] + 1)
                    link(dve.scalar_tensor_tensor(out=rankm[:], in0=rank[:, i, :], scalar=1.0, in1=mem[:, i, :],
                                                  op0=ALU.add, op1=ALU.mult))
                    if i:
                        dve.wait_ge(s_pfull, P_AT[("slot", i - 1)] + 1)
                    dve.tensor_tensor(spread.rearrange("p (e s) -> p e s", e=E),
                                      rankm[:].unsqueeze(2).to_broadcast([P, E, CAP]),
                                      iota_s[:].unsqueeze(1).to_broadcast([P, E, CAP]), ALU.is_equal).then_inc(s_spread, 1)
                elif kind == "slot":
                    i = item[1]
                    o = take(P_AT[item])
                    dve.tensor_copy(slotf[:, i, :], o[:, 0:2 * PAIRS]).then_inc(s_pempty, 1)
                    if i:
                        landed(dve, item)
                        v = slotf[:, i, :].rearrange("p (q z) -> p q z", z=2)
                        link(dve.scalar_tensor_tensor(out=v[:, :, 0], in0=v[:, :, 1], scalar=float(i * P), in1=v[:, :, 0],
                                                      op0=ALU.mult, op1=ALU.add))
                elif kind == "slots":
                    dve.wait_ge(s_pempty, P_AT[("slot", NT - 1)] + 1)
                    link(dve.tensor_reduce(slott[:], slotf[:].rearrange("p i (q z) -> p q z i", z=2)[:, :, 0, :], AX.X, ALU.add))
                    dve.tensor_copy(idx[:], slott[:]).then_inc(s_idx, 1)
                elif kind == "count":
                    o = take(P_AT[item])
                    dve.tensor_reduce(busiest[:], o[:, 0:E], AX.X, ALU.max).then_inc(s_pempty, 1)
                    landed(dve, item)
                    dve.tensor_copy(crowd[:], busiest[:]).then_inc(s_crowd, 1)
                elif kind == "weights" and item[1] < NT - 1:
                    combine_weights(item[1])

            def pair_steps(it, j, first):
                q = 2 * it + j
                for z in range(2):
                    e = 4 * it + (2 * j + z)
                    dve.wait_ge(s_silu, e + 1)
                    if not (first and j == 0):
                        dve.wait_ge(s_down, 4 * it + (2 * j + z - 1))
                    dve.tensor_tensor(hid[:, z, :], gate_act[:, z, :], sbank[z][:, FT * CAP:2 * FT * CAP],
                                      ALU.mult).then_inc(s_hid, 1)
                dve.wait_ge(s_down, 2 * q + 2)
                if first and j == 0:
                    for i in range(NT):
                        dve.wait_ge(s_h2out[i], 16)
                if not first:
                    dve.wait_ge(s_yst[j], 16 * it)
                dve.tensor_copy(yrow[:, j, 0:512], (pbank, obank)[j][0][:]).then_inc(s_yd, 1)

            for j in range(2):
                pair_steps(0, j, True)
            combine_weights(NT - 1)
            with dve.Fori(1, E // 4, 1) as it:
                for j in range(2):
                    pair_steps(it, j, False)

            dve.wait_ge(s_crowd, 1)
            with dve.register("dve_crowd") as r:
                dve.reg_load(r, crowd[0:1, 0:1])
                with dve.If(dve.snap(r) > CAP):
                    with dve.Fori(0, E, 1) as e:
                        dve.tensor_copy(lcur[:], late[:, :, bass.ds(e, 1)].rearrange("p i e -> p (i e)")).then_inc(s_dcur, 1)
                        dve.wait_ge(s_dcur, e + 1)
                        for a in range(FT):
                            dve.wait_ge(s_dsilu, FT * e + (a + 1))
                            dve.tensor_tensor(dense_hid[:, a, :], dense_act[:, a, :], pbank[1][:], ALU.mult).then_inc(s_dhid, 1)
                        for i in range(NT):
                            for half in range(2):
                                dve.wait_ge(s_dy, 2 * NT * e + (2 * i + half + 1))
                                x2 = xo[:, i, half * 512:(half + 1) * 512]
                                dve.scalar_tensor_tensor(out=x2, in0=obank[half][:], scalar=lcur[:, i:i + 1], in1=x2,
                                                         op0=ALU.mult, op1=ALU.add).then_inc(s_dacc, 1)
                        dve.wait_ge(s_dacc, 2 * NT * e + 2 * NT)

            dve.wait_ge(s_lnfb, 16)
            for i in range(NT + 1):
                if i < NT:
                    dve.wait_ge(s_yg[i], 32)
                    for k in range(2):
                        dve.scalar_tensor_tensor(out=xo[:, i, :], in0=ybuf[:, i, k, :], scalar=comb[:, i, k:k + 1],
                                                 in1=xo[:, i, :], op0=ALU.mult, op1=ALU.add).then_inc(s_sum, 1)
                        dve.wait_ge(s_sum, 2 * i + k + 1)
                if i:
                    dve.wait_ge(s_rs3, i)
                    dve.scalar_tensor_tensor(out=orow[:, i - 1, :], in0=xo[:, i - 1, :], scalar=rs[:, 2, i - 1:i],
                                             in1=lnfb, op0=ALU.mult, op1=ALU.mult).then_inc(s_orow, 1)


def bucket_tables():
    import numpy as np
    dist = S - 1 - np.arange(SPAN)
    d = np.maximum(dist, 0)
    exact = BUCKETS // 2
    large = exact + (np.log(np.maximum(d, 1) / exact) / math.log(2048 / exact) * (BUCKETS - exact)).astype(np.int32)
    bucket = np.where(d < exact, d, np.minimum(large, BUCKETS - 1))
    rows = np.zeros((BUCKETS + 2, SPAN), np.float32)
    past = dist >= 0
    rows[bucket[past], np.nonzero(past)[0]] = 1.0
    held = sum(((d % dil == 0) & (d <= window)).astype(int) for window, dil in ((128, 1), (512, 4), (2048, 16)))
    rows[BUCKETS, past] = np.where(held > 0, np.log(np.maximum(held, 1)), NEG)[past]
    rows[BUCKETS + 1, ~past] = NEG
    cols = np.zeros((2, 12), np.float32)
    cols[0, 0:H] = 1.0
    cols[1, :] = 1.0
    return rows, cols


_INS = ["x", "rel_bias", "ln1", "w_in", "w_out", "lam_q1", "lam_k1", "lam_q2", "lam_k2", "subln_g", "b_forget",
        "ln2", "w_group", "b_group", "w_expert", "b_expert", "w_gate", "w_up", "w_down", "ln_f"]


def kernel(**inputs):
    import numpy as _np
    import concourse.bacc as _bacc
    from concourse import mybir as _mybir
    from concourse.bass_utils import run_bass_kernel_spmd as _run

    nc = _bacc.Bacc("TRN2", target_bir_lowering=False, num_devices=1)
    arrays, args = {}, []
    host = {name: _np.ascontiguousarray(inputs[name]) for name in _INS}
    host["bucket_rows"], host["bias_cols"] = bucket_tables()
    for name, a in host.items():
        arrays[f"in_{name}_dram"] = a
        args.append(nc.dram_tensor(f"in_{name}_dram", a.shape, _mybir.dt.from_np(a.dtype), kind="ExternalInput").ap())
    args.append(nc.dram_tensor("out_0_dram", (1, S, D), F32, kind="ExternalOutput").ap())
    hybrid_layer(nc, *args)
    r = _run(nc, [arrays], core_ids=[0])
    return r.results[0]["out_0_dram"]
```

```python
import math
from contextlib import ExitStack

import concourse.bass as bass
from concourse import mybir

ALU = mybir.AluOpType
ACT = mybir.ActivationFunctionType
AX = mybir.AxisListType
F32 = mybir.dt.float32
BF16 = mybir.dt.bfloat16
U32 = mybir.dt.uint32
I32 = mybir.dt.int32

P = 128
S = 512
D = 1024
NT = S // P
KC = D // P
HD = 64
H = 4
GW = H * HD
A, B, C, F = range(4)
BUCKETS = 32
SPAN = S + P - 1
NEG = -1e30
EPS = 1e-6
LAMBDA_INIT = 0.8 - 0.6 * math.exp(-0.3 * 0)

NG, EPG = 4, 8
E = NG * EPG
FE = D // 4
FT = FE // P
PLACE = 64.0
EMPTY = 4096.0
CAP = 64
PAIRS = E // 2
SLOT = KC * GW
NSLOT = 12
EARLY = (4, 5)


def plan_front():
    def project(m, groups):
        return [("proj", m, g, s) for g in groups for s in range(KC)]

    plan = []
    for i in range(NT + 1):
        plan += [("ln1", i)] if i < NT else []
        plan += [("hT", i - 1)] if i else []
        plan += [("table",)] if i == 1 else []
    plan += project(A, range(6))
    fill = {A: project(B, range(6)), B: project(C, range(6)),
            C: project(F, (0, 4, 5, 6, 7)) + [("z",)] + project(F, (2,))[0:4] + [("gates",)] + project(F, (2,))[4:]
               + [("cb", 0), ("cb", 1)]}
    per_mixer = H * NT
    n_units = 4 * per_mixer
    for n in range(n_units + 8):
        m, at = divmod(n, per_mixer)
        between = []
        if m < F:
            count = len(fill[m])
            between = fill[m][at * count // per_mixer:(at + 1) * count // per_mixer]
        if n - per_mixer * F in (0, 1):
            z = n - per_mixer * F
            between = project(F, (1 + 2 * z,)) + [("cb", 2 + z)]
        i, r = divmod(n - per_mixer * F - 8, 4)
        if 0 <= i < NT and r == 0:
            plan.append(("oT", i))
        if n < n_units and m == B:
            plan.append(("score", n))
        elif n < n_units and n % 2 == 0:
            plan += [("score", n), ("score", n + 1)]
        if 0 <= n - 4 < n_units and n % 4 == 3:
            plan.append(("onorm", n // 4 - 1))
        if 0 <= i < NT:
            half = lambda z: [("out", i, z, s) for s in range(KC)]
            if r == 0:
                if i >= 1:
                    plan.append(("norm2", i - 1))
                if i >= 2:
                    plan.append(("rank", i - 2))
                between = half(0)[0:2]
            elif r == 1:
                if i:
                    plan.append(("h2T", i - 1))
                between = half(0)[2:]
            elif r == 2:
                if i >= 2:
                    plan += [("slot", i - 2), ("weights", i - 2)]
                if i:
                    plan += [("route", i - 1), ("pick", i - 1)]
                between = half(1)[0:5]
            else:
                between = half(1)[5:]
        cut = -(-len(between) // 2)
        plan += between[0:cut]
        if 0 <= n - 1 < n_units and (n - 1) // per_mixer == B:
            plan.append(("mix", n - 1))
        if 0 <= n - 2 < n_units:
            plan.append(("turn", n - 2))
        plan += between[cut:]
        if 0 <= n - 3 < n_units:
            plan.append(("pv", n - 3))
        if 0 <= i < NT and r == 3:
            if i == NT - 1:
                plan.append(("rank", i - 1))
            plan.append(("ln2", i))
    last = NT - 1
    plan += [("h2T", last), ("slot", last - 1), ("norm2", last), ("route", last), ("pick", last), ("rank", last),
             ("slot", last), ("slots",), ("count",), ("weights", last - 1), ("weights", last)]
    return plan


def uses(plan, kinds):
    at, first = 0, {}
    for item in plan:
        if item[0] in kinds:
            key = item[:3] if item[0] in ("proj", "out") else item
            if key not in first:
                first[key] = at
                at += kinds[item[0]]
    return first, at


def hybrid_layer(nc, x, rel_bias, ln1, w_in, w_out, lam_q1, lam_k1, lam_q2, lam_k2, subln_g, b_forget,
                 ln2, w_group, b_group, w_expert, b_expert, w_gate, w_up, w_down, ln_f,
                 bucket_rows, bias_cols, out):
    plan = plan_front()
    P_AT, P_N = uses(plan, {"table": 2, "proj": 1, "cb": 1, "out": 1, "route": 1,
                            "rank": 1, "slot": 1, "count": 1})
    T_AT, T_N = uses(plan, {"hT": 2, "turn": 1, "oT": 2, "h2T": 2})
    units = [(n // 16, (n // 4) % 4, n % 4) for n in range(16 * 4)]
    t_of, parts = {}, []
    for n, (m, i, h) in enumerate(units):
        for s in range(2 if m == B else 1):
            t_of[(n, s)] = len(parts)
            parts.append((n, s))

    with ExitStack() as ctx:
        def sb(name, shape, dt=F32):
            return ctx.enter_context(nc.sbuf_tensor(name, shape, dt))

        def sem(name):
            return ctx.enter_context(nc.semaphore(name))

        bank = {b: ctx.enter_context(nc.psum_tensor(f"bank_{b}", [P, 512], F32))
                for b in ("P0", "P1", "S0", "S1", "T0", "T1", "O0", "O1")}
        pbank = [bank["P0"], bank["P1"]]
        sbank = [bank["S0"], bank["S1"]]
        tbank = [bank["T0"], bank["T1"]]
        obank = [bank["O0"], bank["O1"]]

        zcols = H * KC
        ring_flat = sb("ring", [P, NSLOT * SLOT + zcols])
        ring = ring_flat[:, 0:NSLOT * SLOT].rearrange("p (a b) -> p a b", a=NSLOT)
        fv = ring_flat[:, (NSLOT - 1) * SLOT:].rearrange("p (c n) -> p c n", c=KC)
        hT = sb("hT", [P, KC, S])
        xo = sb("xo", [P, NT, D])
        qk = sb("qk", [P, 2, 4, S])
        vv = sb("vv", [P, 2, NT, GW])
        gb = sb("gb", [P, 2, H, S])
        sc = sb("sc", [P, 4, S])
        pt = sb("pt", [P, 2, S])
        hrow = sb("hrow", [P, 2, D])
        junk = sb("junk", [P, D], BF16)
        sqh = sb("sqh", [P, GW])
        lnb = sb("lnb", [P, D])
        ident = sb("ident", [P, P])
        upto = sb("upto", [P, S])
        before = sb("before", [P, P])
        future = sb("future", [P, P])
        iota_e = sb("iota_e", [P, E])
        iota_p = sb("iota_p", [P, E], BF16)
        iota_s = sb("iota_s", [P, CAP], BF16)
        token = sb("token", [P, NT, 3], BF16)
        relb = sb("relb", [BUCKETS + 2, 12])
        lamv = sb("lamv", [P, 4, HD // 2])
        lams = sb("lams", [P, 8])
        subg = sb("subg", [P, HD])
        bf = sb("bf", [P, H])
        wr = sb("wr", [P, KC, NG + E])
        rb = sb("rb", [P, NG + E])
        ms = sb("ms", [P, 4, NT])
        rs = sb("rs", [P, 3, NT])
        negmax = sb("negmax", [P, len(parts)])
        lsum = sb("lsum", [P, len(parts)])
        linv = sb("linv", [P, len(parts)])
        mixc = sb("mixc", [P, 16])
        power = sb("power", [P, H])
        rtmp = sb("rtmp", [P, 4 * NT, H])
        onrm = sb("onrm", [P, 2, H])
        zraw = sb("zraw", [P, NT, H])
        zt = sb("zt", [P, 4, NT * H])
        logit = sb("logit", [P, NT, NG + E])
        pick = sb("pick", [P, 4, E])
        picks = sb("picks", [P, NT, 4])
        oh = sb("oh", [P, NT, 2, E])
        mem = sb("mem", [P, NT, E])
        rank = sb("rank", [P, NT, E])
        rankm = sb("rankm", [P, E], BF16)
        slotf = sb("slotf", [P, NT, 3 * PAIRS])
        slotn = sb("slotn", [P, 3, PAIRS])
        idx = sb("idx", [P, PAIRS], U32)
        dest = sb("dest", [P, PAIRS], U32)
        gexp = sb("gexp", [P, NT, NG])
        gsc = sb("gsc", [P, NT, 4])
        tw = sb("tw", [P, NT, 12])
        comb = sb("comb", [P, NT, 2])
        lcur = sb("lcur", [P, NT])
        busiest = sb("busiest", [P, 1])
        crowd = sb("crowd", [P, 1], I32)

        onehot_rows = sc[0:BUCKETS + 2, 0:2, :].rearrange("p a b -> p (a b)")[:, 0:SPAN]
        table_rows = sc[0:12, 2:4, :].rearrange("p a b -> p (a b)")[:, 0:SPAN]
        oT = vv[:, 0, :, :].rearrange("p i n -> p (i n)").rearrange("p (c t) -> p c t", c=KC)
        xres = qk[:, 0, :, :].rearrange("p (a b) s -> p a (b s)", a=2)
        spread = gb[:, 0, 0:2, :].rearrange("p a b -> p (a b)").bitcast(BF16)
        wout = ring[:, 0:4, :].rearrange("p a b -> p (a b)").rearrange("p (c n) -> p c n", c=KC)
        xg = qk[:, 1, :, :].rearrange("p (a b) s -> p a (b s)", a=2)
        xgT = gb[:, 1, :, :].rearrange("p a b -> p (a b)").rearrange("p (c s) -> p c s", c=2 * KC)
        spare = [[v.rearrange("p (c f) -> p c f", c=KC) for v in pair] for pair in (
            (vv[:].rearrange("p a i n -> p (a i n)"), qk[:, 0, :, :].rearrange("p a s -> p (a s)")),
            [hT[:, 4 * z:4 * z + 4, :].rearrange("p c s -> p (c s)") for z in range(2)])]
        x2T = hT[:, 0:4, :].rearrange("p c s -> p (c s)").rearrange("p (i c t) -> p i c t", i=2, c=KC)
        h2rows = ring[:, 3:5, :].rearrange("p a b -> p (a b)").rearrange("p (i n) -> p i n", i=NT)
        gain2 = sqh[:, 0:KC]
        lnfb = gb[:, 0, 2:4, :].rearrange("p a b -> p (a b)")
        yrow = hrow
        gate_act, hid, hidT = (sc[:, z, :].rearrange("p (j f) -> p j f", j=2) for z in range(3))
        zeros = junk[:].bitcast(F32)
        slott = zt[:].rearrange("p a b -> p (a b)")[:, 0:3 * PAIRS].rearrange("p (q z) -> p q z", z=3)
        late = lamv
        ybuf = ring[:, 0:4, :].rearrange("p a b -> p (a b)").rearrange("p (i k n) -> p i k n", i=NT, k=2)
        orow = ring[:, 4:6, :].rearrange("p a b -> p (a b)").rearrange("p (i n) -> p i n", i=NT)
        dense_act = qk[:, 0, 0:2, :]
        dense_hid = qk[:, 0, 2:4, :]

        table_d = nc.dram_tensor("table_scratch", (12, SPAN), F32, kind="Internal").ap()
        h2_d = nc.dram_tensor("h2_scratch", (S, D), F32, kind="Internal").ap()
        y_d = nc.dram_tensor("y_scratch", (2 * S, D), F32, kind="Internal").ap()

        s_xin = [sem(f"s_xin{i}") for i in range(NT)]
        s_tabin, s_ln1b, s_small, s_ln2b, s_lnfb = map(sem, ("s_tabin", "s_ln1b", "s_small", "s_ln2b", "s_lnfb"))
        s_win = [sem(f"s_win{i}") for i in range(12)]
        s_wout = [sem(f"s_wout{i}") for i in range(4)]
        s_strip = [sem(f"s_strip{m}") for m in range(3)]
        s_xres = [sem(f"s_xres{i}") for i in range(2)]
        s_tabout = sem("s_tabout")
        s_h2out = [sem(f"s_h2out{i}") for i in range(NT)]
        s_const, s_pool = sem("s_const"), sem("s_pool")
        s_zraw = sem("s_zraw")
        N_SMALL = 11
        s_sq, s_hrow = sem("s_sq"), sem("s_hrow")
        s_pfull, s_pempty = sem("s_pfull"), sem("s_pempty")
        s_tfull, s_tempty = sem("s_tfull"), sem("s_tempty")
        s_score, s_biased, s_exp, s_mix = map(sem, ("s_score", "s_biased", "s_exp", "s_mix"))
        s_pv, s_onorm = sem("s_pv"), sem("s_onorm")
        s_lam, s_lamexp = sem("s_lam"), sem("s_lamexp")
        s_zin, s_zabs, s_zexp, s_zln, s_lf = map(sem, ("s_zin", "s_zabs", "s_zexp", "s_zln", "s_lf"))
        s_sq2, s_h2 = map(sem, ("s_sq2", "s_h2"))
        s_pick, s_gexp, s_spread, s_idx, s_dest, s_crowd = map(
            sem, ("s_pick", "s_gexp", "s_spread", "s_idx", "s_dest", "s_crowd"))
        s_top = sem("s_top")
        s_zeros, s_yzero, s_xzero = map(sem, ("s_zeros", "s_yzero", "s_xzero"))
        s_dve = sem("s_dve")
        s_rs1, s_rs2, s_rs3, s_osq, s_ors, s_root = map(sem, ("s_rs1", "s_rs2", "s_rs3", "s_osq", "s_ors", "s_root"))
        s_scaled, s_orow_last = sem("s_scaled"), sem("s_orow_last")
        s_spare = [sem(f"s_spare{z}") for z in range(2)]
        s_dh2, s_dturn, s_dhT = map(sem, ("s_dh2", "s_dturn", "s_dhT"))
        s_wgu = [sem(f"s_wgu{b}") for b in range(4)]
        s_wdn = [sem(f"s_wdn{b}") for b in range(4)]
        s_xg = [sem(f"s_xg{b}") for b in range(2)]
        s_yst = [sem(f"s_yst{b}") for b in range(2)]
        s_mt, s_mx, s_gu, s_silu, s_hid, s_turned, s_hidT, s_down, s_yd, s_ya = map(
            sem, ("s_mt", "s_mx", "s_gu", "s_silu", "s_hid", "s_turned", "s_hidT", "s_down", "s_yd", "s_ya"))
        s_dw, s_dgu, s_dsilu, s_dhid, s_dy, s_dacc, s_dcur = map(
            sem, ("s_dw", "s_dgu", "s_dsilu", "s_dhid", "s_dy", "s_dacc", "s_dcur"))
        s_yg = [sem(f"s_yg{n}") for n in range(2 * NT)]
        s_sum, s_sq3, s_orow, s_out = map(sem, ("s_sum", "s_sq3", "s_orow", "s_out"))

        def landed(eng, item, n=1):
            eng.wait_ge(s_pempty, P_AT[item] + n)

        def turned(eng, item, n=1):
            eng.wait_ge(s_tempty, T_AT[item] + n)

        win_d = w_in[0].rearrange("(p c) n -> p c n", c=KC)
        wout_d = w_out[0].rearrange("(c p) n -> p c n", p=P)

        def expert_chunks(e, b):
            s = 3 * b
            wide = lambda t: ring[:, t, :].rearrange("p (c f) -> p c f", c=KC)
            return ((wide(s), w_gate[0, bass.ds(e, 1)].rearrange("e (p c) f -> p (e c) f", c=KC)),
                    (wide(s + 1), w_up[0, bass.ds(e, 1)].rearrange("e (p c) f -> p (e c) f", c=KC)),
                    (ring[:, s + 2, :].rearrange("p (a n) -> p a n", a=FT),
                     w_down[0, bass.ds(e, 1)].rearrange("e (a p) n -> p (e a) n", p=P)))

        def load_gate_up(eng, e, b, which=(0, 1)):
            for z in which:
                dst, src = expert_chunks(e, b)[z]
                eng.dma_start(dst, src).then_inc(s_wgu[b], 16)

        def load_spare(eng, z, which):
            src = expert_chunks(EARLY[z], 0)[which][1]
            eng.dma_start(spare[z][which], src).then_inc(s_spare[z], 16)

        def load_down(eng, e, b):
            dst, src = expert_chunks(e, b)[2]
            eng.dma_start(dst, src).then_inc(s_wdn[b], 16)

        def gate_up(b):
            return ring[:, 3 * b:3 * b + 2, :].rearrange("p u (c f) -> p c u f", c=KC)

        def down(b):
            return ring[:, 3 * b + 2, :].rearrange("p (a n) -> p a n", a=FT)

        def pair_before(it, j):
            return (it, 0) if j else (it - 1, 1)

        def strip(m):
            return bass.AP(table_d.tensor, m * H * SPAN, [[1, P], [SPAN, H], [1, S]])

        def falling(v):
            return v[:, :, ::-1]

        def lfb_view(h, i):
            n = NT * h + i
            return hrow[:, n // KC, (n % KC) * P:(n % KC + 1) * P]

        blank = ((ident, 0.0), (upto, 1.0), (before, 1.0), (future, 0.0), (power, -0.5))
        block = ctx.enter_context(nc.Block())

        @block.sync
        def _(sp):
            for i in range(NT):
                sp.dma_start(xo[:, i, :], x[0, i * P:(i + 1) * P, :]).then_inc(s_xin[i], 16)
                if i == 0:
                    sp.dma_start(lnb[:], ln1.to_broadcast([P, D])).then_inc(s_ln1b, 16)
            for g in range(12):
                wide = g == 11
                sp.dma_start(fv if wide else ring[:, g, :].rearrange("p (c n) -> p c n", c=KC),
                             win_d[:, :, g * GW:(g + 1) * GW + H * wide]).then_inc(s_win[g], 16)
                if g == 2:
                    landed(sp, ("table",), 2)
                    sp.dma_start(table_d, table_rows).then_inc(s_tabout, 16)
                if g == 3:
                    sp.wait_ge(s_tabout, 16)
                    for m in (A, B):
                        sp.dma_start(gb[:, m % 2], strip(m)).then_inc(s_strip[m], 16)
            sp.wait_ge(s_hrow, NT)
            sp.dma_start(lnb[:], ln2.to_broadcast([P, D])).then_inc(s_ln2b, 16)
            for j in range(4):
                sp.wait_ge(s_pfull, P_AT[("proj", j // 3, 2 * (j % 3) + 1)] + 1)
                sp.dma_start(ring[:, j, :].rearrange("p (c n) -> p c n", c=2),
                             wout_d[:, 2 * j:2 * j + 2, :]).then_inc(s_wout[j], 16)
            sp.wait_ge(s_zeros, 1)
            sp.dma_start(y_d.rearrange("(p a) (h n) -> p (a h) n", p=P, h=2),
                         zeros.unsqueeze(1).to_broadcast([P, 2 * 2 * S // P, D // 2])).then_inc(s_yzero, 16)
            sp.wait_ge(s_biased, t_of[(16 * B - 1, 0)] + 1)
            sp.dma_start(gb[:, 0], strip(C)).then_inc(s_strip[C], 16)
            for z, (m, g) in enumerate(((C, 5), (F, 3))):
                sp.wait_ge(s_pfull, P_AT[("proj", m, g)] + 1)
                load_gate_up(sp, z, z + 2)
                load_down(sp, z, z + 2)
                if z == 0:
                    load_gate_up(sp, 3, 1, (1,))
                    load_down(sp, 3, 1)
            sp.wait_ge(s_score, t_of[(16 * F - 1, 0)] + 1)
            load_spare(sp, 1, 1)
            sp.wait_ge(s_biased, t_of[(16 * F - 1, 0)] + 1)
            sp.dma_start(lnfb, ln_f.rearrange("(a n) -> a n", a=1).to_broadcast([P, D])).then_inc(s_lnfb, 16)
            for i in range(2):
                sp.dma_start(xres[:, i], x[0, i * P:(i + 1) * P, :]).then_inc(s_xres[i], 16)
            for i in range(NT):
                if i + 2 < NT:
                    landed(sp, ("out", i, 1))
                    sp.dma_start(xres[:, i], x[0, (i + 2) * P:(i + 3) * P, :]).then_inc(s_xres[i], 16)
                if i == NT - 1:
                    sp.wait_ge(s_pfull, P_AT[("out", i, 1)] + 1)
                    load_gate_up(sp, 2, 0)
                    load_down(sp, 2, 0)
                    load_gate_up(sp, 3, 1, (0,))
                sp.wait_ge(s_h2, i + 1)
                sp.dma_start(h2_d[i * P:(i + 1) * P, :], hrow[:, i % 2, :]).then_inc(s_h2out[i], 16)
            sp.wait_ge(s_pv, len(units))
            landed(sp, ("out", NT - 1, 1))
            sp.wait_ge(s_pfull, P_AT[("route", NT - 1)] + 1)
            sp.wait_ge(s_xg[0], 16)
            for z, which in ((0, 0), (0, 1), (1, 0)):
                load_spare(sp, z, which)
            def pair_gate_up(it, j, done):
                sp.wait_ge(s_gu, done)
                for z in range(2):
                    load_gate_up(sp, 4 * it + (2 * j + z), 2 * j + z)

            def pair_down(it, j):
                sp.wait_ge(s_down, 2 * it + (j - 1))
                for z in range(2):
                    load_down(sp, 4 * it + (2 * j + z), (2 * j + z + 2) % 4)

            pair_gate_up(1, 1, 1)
            pair_down(1, 0)
            pair_gate_up(2, 0, 2)
            pair_down(1, 1)
            with sp.Fori(2, E // 4 - 1, 1) as it:
                pair_gate_up(it, 1, 2 * it)
                pair_down(it, 0)
                pair_gate_up(it + 1, 0, 2 * it + 1)
                pair_down(it, 1)
            last_it = E // 4 - 1
            pair_gate_up(last_it, 1, 2 * last_it)
            pair_down(last_it, 0)
            pair_down(last_it, 1)
            sp.wait_ge(s_crowd, 1)
            sp.wait_ge(s_down, PAIRS)
            with sp.register("sp_crowd") as r:
                sp.reg_load(r, crowd[0:1, 0:1])
                with sp.If(sp.snap(r) > CAP):
                    sp.dma_start(h2rows, h2_d.rearrange("(i p) n -> p i n", p=P)).then_inc(s_dh2, 16)
                    with sp.Fori(0, E, 1) as e:
                        sp.wait_ge(s_dcur, e + 1)
                        for dst, src in expert_chunks(e, 0):
                            sp.dma_start(dst, src).then_inc(s_dw, 16)
                    sp.wait_ge(s_dacc, 2 * NT * E)
            for j in range(2):
                sp.wait_ge(s_yst[j], 16 * (PAIRS // 2))
            for i in range(NT):
                for k in range(2):
                    r0 = k * S + i * P
                    sp.dma_start(ybuf[:, i, k], y_d[r0:r0 + P, :]).then_inc(s_yg[2 * i + k], 16)
            for i in range(NT):
                if i < NT // 2:
                    sp.wait_ge(s_orow, i + 1)
                else:
                    sp.wait_ge(s_orow_last, i - NT // 2 + 1)
                sp.dma_start(out[0, i * P:(i + 1) * P, :], orow[:, i, :]).then_inc(s_out, 16)
            sp.wait_ge(s_out, 16 * NT)

        @block.gpsimd
        def _(pool):
            for tile, value in blank:
                pool.memset(tile[:], value).then_inc(s_pool, 1)
            pool.iota(iota_e[:], [[1, E]], base=0, channel_multiplier=0,
                      allow_small_or_imprecise_dtypes=True).then_inc(s_const, 1)
            pool.iota(iota_p[:], [[1, E]], base=-int(PLACE), channel_multiplier=0,
                      allow_small_or_imprecise_dtypes=True).then_inc(s_const, 1)
            pool.iota(iota_s[:], [[1, CAP]], base=1, channel_multiplier=0,
                      allow_small_or_imprecise_dtypes=True).then_inc(s_const, 1)
            pool.iota(token[:, :, 0], [[0, NT]], base=0, channel_multiplier=1,
                      allow_small_or_imprecise_dtypes=True).then_inc(s_const, 1)
            pool.memset(token[:, :, 1], 1.0).then_inc(s_const, 1)
            pool.wait_ge(s_pool, len(blank))
            for tile, op, fill, base, step, cm in (
                    (ident, ALU.not_equal, 1.0, 0, -1, 1), 
                    (upto, ALU.is_ge, 0.0, 0, 1, -1), (before, ALU.is_gt, 0.0, 0, 1, -1),
                    (future, ALU.is_ge, NEG, P - 1, -1, -1)):
                pool.affine_select(out=tile[:], in_=tile[:], compare_op=op, fill=fill, base=base,
                                   pattern=[[step, tile.shape[1]]], channel_multiplier=cm).then_inc(s_const, 1)
            roots = [0]

            def inverse_root(dst, src, scale):
                n = src.shape[1]
                tmp = rtmp[:, roots[0], 0:n]
                roots[0] += 1
                pool.tensor_scalar(tmp, src, scale, EPS, ALU.mult, ALU.add).then_inc(s_root, 1)
                pool.wait_ge(s_root, roots[0])
                return pool.tensor_tensor(dst, tmp, power[:, 0:n], ALU.pow)

            for item in plan:
                kind = item[0]
                if kind == "ln1":
                    i = item[1]
                    pool.wait_ge(s_sq, i + 1)
                    inverse_root(rs[:, 0, i:i + 1], ms[:, 0, i:i + 1], 1.0).then_inc(s_rs1, 1)
                    if i == NT - 1:
                        pool.memset(zeros, 0.0).then_inc(s_zeros, 1)
                elif kind == "ln2":
                    i = item[1]
                    pool.wait_ge(s_sq2, i + 1)
                    inverse_root(rs[:, 1, i:i + 1], ms[:, 1, i:i + 1], 1.0).then_inc(s_rs2, 1)
                elif kind == "onorm" and item[1] // 4 == B:
                    pool.wait_ge(s_osq, item[1] - 4 * B + 1)
                    inverse_root(onrm[:, 1, :], onrm[:, 0, :], 1.0 / HD).then_inc(s_ors, 1)

            pool.wait_ge(s_score, len(parts))
            pool.memset(xg, 0.0).then_inc(s_xzero, 1)

            def gather(pair):
                pool.indirect_dma_start(out=xg[:, pair % 2], out_offset=None, in_=h2_d[:, :],
                                        in_offset=bass.IndirectOffsetOnAxis(ap=idx[:, pair:pair + 1], axis=0),
                                        bounds_check=S - 1, oob_is_err=False).then_inc(s_xg[pair % 2], 16)

            pool.wait_ge(s_xzero, 1)
            pool.wait_ge(s_idx, 1)
            for i in range(NT):
                pool.wait_ge(s_h2out[i], 16)
            gather(0)
            gather(1)
            pool.wait_ge(s_dest, 1)
            pool.wait_ge(s_yzero, 16)
            for pair in range(PAIRS + 1):
                if pair + 2 < PAIRS:
                    pool.wait_ge(s_mt, 2 * pair + 2)
                    gather(pair + 2)
                if pair:
                    y = pair - 1
                    pool.wait_ge(s_yd, y + 1)
                    pool.wait_ge(s_ya, y + 1)
                    pool.indirect_dma_start(out=y_d[:, :], in_=yrow[:, y % 2, :], in_offset=None,
                                            out_offset=bass.IndirectOffsetOnAxis(ap=dest[:, y:y + 1], axis=0),
                                            bounds_check=2 * S - 1, oob_is_err=False).then_inc(s_yst[y % 2], 16)
            for i in range(NT):
                pool.wait_ge(s_sq3, i + 1)
                inverse_root(rs[:, 2, i:i + 1], ms[:, 2, i:i + 1], 1.0).then_inc(s_rs3, 1)
                if 0 < i <= NT // 2:
                    if i == 1:
                        pool.wait_ge(s_lnfb, 16)
                    pool.wait_ge(s_scaled, i)
                    pool.tensor_tensor(orow[:, i - 1, :], orow[:, i - 1, :], lnfb, ALU.mult).then_inc(s_orow, 1)

        @block.scalar
        def _(act):
            act.dma_start(onehot_rows, bucket_rows).then_inc(s_tabin, 16)
            act.dma_start(relb[0:BUCKETS, :], rel_bias).then_inc(s_tabin, 16)
            act.dma_start(relb[BUCKETS:BUCKETS + 2, :], bias_cols).then_inc(s_tabin, 16)

            def copy_out(k, dst, src):
                act.wait_ge(s_tfull, k + 1)
                act.activation(dst, src, ACT.Copy).then_inc(s_tempty, 1)

            act.wait_ge(s_pool, len(blank))
            act.activation(lcur[:, 0:1], power[:, 0:1], ACT.Square)

            for item in plan:
                kind = item[0]
                if item == ("proj", A, 0, 0):
                    for z, v in enumerate((lam_q1, lam_k1, lam_q2, lam_k2)):
                        act.dma_start(lamv[:, z, :], v.to_broadcast([P, HD // 2])).then_inc(s_small, 16)
                    act.dma_start(subg[:], subln_g.to_broadcast([P, HD])).then_inc(s_small, 16)
                    act.dma_start(bf[:], b_forget.to_broadcast([P, H])).then_inc(s_small, 16)
                    act.dma_start(wr[:, :, 0:NG], w_group[0].rearrange("(c p) n -> p c n", p=P)).then_inc(s_small, 16)
                    act.dma_start(wr[:, :, NG:], w_expert[0].rearrange("(c p) n -> p c n", p=P)).then_inc(s_small, 16)
                    act.dma_start(gain2, ln2[0].rearrange("(c p) -> p c", p=P),
                                  allow_slow_non_contiguous=True).then_inc(s_small, 16)
                    act.dma_start(rb[:, 0:NG], b_group.to_broadcast([P, NG])).then_inc(s_small, 16)
                    act.dma_start(rb[:, NG:], b_expert[0:1].rearrange("a g e -> a (g e)").to_broadcast([P, E])).then_inc(s_small, 16)
                if kind == "ln1":
                    i = item[1]
                    act.wait_ge(s_xin[i], 16)
                    if i:
                        act.wait_ge(s_sq, i)
                    act.activation(junk[:], xo[:, i, :], ACT.Square, scale=1.0 / 32,
                                   accum_out=ms[:, 0, i:i + 1]).then_inc(s_sq, 1)
                elif kind in ("hT", "h2T"):
                    i = item[1]
                    if kind == "h2T" and i >= 2:
                        act.wait_ge(s_pfull, P_AT[("route", i - 2)] + 1)
                    for z in range(2):
                        k = T_AT[item] + z
                        dst = hT[:, 4 * z:4 * z + 4, i * P:(i + 1) * P] if kind == "hT" else x2T[:, i % 2, 4 * z:4 * z + 4, :]
                        copy_out(k, dst, tbank[k % 2][:].rearrange("p (c t) -> p c t", c=4))
                elif kind == "score":
                    n = item[1]
                    if n == 16 * A:
                        act.wait_ge(s_lam, 2)
                        act.activation(lams[:, 2:4], lams[:, 0:2], ACT.Exp).then_inc(s_lamexp, 1)
                    m, i, h = units[n]
                    for s in range(2 if m == B else 1):
                        t = t_of[(n, s)]
                        e = sc[:, t % 4, 0:(i + 1) * P]
                        act.wait_ge(s_biased, t + 1)
                        act.activation(e, e, ACT.Exp, bias=negmax[:, t:t + 1], scale=-1.0,
                                       accum_out=lsum[:, t:t + 1]).then_inc(s_exp, 1)
                elif kind == "turn":
                    n = item[1]
                    k = T_AT[item]
                    nk = (units[n][1] + 1) * P
                    if n >= 2:
                        act.wait_ge(s_pv, n - 1)
                    copy_out(k, pt[:, n % 2, 0:nk], tbank[k % 2][:, 0:nk])
                elif kind == "z":
                    act.wait_ge(s_zin, 1)
                    act.activation(zt[:, 1, :], zt[:, 0, :], ACT.Abs).then_inc(s_zabs, 1)
                    act.wait_ge(s_zabs, 1)
                    act.activation(zt[:, 2, :], zt[:, 1, :], ACT.Exp, scale=-1.0).then_inc(s_zexp, 1)
                    act.wait_ge(s_zexp, 1)
                    act.activation(zt[:, 3, :], zt[:, 2, :], ACT.Ln, bias=1.0).then_inc(s_zln, 1)
                elif kind == "oT":
                    i = item[1]
                    for z in range(2):
                        k = T_AT[item] + z
                        if i and not z:
                            act.wait_ge(s_pfull, P_AT[("out", i - 1, 1)] + 1)
                        copy_out(k, falling(oT[:, 4 * z:4 * z + 4, :]), tbank[k % 2][:].rearrange("p (c t) -> p c t", c=4))
                elif kind == "ln2":
                    i = item[1]
                    if i == 0:
                        act.wait_ge(s_yzero, 16)
                    landed(act, ("out", i, 1))
                    if i:
                        act.wait_ge(s_sq2, i)
                    act.activation(junk[:], xo[:, i, :], ACT.Square, scale=1.0 / 32,
                                   accum_out=ms[:, 1, i:i + 1]).then_inc(s_sq2, 1)
                elif kind == "weights":
                    i = item[1]
                    act.wait_ge(s_top, i + 1)
                    act.activation(gexp[:, i, :], logit[:, i, 0:NG], ACT.Exp, bias=picks[:, i, 3:4],
                                   accum_out=gsc[:, i, 0:1]).then_inc(s_gexp, 1)
                    act.activation(gsc[:, i, 1:2], picks[:, i, 1:2], ACT.Exp, scale=-1.0,
                                   bias=picks[:, i, 2:3]).then_inc(s_gexp, 1)

            def rows_to_chunks(q, j):
                for z in range(2):
                    act.wait_ge(s_mt, 2 * q + (z + 1))
                    act.activation(xgT[:, 8 * j + 4 * z:8 * j + 4 * z + 4, :],
                                   tbank[z][:].rearrange("p (c t) -> p c t", c=4), ACT.Copy).then_inc(s_mx, 1)

            def rows_out(it, j, first=False):
                q = 2 * it + j
                act.wait_ge(s_down, q + 1)
                if not first:
                    act.wait_ge(s_yst[j], 16 * it)
                act.activation(yrow[:, j, 512:1024], (pbank, obank)[j][1][:], ACT.Copy).then_inc(s_ya, 1)

            def pair_steps(it, j, before_first=False, last=False):
                q = 2 * it + j
                act.wait_ge(s_gu, q + 1)
                act.activation(gate_act[:, j, :], sbank[j][:, 0:FE], ACT.Silu).then_inc(s_silu, 1)
                if not last:
                    rows_to_chunks(q + 1, (j + 1) % 2)
                rows_out(*pair_before(it, j), first=before_first)

            rows_to_chunks(0, 0)
            act.wait_ge(s_gu, 1)
            act.activation(gate_act[:, 0, :], sbank[0][:, 0:FE], ACT.Silu).then_inc(s_silu, 1)
            rows_to_chunks(1, 1)
            pair_steps(0, 1, before_first=True)
            pair_steps(1, 0, before_first=True)
            pair_steps(1, 1)
            with act.Fori(2, E // 4 - 1, 1) as it:
                for j in range(2):
                    pair_steps(it, j)
            last_it = E // 4 - 1
            pair_steps(last_it, 0)
            pair_steps(last_it, 1, last=True)
            rows_out(last_it, 1)

            act.wait_ge(s_crowd, 1)
            with act.register("act_crowd") as r:
                act.reg_load(r, crowd[0:1, 0:1])
                with act.If(act.snap(r) > CAP):
                    for n in range(2 * NT):
                        i, z = divmod(n, 2)
                        act.wait_ge(s_dturn, n + 1)
                        act.activation(hT[:, 4 * z:4 * z + 4, i * P:(i + 1) * P],
                                       tbank[z][:].rearrange("p (c t) -> p c t", c=4), ACT.Copy).then_inc(s_dhT, 1)
                    with act.Fori(0, E, 1) as e:
                        for a in range(FT):
                            act.wait_ge(s_dgu, FT * e + (a + 1))
                            act.activation(dense_act[:, a, :], pbank[0][:], ACT.Silu).then_inc(s_dsilu, 1)
            for i in range(NT):
                act.wait_ge(s_sum, 2 * i + 2)
                if i:
                    act.wait_ge(s_sq3, i)
                act.activation(junk[:], xo[:, i, :], ACT.Square, scale=1.0 / 32,
                               accum_out=ms[:, 2, i:i + 1]).then_inc(s_sq3, 1)
                if 0 < i <= NT // 2:
                    act.wait_ge(s_rs3, i)
                    act.activation(orow[:, i - 1, :], xo[:, i - 1, :], ACT.Copy, scale=rs[:, 2, i - 1:i]).then_inc(s_scaled, 1)

        @block.tensor
        def _(pe):
            def open_p(k):
                if k >= 2:
                    pe.wait_ge(s_pempty, k - 1)
                return pbank[k % 2]

            def open_t(k):
                if k >= 2:
                    pe.wait_ge(s_tempty, k - 1)
                return tbank[k % 2]

            def turn8(item, src):
                for z in range(2):
                    k = T_AT[item] + z
                    t = open_t(k)
                    for c in range(4):
                        last = pe.transpose(t[:, c * P:(c + 1) * P], src[:, (4 * z + c) * P:(4 * z + c + 1) * P], ident[:])
                    last.then_inc(s_tfull, 1)

            for item in plan:
                kind = item[0]
                if kind == "table":
                    pe.wait_ge(s_const, 9)
                    pe.wait_ge(s_tabin, 48)
                    k = P_AT[item]
                    for z, (a, b) in enumerate(((0, 512), (512, SPAN))):
                        pe.matmul(open_p(k + z)[0:12, 0:b - a], relb[:], onehot_rows[:, a:b],
                                  start=True, stop=True).then_inc(s_pfull, 1)
                elif kind == "hT":
                    i = item[1]
                    pe.wait_ge(s_hrow, i + 1)
                    turn8(item, hrow[:, i % 2, :])
                elif kind == "proj":
                    m, g, step = item[1:]
                    k = P_AT[item[:3]]
                    if (m, g, step) == (A, 0, 0):
                        turned(pe, ("hT", NT - 1), 2)
                    chunk = 3 * m + min(g // 2, 2)
                    if g % 2 == 0 and step == 0:
                        pe.wait_ge(s_win[chunk], 16)
                    w = ring[:, chunk, :].rearrange("p (c n) -> p c n", c=KC)
                    o = pbank[k % 2] if step else open_p(k)
                    if g < 4:
                        last = pe.matmul(o[:], w[:, step, (g % 2) * P:(g % 2 + 1) * P], hT[:, step, :],
                                         start=(step == 0), stop=(step == KC - 1))
                    elif m == F:
                        last = pe.matmul(o[:, 0:GW + H], hT[:, step, (g - 4) * P:(g - 3) * P], fv[:, step, :],
                                         start=(step == 0), stop=(step == KC - 1))
                    else:
                        i, c0 = divmod(2 * step, KC)
                        t0 = (2 * (g - 4) + i) * P
                        for c in (c0, c0 + 1):
                            last = pe.matmul(o[:, i * GW:(i + 1) * GW], hT[:, c, t0:t0 + P], w[:, c, :],
                                             start=(c == 0), stop=(c == KC - 1))
                    if step == KC - 1:
                        last.then_inc(s_pfull, 1)
                elif kind == "cb":
                    h = item[1]
                    o = open_p(P_AT[item])
                    pe.wait_ge(s_lf, NT * h + NT)
                    for i in range(NT):
                        last = pe.matmul(o[:, i * P:S], lfb_view(h, i), upto[:, 0:S - i * P],
                                         start=(i == 0), stop=(i == NT - 1))
                    last.then_inc(s_pfull, 1)
                elif kind == "score" and (units[item[1]][0] == B or item[1] % 2 == 0):
                    n = item[1]
                    m, i, h = units[n]
                    nk = (i + 1) * P
                    if i == 0 and h % 2 == 0:
                        landed(pe, ("proj", m, h // 2))
                        landed(pe, ("proj", m, 2 + h // 2))
                    t = t_of[(n, 0)]
                    if t >= 2:
                        pe.wait_ge(s_biased, t)
                    kd = HD // 2 if m == B else HD
                    for z in range(2):
                        r0 = (h % 2) * HD + z * kd if m == B else z * HD
                        q = qk[r0:r0 + kd, m % 2, h // 2, i * P:(i + 1) * P]
                        k = qk[r0:r0 + kd, m % 2, 2 + h // 2, 0:nk]
                        last = pe.matmul(sbank[(t + z) % 2][:, 0:nk], q, k, start=True, stop=(m != F))
                        if m != F:
                            last.then_inc(s_score, 1)
                    if m == F:
                        for z in range(2):
                            pe.matmul(sbank[(t + z) % 2][:, i * P:nk], ident[:], future[:], start=False,
                                      stop=True).then_inc(s_score, 1)
                elif kind == "turn":
                    n = item[1]
                    m, i, h = units[n]
                    k = T_AT[item]
                    t = t_of[(n, 0)]
                    if m == B:
                        pe.wait_ge(s_mix, n - 16 * B + 1)
                    else:
                        pe.wait_ge(s_exp, t + 1)
                    o = open_t(k)
                    for b in range(i + 1):
                        last = pe.transpose(o[:, b * P:(b + 1) * P], sc[:, t % 4, b * P:(b + 1) * P], ident[:])
                    last.then_inc(s_tfull, 1)
                elif kind == "pv":
                    n = item[1]
                    m, i, h = units[n]
                    turned(pe, ("turn", n))
                    if h == 0:
                        if n // 4 >= 2:
                            pe.wait_ge(s_onorm, n // 4 - 1)
                        landed(pe, ("proj", m, 4 + (i if m == F else i // 2)))
                    o = obank[(n // 4) % 2]
                    for b in range(i + 1):
                        last = pe.matmul(o[:, h * HD:(h + 1) * HD], pt[:, n % 2, b * P:(b + 1) * P],
                                         vv[:, m % 2, b, h * HD:(h + 1) * HD], start=(b == 0), stop=(b == i))
                    last.then_inc(s_pv, 1)
                elif kind == "oT":
                    i = item[1]
                    pe.wait_ge(s_onorm, 4 * F + i + 1)
                    turn8(item, xo[:, i, :])
                elif kind == "out":
                    i, z, c = item[1:]
                    k = P_AT[item[:3]]
                    if z == 0 and c % 4 == 0:
                        turned(pe, ("oT", i), 1 + c // 4)
                        if i == 0 and c == 0:
                            for j in range(4):
                                pe.wait_ge(s_wout[j], 16)
                    o = pbank[k % 2] if c else open_p(k)
                    last = pe.matmul(o[:], oT[:, c, :], wout[:, c, z * 512:(z + 1) * 512],
                                     start=(c == 0), stop=(c == KC - 1))
                    if c == KC - 1:
                        last.then_inc(s_pfull, 1)
                elif kind == "h2T":
                    i = item[1]
                    landed(pe, ("out", i, 1))
                    turn8(item, xo[:, i, :])
                elif kind == "route":
                    i = item[1]
                    o = open_p(P_AT[item])
                    for c in range(KC):
                        if c % 4 == 0:
                            turned(pe, ("h2T", i), 1 + c // 4)
                        last = pe.matmul(o[:, 0:NG + E], x2T[:, i % 2, c, :], wr[:, c, :],
                                         start=(c == 0), stop=(c == KC - 1))
                    last.then_inc(s_pfull, 1)
                elif kind in ("rank", "count"):
                    i = item[1] if kind == "rank" else NT
                    o = open_p(P_AT[item])
                    for z in range(min(i, NT - 1) + 1):
                        pe.wait_ge(s_pick, z + 1)
                        own = kind == "rank" and z == i
                        last = pe.matmul(o[:, 0:E], before[:] if own else upto[:, P:2 * P], mem[:, z, :],
                                         start=(z == 0), stop=(z == min(i, NT - 1)))
                    last.then_inc(s_pfull, 1)
                elif kind == "slot":
                    i = item[1]
                    o = open_p(P_AT[item])
                    pe.wait_ge(s_spread, i + 1)
                    for q in range(PAIRS):
                        last = pe.matmul(o[:, 3 * q:3 * q + 3], spread[:, q * P:(q + 1) * P], token[:, i, :],
                                         start=True, stop=True)
                    last.then_inc(s_pfull, 1)

            def turn_rows(q, j, first):
                for z in range(2):
                    if not first:
                        pe.wait_ge(s_mx, 2 * q + (z - 1))
                    for c in range(4):
                        last = pe.transpose(tbank[z][:, c * P:(c + 1) * P],
                                            xg[:, j, (4 * z + c) * P:(4 * z + c + 1) * P], ident[:])
                    last.then_inc(s_mt, 1)

            half_of = lambda v, z: v[z * CAP:(z + 1) * CAP, :]

            def gate_up_products(it, j, first=False, early=False):
                q = 2 * it + j
                wide = [(2 * j + z + 2 * first) % 4 for z in range(2)]
                for z, b in enumerate(wide):
                    if early:
                        pe.wait_ge(s_spare[z], 32)
                    else:
                        pe.wait_ge(s_wgu[b], 32 * it + (32 if first or j == 1 else 0))
                if not first:
                    pe.wait_ge(s_hidT, 2 * it + (j - 1))
                for c in range(KC):
                    if c == 0:
                        pe.wait_ge(s_mx, 2 * q + (2 if early else 1))
                    elif c == KC // 2 and not early:
                        pe.wait_ge(s_mx, 2 * q + 2)
                    for z, b in enumerate(wide):
                        x_of = lambda c: xgT[:, 8 * j + c, z * CAP:(z + 1) * CAP]
                        if early:
                            u = 2 * c // KC
                            for c2 in ((2 * c) % KC, (2 * c + 1) % KC):
                                last = pe.matmul(half_of(sbank[j], z)[:, u * FE:(u + 1) * FE], x_of(c2),
                                                 spare[z][u][:, c2, :], start=(c2 == 0), stop=(c2 == KC - 1))
                        else:
                            last = pe.matmul(half_of(sbank[j], z), x_of(c), gate_up(b)[:, c, :, :],
                                             start=(c == 0), stop=(c == KC - 1))
                last.then_inc(s_gu, 1)

            def turn_hidden(it, j):
                pe.wait_ge(s_hid, 2 * it + j + 1)
                for a in range(FT):
                    last = pe.transpose(sbank[j][:, a * P:(a + 1) * P], hid[:, j, a * P:(a + 1) * P], ident[:])
                last.then_inc(s_turned, 1)

            def down_products(it, j, first=False):
                q = 2 * it + j
                buffers = [(2 * j + z + 2) % 4 for z in range(2)]
                pe.wait_ge(s_hidT, q + 1)
                for b in buffers:
                    pe.wait_ge(s_wdn[b], 16 * it + 16)
                if not first:
                    pe.wait_ge(s_yd, 2 * it + (j - 1))
                    pe.wait_ge(s_ya, 2 * it + (j - 1))
                y = (pbank, obank)[j]
                for half in range(2):
                    for a in range(FT):
                        for z, b in enumerate(buffers):
                            slots = slice(a * P + z * CAP, a * P + (z + 1) * CAP)
                            last = pe.matmul(half_of(y[half], z), hidT[:, j, slots],
                                             down(b)[:, a, half * 512:(half + 1) * 512],
                                             start=(a == 0), stop=(a == FT - 1))
                last.then_inc(s_down, 1)

            def next_rows(it, j):
                pe.wait_ge(s_xg[(j + 1) % 2], 16 * (it + j) + 16)
                turn_rows(2 * it + j + 1, (j + 1) % 2, False)

            def pair_steps(it, j, first=False, early=False, before_first=False, last_pair=False):
                gate_up_products(it, j, first, early)
                turn_hidden(*pair_before(it, j))
                if not last_pair:
                    next_rows(it, j)
                down_products(*pair_before(it, j), first=before_first)

            pe.wait_ge(s_tempty, T_N)
            pe.wait_ge(s_pempty, P_N)
            pe.wait_ge(s_xg[0], 16)
            turn_rows(0, 0, True)
            gate_up_products(0, 0, first=True)
            next_rows(0, 0)
            pair_steps(0, 1, first=True, before_first=True)
            pair_steps(1, 0, early=True, before_first=True)
            pair_steps(1, 1)
            with pe.Fori(2, E // 4 - 1, 1) as it:
                for j in range(2):
                    pair_steps(it, j)
            last_it = E // 4 - 1
            pair_steps(last_it, 0)
            pair_steps(last_it, 1, last_pair=True)
            turn_hidden(last_it, 1)
            down_products(last_it, 1)

            pe.wait_ge(s_crowd, 1)
            with pe.register("pe_crowd") as r:
                pe.reg_load(r, crowd[0:1, 0:1])
                with pe.If(pe.snap(r) > CAP):
                    pe.wait_ge(s_yd, PAIRS)
                    pe.wait_ge(s_ya, PAIRS)
                    pe.wait_ge(s_dh2, 16)
                    for i in range(NT):
                        for z in range(2):
                            n = 2 * i + z
                            if n >= 2:
                                pe.wait_ge(s_dhT, n - 1)
                            for c in range(4):
                                last = pe.transpose(tbank[z][:, c * P:(c + 1) * P],
                                                    h2rows[:, i, (4 * z + c) * P:(4 * z + c + 1) * P], ident[:])
                            last.then_inc(s_dturn, 1)
                    pe.wait_ge(s_dhT, 2 * NT)
                    with pe.Fori(0, E, 1) as e:
                        pe.wait_ge(s_dw, 48 * e + 48)
                        pe.wait_ge(s_dcur, e + 1)
                        for a in range(FT):
                            if a:
                                pe.wait_ge(s_dhid, FT * e + a)
                            for u in range(2):
                                for c in range(KC):
                                    last = pe.matmul(pbank[u][:], gate_up(0)[:, c, u, a * P:(a + 1) * P], hT[:, c, :],
                                                     start=(c == 0), stop=(c == KC - 1))
                            last.then_inc(s_dgu, 1)
                        pe.wait_ge(s_dhid, FT * e + FT)
                        for i in range(NT):
                            for half in range(2):
                                n = 2 * i + half
                                if n >= 2:
                                    pe.wait_ge(s_dacc, 2 * NT * e + (n - 1))
                                for a in range(FT):
                                    last = pe.matmul(obank[half][:], dense_hid[:, a, i * P:(i + 1) * P],
                                                     down(0)[:, a, half * 512:(half + 1) * 512],
                                                     start=(a == 0), stop=(a == FT - 1))
                                last.then_inc(s_dy, 1)

        @block.vector
        def _(dve):
            steps = [0]

            def link(ins):
                steps[0] += 1
                ins.then_inc(s_dve, 1)
                dve.wait_ge(s_dve, steps[0])

            def permuted(row):
                return row.rearrange("p (c j) -> p j c", c=KC)

            def normalise(dst, src, r):
                return dve.scalar_tensor_tensor(out=permuted(dst), in0=src.rearrange("p (j c) -> p j c", c=KC),
                                                scalar=r, in1=lnb[:].rearrange("p (j c) -> p j c", c=KC),
                                                op0=ALU.mult, op1=ALU.mult)

            def take(k):
                dve.wait_ge(s_pfull, k + 1)
                return pbank[k % 2]

            def first_max(v, n, top, onehot, i):
                link(dve.tensor_reduce(top, v, AX.X, ALU.max))
                link(dve.scalar_tensor_tensor(out=pick[:, 2, 0:n], in0=v, scalar=top, in1=iota_p[:, 0:n],
                                              op0=ALU.is_equal, op1=ALU.mult))
                link(dve.tensor_reduce(picks[:, i, 0:1], pick[:, 2, 0:n], AX.X, ALU.min))
                if onehot is not None:
                    link(dve.tensor_scalar(onehot, pick[:, 2, 0:n], picks[:, i, 0:1], None, ALU.is_equal))

            def combine_weights(i):
                w = lambda c: tw[:, i, c:c + 1]
                dve.wait_ge(s_gexp, 2 * i + 2)
                link(dve.reciprocal(w(0), gsc[:, i, 0:1]))
                link(dve.tensor_scalar(w(1), gsc[:, i, 1:2], 1.0, None, ALU.add))
                link(dve.reciprocal(w(2), w(1)))
                link(dve.tensor_tensor(w(3), w(0), w(2), ALU.mult))
                link(dve.tensor_tensor(w(4), w(3), gsc[:, i, 1:2], ALU.mult))
                for k in range(2):
                    link(dve.tensor_tensor_reduce(pick[:, 1, :], oh[:, i, k, :], rank[:, i, :], 1.0, 0.0,
                                                  ALU.mult, ALU.add, w(5 + k)))
                link(dve.tensor_scalar(tw[:, i, 9:11], tw[:, i, 5:7], float(CAP), None, ALU.is_lt))
                link(dve.tensor_tensor(comb[:, i, :], tw[:, i, 3:5], tw[:, i, 9:11], ALU.mult))
                link(dve.tensor_scalar(pick[:, 0, :], oh[:, i, 0, :], w(3), None, ALU.mult))
                link(dve.scalar_tensor_tensor(out=pick[:, 1, :], in0=oh[:, i, 1, :], scalar=w(4),
                                              in1=pick[:, 0, :], op0=ALU.mult, op1=ALU.add))
                link(dve.scalar_tensor_tensor(out=late[:, i, :], in0=rank[:, i, :], scalar=float(CAP),
                                              in1=pick[:, 1, :], op0=ALU.is_ge, op1=ALU.mult))

            for item in plan:
                kind = item[0]
                if kind == "table":
                    for z, (a, b) in enumerate(((0, 512), (512, SPAN))):
                        o = take(P_AT[item] + z)
                        dve.tensor_copy(table_rows[:, a:b], o[0:12, 0:b - a]).then_inc(s_pempty, 1)
                elif kind == "ln1":
                    i = item[1]
                    if i == 0:
                        dve.wait_ge(s_ln1b, 16)
                    if i >= 2:
                        dve.wait_ge(s_tfull, T_AT[("hT", i - 2)] + 2)
                    dve.wait_ge(s_rs1, i + 1)
                    dve.wait_ge(s_xin[i], 16)
                    normalise(hrow[:, i % 2, :], xo[:, i, :], rs[:, 0, i:i + 1]).then_inc(s_hrow, 1)
                elif kind == "proj" and item[3] == KC - 1:
                    m, g = item[1:3]
                    o = take(P_AT[item[:3]])
                    if g < 2:
                        scale = (HD // 2 if m == B else HD) ** -0.5
                        dve.tensor_scalar(falling(qk[:, m % 2, g, :].rearrange("p (i t) -> p i t", i=NT)),
                                          o[:].rearrange("p (i t) -> p i t", i=NT), scale, None,
                                          ALU.mult).then_inc(s_pempty, 1)
                    elif g < 4:
                        dve.tensor_copy(qk[:, m % 2, g, :], o[:]).then_inc(s_pempty, 1)
                    elif m == F:
                        dve.tensor_copy(vv[:, 1, g - 4, :], o[:, 0:GW]).then_inc(s_zraw, 1)
                        dve.tensor_copy(zraw[:, g - 4, :], o[:, GW:GW + H]).then_inc(s_pempty, 1)
                    else:
                        dve.tensor_copy(vv[:, m % 2, 2 * (g - 4):2 * (g - 4) + 2, :],
                                        o[:].rearrange("p (i n) -> p i n", i=2)).then_inc(s_pempty, 1)
                elif kind == "z":
                    landed(dve, ("proj", F, 7))
                    dve.tensor_tensor(zt[:, 0, :].rearrange("p (i h) -> p i h", h=H), zraw[:],
                                      bf[:].unsqueeze(1).to_broadcast([P, NT, H]), ALU.add).then_inc(s_zin, 1)
                    dve.wait_ge(s_zin, 1)
                elif kind == "gates":
                    dve.wait_ge(s_zabs, 1)
                    link(dve.tensor_scalar(zt[:, 0, :], zt[:, 0, :], 0.0, None, ALU.min))
                    dve.wait_ge(s_zln, 1)
                    link(dve.tensor_tensor(zt[:, 0, :], zt[:, 0, :], zt[:, 3, :], ALU.subtract))
                    for h in range(H):
                        for i in range(NT):
                            gates = zt[:, 0, i * H + h:i * H + h + 1]
                            dve.tensor_copy(lfb_view(h, i), gates.to_broadcast([P, P])).then_inc(s_lf, 1)
                elif kind == "cb":
                    h = item[1]
                    if h == 0:
                        dve.wait_ge(s_biased, t_of[(16 * C - 1, 1)] + 1)
                    dve.tensor_scalar(gb[:, 1, h, :], take(P_AT[item])[:], -1.0, None, ALU.mult).then_inc(s_pempty, 1)
                elif kind == "score":
                    n = item[1]
                    m, i, h = units[n]
                    nk = (i + 1) * P
                    if n == 16 * A:
                        dve.wait_ge(s_small, 16 * N_SMALL)
                        link(dve.tensor_tensor(wr[:], wr[:], gain2.unsqueeze(2).to_broadcast([P, KC, NG + E]),
                                               ALU.mult))
                        for z in range(2):
                            dve.tensor_tensor_reduce(lamv[:, 2 * z, :], lamv[:, 2 * z, :], lamv[:, 2 * z + 1, :], 1.0, 0.0,
                                                     ALU.mult, ALU.add, lams[:, z:z + 1]).then_inc(s_lam, 1)
                    if n == 16 * A + 1:
                        dve.wait_ge(s_lamexp, 1)
                        link(dve.tensor_tensor(lams[:, 4:5], lams[:, 2:3], lams[:, 3:4], ALU.subtract))
                        link(dve.tensor_scalar(lams[:, 5:6], lams[:, 4:5], LAMBDA_INIT, -1.0, ALU.add, ALU.mult))
                        link(dve.tensor_scalar(subg[:], subg[:], 1.0 - LAMBDA_INIT, None, ALU.mult))
                    if n % 16 == 0 and m != F:
                        dve.wait_ge(s_strip[m], 16)
                    if i == 0 and m == F:
                        landed(dve, ("cb", h))
                    for s in range(2 if m == B else 1):
                        t = t_of[(n, s)]
                        bias = gb[:, m % 2, h, (0 if m == F else S - nk):(nk if m == F else S)]
                        if t >= 4:
                            dve.wait_ge(s_tfull, T_AT[("turn", parts[t - 4][0])] + 1)
                        dve.wait_ge(s_score, t + 1)
                        dve.tensor_tensor_reduce(sc[:, t % 4, 0:nk], sbank[t % 2][:, 0:nk], bias, -1.0, 3e38,
                                                 ALU.add, ALU.min, negmax[:, t:t + 1]).then_inc(s_biased, 1)
                elif kind == "mix":
                    n = item[1]
                    m, i, h = units[n]
                    nk = (i + 1) * P
                    t = t_of[(n, 0)]
                    dve.wait_ge(s_exp, t + 2)
                    link(dve.reciprocal(linv[:, t:t + 2], lsum[:, t:t + 2]))
                    c = mixc[:, n % 16:n % 16 + 1]
                    link(dve.scalar_tensor_tensor(out=c, in0=lsum[:, t:t + 1], scalar=lams[:, 5:6],
                                                  in1=linv[:, t + 1:t + 2], op0=ALU.mult, op1=ALU.mult))
                    dve.scalar_tensor_tensor(out=sc[:, t % 4, 0:nk], in0=sc[:, (t + 1) % 4, 0:nk], scalar=c,
                                             in1=sc[:, t % 4, 0:nk], op0=ALU.mult, op1=ALU.add).then_inc(s_mix, 1)
                elif kind == "onorm":
                    g4 = item[1]
                    m, i, _ = units[4 * g4]
                    dve.wait_ge(s_pv, 4 * g4 + 4)
                    t = t_of[(4 * g4, 0)]
                    o = obank[g4 % 2][:, 0:GW].rearrange("p (h n) -> p h n", h=H)
                    dst = xo[:, i, m * GW:(m + 1) * GW].rearrange("p (h n) -> p h n", h=H)
                    wide = lambda v: v.unsqueeze(2).to_broadcast([P, H, HD])
                    if m != B:
                        link(dve.reciprocal(linv[:, t:t + H], lsum[:, t:t + H]))
                        dve.tensor_tensor(dst, o, wide(linv[:, t:t + H]), ALU.mult).then_inc(s_onorm, 1)
                    else:
                        l1 = linv[:, t:t + 2 * H].rearrange("p (h s) -> p h s", s=2)[:, :, 0]
                        dve.tensor_tensor(dst, o, wide(l1), ALU.mult).then_inc(s_onorm, 1)
                        dve.wait_ge(s_onorm, g4 + 1)
                        sq = sqh[:]
                        link(dve.tensor_tensor(sq.rearrange("p (h n) -> p h n", h=H), dst, dst, ALU.mult))
                        dve.tensor_reduce(onrm[:, 0, :], sq.rearrange("p (h n) -> p h n", h=H), AX.X,
                                          ALU.add).then_inc(s_osq, 1)
                        dve.wait_ge(s_ors, g4 - 4 * B + 1)
                        link(dve.tensor_tensor(dst, dst, wide(onrm[:, 1, :]), ALU.mult))
                        link(dve.tensor_tensor(dst, dst, subg[:].unsqueeze(1).to_broadcast([P, H, HD]), ALU.mult))
                elif kind == "out" and item[3] == KC - 1:
                    i, z = item[1:3]
                    dve.wait_ge(s_xres[i % 2], 16 * (i // 2 + 1))
                    o = take(P_AT[item[:3]])
                    dve.tensor_tensor(xo[:, i, z * 512:(z + 1) * 512], o[:], xres[:, i % 2, z * 512:(z + 1) * 512],
                                      ALU.add).then_inc(s_pempty, 1)
                elif kind == "norm2":
                    i = item[1]
                    if i == 0:
                        dve.wait_ge(s_ln2b, 16)
                    if i >= 2:
                        dve.wait_ge(s_h2out[i - 2], 16)
                    dve.wait_ge(s_rs2, i + 1)
                    normalise(hrow[:, i % 2, :], xo[:, i, :], rs[:, 1, i:i + 1]).then_inc(s_h2, 1)
                elif kind == "route":
                    i = item[1]
                    dve.wait_ge(s_rs2, i + 1)
                    o = take(P_AT[item])
                    dve.scalar_tensor_tensor(out=logit[:, i, :], in0=o[:, 0:NG + E], scalar=rs[:, 1, i:i + 1],
                                             in1=rb[:], op0=ALU.mult, op1=ALU.add).then_inc(s_pempty, 1)
                    landed(dve, item)
                elif kind == "pick":
                    i = item[1]
                    g, e = logit[:, i, 0:NG], logit[:, i, NG:]
                    top, v1, v2 = pick[:, 3, 8:9], picks[:, i, 1:2], picks[:, i, 2:3]
                    first_max(g, NG, top, None, i)
                    link(dve.tensor_scalar(pick[:, 3, 0:NG], pick[:, 2, 0:NG], picks[:, i, 0:1], NEG,
                                           ALU.not_equal, ALU.mult))
                    link(dve.tensor_tensor(pick[:, 0, :].rearrange("p (g e) -> p g e", g=NG),
                                           e.rearrange("p (g e) -> p g e", g=NG),
                                           pick[:, 3, 0:NG].unsqueeze(2).to_broadcast([P, NG, EPG]), ALU.add))
                    first_max(pick[:, 0, :], E, v1, oh[:, i, 0, :], i)
                    link(dve.scalar_tensor_tensor(out=pick[:, 0, :], in0=oh[:, i, 0, :], scalar=2 * NEG,
                                                  in1=pick[:, 0, :], op0=ALU.mult, op1=ALU.add))
                    first_max(pick[:, 0, :], E, v2, oh[:, i, 1, :], i)
                    dve.tensor_tensor(mem[:, i, :], oh[:, i, 0, :], oh[:, i, 1, :], ALU.add).then_inc(s_pick, 1)
                    link(dve.tensor_scalar(token[:, i, 2:3], picks[:, i, 0:1], PLACE, None, ALU.add))
                    dve.tensor_scalar(picks[:, i, 3:4], top, -1.0, None, ALU.mult).then_inc(s_top, 1)
                elif kind == "rank":
                    i = item[1]
                    o = take(P_AT[item])
                    dve.tensor_copy(rank[:, i, :], o[:, 0:E]).then_inc(s_pempty, 1)
                    dve.wait_ge(s_pempty, P_AT[item] + 1)
                    link(dve.scalar_tensor_tensor(out=rankm[:], in0=rank[:, i, :], scalar=1.0, in1=mem[:, i, :],
                                                  op0=ALU.add, op1=ALU.mult))
                    if i:
                        dve.wait_ge(s_pfull, P_AT[("slot", i - 1)] + 1)
                    dve.tensor_tensor(spread.rearrange("p (e s) -> p e s", e=E),
                                      rankm[:].unsqueeze(2).to_broadcast([P, E, CAP]),
                                      iota_s[:].unsqueeze(1).to_broadcast([P, E, CAP]), ALU.is_equal).then_inc(s_spread, 1)
                elif kind == "slot":
                    i = item[1]
                    o = take(P_AT[item])
                    dve.tensor_copy(slotf[:, i, :], o[:, 0:3 * PAIRS]).then_inc(s_pempty, 1)
                    if i:
                        landed(dve, item)
                        v = slotf[:, i, :].rearrange("p (q z) -> p q z", z=3)
                        link(dve.scalar_tensor_tensor(out=v[:, :, 0], in0=v[:, :, 1], scalar=float(i * P), in1=v[:, :, 0],
                                                      op0=ALU.mult, op1=ALU.add))
                elif kind == "slots":
                    dve.wait_ge(s_pempty, P_AT[("slot", NT - 1)] + 1)
                    link(dve.tensor_reduce(slott, slotf[:].rearrange("p i (q z) -> p q z i", z=3), AX.X, ALU.add))
                    row, taken, second = (slott[:, :, z] for z in range(3))
                    link(dve.scalar_tensor_tensor(out=slotn[:, 0, :], in0=taken, scalar=-EMPTY, in1=row,
                                                  op0=ALU.mult, op1=ALU.add))
                    dve.tensor_scalar(idx[:], slotn[:, 0, :], EMPTY, None, ALU.add).then_inc(s_idx, 1)
                    lower = upto[:, CAP - 1:CAP]
                    link(dve.scalar_tensor_tensor(out=slotn[:, 1, :], in0=second, scalar=lower, in1=iota_e[:, 1::2],
                                                  op0=ALU.add, op1=ALU.is_equal))
                    link(dve.scalar_tensor_tensor(out=slotn[:, 2, :], in0=slotn[:, 1, :], scalar=float(S),
                                                  in1=slotn[:, 0, :], op0=ALU.mult, op1=ALU.add))
                    dve.tensor_scalar(dest[:], slotn[:, 2, :], EMPTY, None, ALU.add).then_inc(s_dest, 1)
                elif kind == "count":
                    o = take(P_AT[item])
                    dve.tensor_reduce(busiest[:], o[:, 0:E], AX.X, ALU.max).then_inc(s_pempty, 1)
                    landed(dve, item)
                    dve.tensor_copy(crowd[:], busiest[:]).then_inc(s_crowd, 1)
                elif kind == "weights" and item[1] < NT - 1:
                    combine_weights(item[1])

            def hidden(it, j):
                dve.wait_ge(s_silu, 2 * it + j + 1)
                dve.tensor_tensor(hid[:, j, :], gate_act[:, j, :], sbank[j][:, FE:2 * FE], ALU.mult).then_inc(s_hid, 1)

            def hidden_turned(it, j):
                dve.wait_ge(s_turned, 2 * it + j + 1)
                dve.tensor_copy(hidT[:, j, :], sbank[j][:, 0:FE]).then_inc(s_hidT, 1)

            def rows_out(it, j, first=False):
                dve.wait_ge(s_down, 2 * it + j + 1)
                if first and j == 0:
                    for i in range(NT):
                        dve.wait_ge(s_h2out[i], 16)
                if not first:
                    dve.wait_ge(s_yst[j], 16 * it)
                dve.tensor_copy(yrow[:, j, 0:512], (pbank, obank)[j][0][:]).then_inc(s_yd, 1)

            def pair_steps(it, j, before_first=False):
                hidden_turned(*pair_before(it, j))
                hidden(it, j)
                rows_out(*pair_before(it, j), first=before_first)

            hidden(0, 0)
            pair_steps(0, 1, before_first=True)
            combine_weights(NT - 1)
            pair_steps(1, 0, before_first=True)
            pair_steps(1, 1)
            with dve.Fori(2, E // 4, 1) as it:
                for j in range(2):
                    pair_steps(it, j)
            last_it = E // 4 - 1
            hidden_turned(last_it, 1)
            rows_out(last_it, 1)

            dve.wait_ge(s_crowd, 1)
            with dve.register("dve_crowd") as r:
                dve.reg_load(r, crowd[0:1, 0:1])
                with dve.If(dve.snap(r) > CAP):
                    with dve.Fori(0, E, 1) as e:
                        dve.tensor_copy(lcur[:], late[:, :, bass.ds(e, 1)].rearrange("p i e -> p (i e)")).then_inc(s_dcur, 1)
                        dve.wait_ge(s_dcur, e + 1)
                        for a in range(FT):
                            dve.wait_ge(s_dsilu, FT * e + (a + 1))
                            dve.tensor_tensor(dense_hid[:, a, :], dense_act[:, a, :], pbank[1][:], ALU.mult).then_inc(s_dhid, 1)
                        for i in range(NT):
                            for half in range(2):
                                dve.wait_ge(s_dy, 2 * NT * e + (2 * i + half + 1))
                                x2 = xo[:, i, half * 512:(half + 1) * 512]
                                dve.scalar_tensor_tensor(out=x2, in0=obank[half][:], scalar=lcur[:, i:i + 1], in1=x2,
                                                         op0=ALU.mult, op1=ALU.add).then_inc(s_dacc, 1)
                        dve.wait_ge(s_dacc, 2 * NT * e + 2 * NT)

            dve.wait_ge(s_lnfb, 16)
            for i in range(NT):
                for k in range(2):
                    dve.wait_ge(s_yg[2 * i + k], 16)
                    dve.scalar_tensor_tensor(out=xo[:, i, :], in0=ybuf[:, i, k, :], scalar=comb[:, i, k:k + 1],
                                             in1=xo[:, i, :], op0=ALU.mult, op1=ALU.add).then_inc(s_sum, 1)
                    dve.wait_ge(s_sum, 2 * i + k + 1)
            for i in range(NT // 2, NT):
                dve.wait_ge(s_rs3, i + 1)
                dve.scalar_tensor_tensor(out=orow[:, i, :], in0=xo[:, i, :], scalar=rs[:, 2, i:i + 1],
                                         in1=lnfb, op0=ALU.mult, op1=ALU.mult).then_inc(s_orow_last, 1)


def bucket_tables():
    import numpy as np
    dist = S - 1 - np.arange(SPAN)
    d = np.maximum(dist, 0)
    exact = BUCKETS // 2
    large = exact + (np.log(np.maximum(d, 1) / exact) / math.log(2048 / exact) * (BUCKETS - exact)).astype(np.int32)
    bucket = np.where(d < exact, d, np.minimum(large, BUCKETS - 1))
    rows = np.zeros((BUCKETS + 2, SPAN), np.float32)
    past = dist >= 0
    rows[bucket[past], np.nonzero(past)[0]] = 1.0
    held = sum(((d % dil == 0) & (d <= window)).astype(int) for window, dil in ((128, 1), (512, 4), (2048, 16)))
    rows[BUCKETS, past] = np.where(held > 0, np.log(np.maximum(held, 1)), NEG)[past]
    rows[BUCKETS + 1, ~past] = NEG
    cols = np.zeros((2, 12), np.float32)
    cols[0, 0:H] = 1.0
    cols[1, :] = 1.0
    return rows, cols


_INS = ["x", "rel_bias", "ln1", "w_in", "w_out", "lam_q1", "lam_k1", "lam_q2", "lam_k2", "subln_g", "b_forget",
        "ln2", "w_group", "b_group", "w_expert", "b_expert", "w_gate", "w_up", "w_down", "ln_f"]


def kernel(**inputs):
    import numpy as _np
    import concourse.bacc as _bacc
    from concourse import mybir as _mybir
    from concourse.bass_utils import run_bass_kernel_spmd as _run

    nc = _bacc.Bacc("TRN2", target_bir_lowering=False, num_devices=1)
    arrays, args = {}, []
    host = {name: _np.ascontiguousarray(inputs[name]) for name in _INS}
    host["bucket_rows"], host["bias_cols"] = bucket_tables()
    for name, a in host.items():
        arrays[f"in_{name}_dram"] = a
        args.append(nc.dram_tensor(f"in_{name}_dram", a.shape, _mybir.dt.from_np(a.dtype), kind="ExternalInput").ap())
    args.append(nc.dram_tensor("out_0_dram", (1, S, D), F32, kind="ExternalOutput").ap())
    hybrid_layer(nc, *args)
    r = _run(nc, [arrays], core_ids=[0])
    return r.results[0]["out_0_dram"]
```
